# Optimizing a Trainium2 kernel written in Bass

```python
import jax
import jax.numpy as jnp
from jax import lax
import numpy as np

D_MODEL = 1024
BATCH = 1
SEQ = 512
DEPTH = 1

GRID_W = 64
CTX_LEN = 256
HEAD_DIM = 64
NA_WIDTH = D_MODEL // 2
NA_HEADS = NA_WIDTH // HEAD_DIM
NA_ROWS = 8
NA_COLS = 16
CONV_CH = D_MODEL // 4
CONV_K = 3
FOURIER_WIDTH = D_MODEL - NA_WIDTH - CONV_CH
FOURIER_GROUPS = 4
FOURIER_GROUP_DIM = FOURIER_WIDTH // FOURIER_GROUPS
IN_WIDTH = 3 * NA_WIDTH + 3 * CONV_CH + FOURIER_WIDTH
N_EXPERTS = 16
CAPACITY_FACTOR = 2
EXPERT_HIDDEN = 256 * (-(-8 * D_MODEL // (3 * 256)))
N_MOD = 6
RMS_EPS = 1e-6
NEG_INF = -1e30

kernel_name = 'hybrid_na_conv_fourier_ec_block'

def rms_norm(x, g):
    xf = x.astype(jnp.float32)
    y = xf * lax.rsqrt(jnp.mean(xf * xf, axis=-1, keepdims=True) + RMS_EPS)
    return (y * g.astype(jnp.float32)).astype(x.dtype)

def group_rms(t):
    tf = t.astype(jnp.float32)
    return tf * lax.rsqrt(jnp.mean(tf * tf, axis=-1, keepdims=True) + RMS_EPS)

def modulate(h, shift, scale):
    return h * (1 + scale) + shift

def split_proj(p):
    b, n, _ = p.shape
    heads = lambda t: t.reshape(b, n, NA_HEADS, HEAD_DIM)
    q = heads(p[..., 0:NA_WIDTH])
    k = heads(p[..., NA_WIDTH:2 * NA_WIDTH])
    v = heads(p[..., 2 * NA_WIDTH:3 * NA_WIDTH])
    o = 3 * NA_WIDTH
    bg = p[..., o:o + CONV_CH]
    cg = p[..., o + CONV_CH:o + 2 * CONV_CH]
    u = p[..., o + 2 * CONV_CH:o + 3 * CONV_CH]
    f = p[..., o + 3 * CONV_CH:]
    return q, k, v, bg, cg, u, f

def neighbourhood_attention(q, k, v, k_ctx, v_ctx, rpb):
    b, n, h, dh = q.shape
    rows = n // GRID_W
    wr = min(NA_ROWS, rows)
    qg = q.reshape(b, rows, GRID_W, h, dh)
    kg = k.reshape(b, rows, GRID_W, h, dh)
    vg = v.reshape(b, rows, GRID_W, h, dh)
    r = jnp.arange(rows)
    row_start = jnp.clip(r - wr // 2, 0, rows - wr)
    row_idx = row_start[:, None] + jnp.arange(wr)[None, :]
    k_rows = kg[:, row_idx]
    v_rows = vg[:, row_idx]
    cols = jnp.arange(GRID_W)
    col_start = jnp.clip(cols - NA_COLS // 2, 0, GRID_W - NA_COLS)
    col_in = (cols[None, :] >= col_start[:, None]) & (cols[None, :] < col_start[:, None] + NA_COLS)
    dr = row_idx - r[:, None] + (NA_ROWS - 1)
    dc = jnp.clip(cols[None, :] - cols[:, None], -(NA_COLS - 1), NA_COLS - 1) + (NA_COLS - 1)
    bias = rpb[:, dr[:, None, :, None], dc[None, :, None, :]]
    scale = HEAD_DIM ** -0.5
    s_win = jnp.einsum('brqhd,brikhd->bhrqik', qg, k_rows, preferred_element_type=jnp.float32) * scale + bias
    s_win = jnp.where(col_in[:, None, :], s_win, NEG_INF)
    s_ctx = jnp.einsum('brqhd,bjhd->bhrqj', qg, k_ctx, preferred_element_type=jnp.float32) * scale
    n_win = wr * GRID_W
    s = jnp.concatenate([s_win.reshape(b, h, rows, GRID_W, n_win), s_ctx], axis=-1)
    p = jax.nn.softmax(s, axis=-1).astype(v.dtype)
    p_win = p[..., :n_win].reshape(b, h, rows, GRID_W, wr, GRID_W)
    p_ctx = p[..., n_win:]
    out = jnp.einsum('bhrqik,brikhd->brqhd', p_win, v_rows) + jnp.einsum('bhrqj,bjhd->brqhd', p_ctx, v_ctx)
    return out.reshape(b, n, h * dh)

def context_attention(q, k, v):
    b, l, h, dh = q.shape
    s = jnp.einsum('bihd,bjhd->bhij', q, k, preferred_element_type=jnp.float32) * (HEAD_DIM ** -0.5)
    p = jax.nn.softmax(s, axis=-1).astype(v.dtype)
    return jnp.einsum('bhij,bjhd->bihd', p, v).reshape(b, l, h * dh)

def short_gated_conv(bg, cg, u, w):
    z = cg * u
    zc = lax.conv_general_dilated(z, w[:, None, :], window_strides=(1,),
                                  padding=[(CONV_K // 2, CONV_K // 2)],
                                  dimension_numbers=('NWC', 'WIO', 'NWC'),
                                  feature_group_count=z.shape[-1])
    return bg * zc

def fourier_mix(f):
    b, n, _ = f.shape
    fg = f.reshape(b, n, FOURIER_GROUPS, FOURIER_GROUP_DIM).astype(jnp.float32)
    y = jnp.fft.fft2(fg, axes=(1, 3), norm='ortho').real
    return y.reshape(b, n, FOURIER_WIDTH).astype(f.dtype)

def merge_groups(na, cv, fo, g_mix_out, w_out):
    y = jnp.concatenate([group_rms(na), group_rms(cv), group_rms(fo)], axis=-1) * g_mix_out.astype(jnp.float32)
    return y.astype(na.dtype) @ w_out

def expert_choice_ffn(h, w_router, w_gate, w_up, w_down):
    b, n, d = h.shape
    cap = CAPACITY_FACTOR * n // N_EXPERTS
    aff = jax.nn.softmax((h @ w_router).astype(jnp.float32), axis=-1)
    gates, idx = lax.top_k(jnp.swapaxes(aff, 1, 2), cap)
    xs = jax.vmap(lambda hb, ib: hb[ib])(h, idx)
    hid = jax.nn.silu(jnp.einsum('becd,edf->becf', xs, w_gate)) * jnp.einsum('becd,edf->becf', xs, w_up)
    out = jnp.einsum('becf,efd->becd', hid, w_down) * gates[..., None].astype(h.dtype)
    return jax.vmap(lambda ib, ob: jnp.zeros((n, d), h.dtype).at[ib.reshape(-1)].add(ob.reshape(-1, d)))(idx, out)

def hybrid_layer(x, ctx, mod_x, mod_c, g_pre_mix, g_post_mix, g_pre_ffn, g_post_ffn,
                 w_in, rpb, conv_w, g_mix_out, w_out, w_router, w_gate, w_up, w_down, ctx_out):
    sh1, sc1, g1, sh2, sc2, g2 = [t[:, None, :] for t in jnp.split(mod_x, N_MOD, axis=-1)]
    sh1c, sc1c, g1c, sh2c, sc2c, g2c = [t[None, None, :] for t in jnp.split(mod_c, N_MOD, axis=-1)]
    h = modulate(rms_norm(x, g_pre_mix), sh1, sc1)
    hc = modulate(rms_norm(ctx, g_pre_mix), sh1c, sc1c)
    q, k, v, bg, cg, u, f = split_proj(h @ w_in)
    qc, kc, vc, bgc, cgc, uc, fc = split_proj(hc @ w_in)
    na = neighbourhood_attention(q, k, v, kc, vc, rpb)
    cv = short_gated_conv(bg, cg, u, conv_w)
    fo = fourier_mix(f)
    x = x + g1 * rms_norm(merge_groups(na, cv, fo, g_mix_out, w_out), g_post_mix)
    h2 = modulate(rms_norm(x, g_pre_ffn), sh2, sc2)
    x = x + g2 * rms_norm(expert_choice_ffn(h2, w_router, w_gate, w_up, w_down), g_post_ffn)
    if ctx_out:
        na_c = context_attention(qc, kc, vc)
        cv_c = short_gated_conv(bgc, cgc, uc, conv_w)
        fo_c = fourier_mix(fc)
        ctx = ctx + g1c * rms_norm(merge_groups(na_c, cv_c, fo_c, g_mix_out, w_out), g_post_mix)
        h2c = modulate(rms_norm(ctx, g_pre_ffn), sh2c, sc2c)
        ctx = ctx + g2c * rms_norm(expert_choice_ffn(h2c, w_router, w_gate, w_up, w_down), g_post_ffn)
    return x, ctx

def setup_inputs(seed: int = 0) -> dict:
    key = jax.random.key(seed)
    ks = jax.random.split(key, 20)
    d = D_MODEL
    nrm = lambda k, shape, s: jax.random.normal(k, shape, jnp.float32) * s
    return {
        'x': nrm(ks[0], (BATCH, SEQ, d), 1.0),
        'c': nrm(ks[1], (BATCH, d), 1.0),
        'ctx': nrm(ks[2], (BATCH, CTX_LEN, d), 1.0),
        'c_ctx': nrm(ks[3], (d,), 1.0),
        'w_mod': nrm(ks[4], (DEPTH, d, N_MOD * d), 0.5 * d ** -0.5),
        'b_mod': nrm(ks[5], (DEPTH, N_MOD * d), 0.02),
        'g_pre_mix': 1.0 + nrm(ks[6], (DEPTH, d), 0.05),
        'g_post_mix': 1.0 + nrm(ks[7], (DEPTH, d), 0.05),
        'g_pre_ffn': 1.0 + nrm(ks[8], (DEPTH, d), 0.05),
        'g_post_ffn': 1.0 + nrm(ks[9], (DEPTH, d), 0.05),
        'w_in': nrm(ks[10], (DEPTH, d, IN_WIDTH), d ** -0.5),
        'rpb': nrm(ks[11], (DEPTH, NA_HEADS, 2 * NA_ROWS - 1, 2 * NA_COLS - 1), 0.1),
        'conv_w': nrm(ks[12], (DEPTH, CONV_K, CONV_CH), CONV_K ** -0.5),
        'g_mix_out': 1.0 + nrm(ks[13], (DEPTH, d), 0.05),
        'w_out': nrm(ks[14], (DEPTH, d, d), d ** -0.5),
        'w_router': nrm(ks[15], (DEPTH, d, N_EXPERTS), d ** -0.5),
        'w_gate': nrm(ks[16], (DEPTH, N_EXPERTS, d, EXPERT_HIDDEN), d ** -0.5),
        'w_up': nrm(ks[17], (DEPTH, N_EXPERTS, d, EXPERT_HIDDEN), d ** -0.5),
        'w_down': nrm(ks[18], (DEPTH, N_EXPERTS, EXPERT_HIDDEN, d), EXPERT_HIDDEN ** -0.5),
    }

def reference(x, c, ctx, c_ctx, w_mod, b_mod, g_pre_mix, g_post_mix, g_pre_ffn, g_post_ffn,
              w_in, rpb, conv_w, g_mix_out, w_out, w_router, w_gate, w_up, w_down):
    silu_c = jax.nn.silu(c)
    silu_cc = jax.nn.silu(c_ctx)
    for layer in range(DEPTH):
        mod_x = silu_c @ w_mod[layer] + b_mod[layer]
        mod_c = silu_cc @ w_mod[layer] + b_mod[layer]
        x, ctx = hybrid_layer(x, ctx, mod_x, mod_c, g_pre_mix[layer], g_post_mix[layer],
                              g_pre_ffn[layer], g_post_ffn[layer], w_in[layer], rpb[layer],
                              conv_w[layer], g_mix_out[layer], w_out[layer], w_router[layer],
                              w_gate[layer], w_up[layer], w_down[layer], layer < DEPTH - 1)
    return x


_drawn_inputs = setup_inputs


def setup_inputs(seed=0):
    import zlib

    import numpy as np

    out = dict(_drawn_inputs(seed))
    spreads = {}
    factors = {'g_post_ffn': 3.803, 'rpb': 2.994}
    for name, (base, spread) in spreads.items():
        noise = np.random.default_rng([zlib.crc32(name.encode()), seed]).standard_normal(out[name].shape)
        drawn = base * np.exp(spread * noise) if base else spread * noise
        out[name] = jnp.asarray(drawn.astype(out[name].dtype))
    for name, factor in factors.items():
        out[name] = (out[name] * factor).astype(out[name].dtype)
    return out
```

```python
from contextlib import ExitStack

import numpy as np

import concourse.bass as bass
from concourse import mybir

F32 = mybir.dt.float32
ALU = mybir.AluOpType
ACT = mybir.ActivationFunctionType
AX_X = mybir.AxisListType.X

P = 128
D = 1024
KT = D // P
SEQ, CTX = 512, 256
NT = SEQ // P
CT = CTX // P
GRID_W, ROWS = 64, 8
HEADS, DH = 8, 64
PAIRS = HEADS // 2
WIN_C = 16
NA_W, CONV_W, FO_W = 512, 256, 256
EPS = 1e-6
MASKED = -1e30
SCALE = DH ** -0.5
E, CAP = 16, 64
HID = 2816

Q_TILES = (1, 2, 0, 3)
KEY_TILES = {0: (3, 0), 1: (0, 1), 2: (1, 2), 3: (2, 3)}

RING = 12
SLOT = 2048
HALVES = (512, 512, 384)
CHUNK0 = (0, 1024, 2048)
GU_SLOTS = len(HALVES) * 8
HB = [(c, j) for c in range(3) for j in range(HALVES[c] // P)]
DOWN_SLOTS = len(HB)
STAGE = GU_SLOTS + DOWN_SLOTS
TURN = 36
assert TURN % RING == 0 and TURN == STAGE + 1
PRE = [("mod", 0, k) for k in range(KT)] + [("in", g, h) for g in range(5) for h in range(2)] \
    + [("mod", 1, k) for k in range(KT)] + [("mod", 2, k) for k in range(KT)] + [("dft", 0, 0)] \
    + [("out", 0, k) for k in range(4)]
NPRE = len(PRE)
IN_K, IN_Q, IN_V, IN_BC, IN_UF = range(5)
IN_COLS = (512, 0, 1024, 1536, 2048)


def units():
    return [(t, h) for t in Q_TILES for h in range(HEADS)]


def pre_fills():
    ev = ("act", "dve")
    out = [(("xT", k), ev[k % 2], ev[k % 2]) for k in range(6)]
    out += [(("mod", 0), "first", "first"), (("modT", 0), "first", "first")]
    out += [(("xT", k), ev[k % 2], ev[k % 2]) for k in (6, 7)]
    out += [(("cT", k), ev[k % 2], ev[k % 2]) for k in range(4)]
    names = [("kc", b) for b in range(2)] + [("k", b) for b in range(4)] + [("q", b) for b in range(4)] \
        + [("vc", b) for b in range(CT)] + [("v", b) for b in range(4)] + [("bg", b) for b in range(2)] \
        + [("cg", b) for b in range(2)]
    out += [(n, ev[i % 2], ev[i % 2]) for i, n in enumerate(names)]
    out += [(("u", b), "dve", "dve") for b in range(2)] + [(("f", b), "act", "act") for b in range(2)]
    out += [(("mod", g), "dve", "dve") for g in (1, 2)]
    out += [(("dft1", b), ev[b % 2], ev[b % 2]) for b in range(4)]
    out += [(("dft2", b), "act", "dve") for b in range(2)]
    n = len(units())
    for i in range(n + 4):
        if i < n:
            out.append((("S", i), "dve", "act"))
        if 2 <= i < n + 2:
            out.append((("PT", i - 2), "dve", "dve"))
        if i >= 4 and i % 2 == 1:
            out.append((("PO", i - 4), "act", "act"))
    out += [(("ss", b), None, "act") for b in range(3)]
    out += [(("bc", b), ev[b % 2], ev[b % 2]) for b in range(8)]
    for t in range(NT + 1):
        if t < NT:
            out += [(("y", t, b), "act", "dve") for b in range(2)]
        if t >= 1:
            out += [(("h2T", t - 1, b), "act", "act") for b in range(2)] + [(("rt", t - 1), "act", "act")]
    out += [(("affT", 0), "dve", "dve"), (("posT", 0), "dve", "dve"), (("xs", 0), "act", "act")]
    return out


def build_block(nc, x, cT, ctx, w_mod, b_mod, colv, g_post_mix, g_pre_ffn, g_post_ffn, w_in, rpbT, w_out,
                w_router, w_gate, w_up, w_down, consts, dft, out):
    fills = pre_fills()
    number = {name: i for i, (name, _, _) in enumerate(fills)}
    read_no = {n: sum(r == f[1] for _, r, _ in fills[:number[n]]) + 1 for n in number for f in [fills[number[n]]]}
    free_no = {n: sum(l == f[2] for _, _, l in fills[:number[n]]) + 1 for n in number for f in [fills[number[n]]]}

    with ExitStack() as stack:
        def sb(name, *shape):
            return stack.enter_context(nc.sbuf_tensor(name, [P, *shape], F32))

        def sem(name):
            return stack.enter_context(nc.semaphore(name))

        bank = [stack.enter_context(nc.psum_tensor(f"bank{i}", [P, 512], F32)) for i in range(8)]

        ring = sb("ring", RING, SLOT)
        cst = sb("cst", 128 + 512 + 128)
        ident, sel, iota = cst[:, 0:128], cst[:, 128:640].rearrange("p (g n) -> p g n", g=4), cst[:, 640:768]
        ones = sb("ones", 128)
        cols = sb("cols", 22)
        g_pre_col, g_mix_col = cols[:, 0:8], cols[:, 8:16]
        conv_w = cols[:, 16:22].rearrange("p (b j) -> p b j", b=2)
        w_rt = sb("w_rt", KT, E)
        dd = sb("dd", 256)
        c_sb = sb("c_sb", KT, 2)
        s_pad = sb("s_pad", KT, 32)
        mod_row = sb("mod_row", 3, 512)
        one_col = sb("one_col", 1)
        eps_col = sb("eps_col", 1)
        mod_scale, mod_shift = sb("mod_scale", 2, KT), sb("mod_shift", 2, KT)
        x_ss, x_sd, x_rs = sb("x_ss", 6), sb("x_sd", 6), sb("x_rs", 6)
        neg_max, win_max, ctx_max = sb("neg_max", 32), sb("win_max", 32), sb("ctx_max", 32)
        sums, total, inv = sb("sums", 32, 2), sb("total", 32), sb("inv", 32)
        y_ss, y_s1, y_sd, y_rs = sb("y_ss", NT, 2), sb("y_s1", NT), sb("y_sd", NT), sb("y_rs", NT)
        z_ss, z_sd, z_rs = sb("z_ss", NT), sb("z_sd", NT), sb("z_rs", NT)
        logit, aff = sb("logit", NT, E), sb("aff", NT, E)
        r_max, r_sum, r_inv = sb("r_max", NT), sb("r_sum", NT), sb("r_inv", NT)
        place = sb("place", NT, E + 2)
        top8 = sb("top8", 8)

        arena = sb("arena", 112 * 256)

        def at(kb, *shape):
            n = int(np.prod(shape))
            o = int(kb * 256)
            v = arena[:, o:o + n]
            if len(shape) == 2:
                v = v.rearrange("p (a b) -> p a b", a=shape[0])
            if len(shape) == 3:
                v = v.rearrange("p (a b c) -> p a b c", a=shape[0], b=shape[1])
            return v

        hT = at(0, KT, SEQ)
        yT = at(0, KT, SEQ)
        acc = at(0, NT, D)
        hcT = at(16, KT, CTX)
        raw_bias = at(16, HEADS, 256)
        qTp = at(24, HEADS, SEQ)
        kT = at(40, PAIRS, SEQ)
        kcT = at(48, PAIRS, CTX)
        v_sb = at(52, 4, NA_W)
        vc_sb = at(60, CT, NA_W)
        HEAD_W = (2 * WIN_C - 1) * ROWS
        shifted = at(64, 64 + HEADS * HEAD_W + 64)[0:ROWS]
        bg_sb = at(64, 2, SEQ)
        z_sb = at(68, 2, 528)
        f_sb = at(72.25, 2, SEQ)
        x_rows = at(76.25, NT, D)
        x1 = at(76.25, NT, D)
        bias = [at(76.25, HEADS, 256), at(84.25, HEADS, 256)]
        ctx_rows = at(92.25, CT, D)
        prob = [at(92.25 + 2 * i, 512) for i in range(4)]
        b_row = at(100.25, 3, 512)
        g_row = at(106.25, 2, 512)
        dft_g = at(100.25, 4, 512)
        dft_o = at(108.25, 2, 256)
        probT = [at(100.25 + 2 * i, 512) for i in range(4)]
        junk = at(40, D)
        h2 = at(24, NT, D)
        gain4 = at(16, D)
        gain1, gain2, shift2 = at(40, D), at(44, D), at(48, D)
        y_tmp = [at(52, D), at(56, D)]
        sq = [at(60, 512), at(62, 512)]
        rb = [at(64 + 2 * i, 512) for i in range(3)]
        sd = [at(70, 512), at(72, 512), at(74, 512)]
        h2T = [at(92.25, KT, P), at(96.25, KT, P)]
        sq_row = at(100.25, D)
        work, chosen, count, one_row, rank = [at(k, 512)[0:E] for k in (60, 62, 64, 66, 68)]
        xsT = [at(20, KT, CAP), at(22, KT, CAP)]
        out_e = at(40, D)
        silu_g = [at(44, 512), at(46, 512)]
        hid = [at(48, 512), at(50, 512)]
        hidT = at(52, DOWN_SLOTS, P)
        gateT = [at(58, 512), at(60, 512)]
        pick = at(62, NT, CAP)
        gate_pick = at(64, NT, 2 * CAP)
        fin = [at(24 + 4 * t, D) for t in range(NT)]
        out_sq = at(44, D)

        loaded = [sem(f"slot_loaded{i}") for i in range(RING)]
        x_loaded = [sem(f"x_loaded{t}") for t in range(NT)]
        c_loaded, ident_loaded, consts_loaded = sem("c_loaded"), sem("ident_loaded"), sem("consts_loaded")
        rows_loaded, ctx_loaded, shifted_loaded = sem("rows_loaded"), sem("ctx_loaded"), sem("shifted_loaded")
        raw_loaded, x_again, stored = sem("raw_loaded"), sem("x_again"), sem("stored")
        filled = {e: sem(f"filled_for_{e}") for e in ("act", "dve", "first")}
        drained = {e: sem(f"drained_by_{e}") for e in ("act", "dve", "first")}
        slots_used = sem("slots_used")
        pool_set, dve_set = sem("pool_set"), sem("dve_set")
        act_chain, dve_chain, pool_chain = sem("act_chain"), sem("dve_chain"), sem("pool_chain")
        silu_ready, x_sd_ready, xn_ready = sem("silu_ready"), sem("x_sd_ready"), sem("xn_ready")
        rows_ready, bias_ready, odd_copied = sem("rows_ready"), sem("bias_ready"), sem("odd_copied")
        scores_ready, inv_ready, prob_ready = sem("scores_ready"), sem("inv_ready"), sem("prob_ready")
        conv_ready = sem("conv_ready")
        squares_ready, squares_used, yT_ready = sem("squares_ready"), sem("squares_used"), sem("yT_ready")
        y_sums, y_added, y_sd_ready = sem("y_sums"), sem("y_added"), sem("y_sd_ready")
        x1_ready, z_sd_ready, h2_scaled, h2_ready = sem("x1_ready"), sem("z_sd_ready"), sem("h2_scaled"), sem("h2_ready")
        r_sub_ready, r_exp_ready, aff_ready = sem("r_sub_ready"), sem("r_exp_ready"), sem("aff_ready")
        rank_ready, start_zero = sem("rank_ready"), sem("start_zero")
        silu_done, hid_ready = sem("silu_done"), sem("hid_ready")
        t_filled, t_drained = sem("t_filled"), sem("t_drained")
        m_filled, m_drained = sem("m_filled"), sem("m_drained")
        d_drained = sem("d_drained")
        pick_ready, gate_pick_ready = sem("pick_ready"), sem("gate_pick_ready")
        last_filled, acc_done, f_sd_ready, f_scaled, f_ready = (
            sem("last_filled"), sem("acc_done"), sem("f_sd_ready"), sem("f_scaled"), sem("f_ready"))

        def bank_of(name):
            return bank[number[name] % 8]

        def reader(name):
            return fills[number[name]][1]

        def open_fill(pe, name):
            i = number[name]
            if i >= 8:
                old = fills[i - 8]
                pe.wait_ge(drained[old[2]], free_no[old[0]])
            return bank[i % 8]

        def fill_done(ins, name):
            ins.then_inc(filled[reader(name)], 1)

        def wait_fill(eng, name):
            eng.wait_ge(filled[reader(name)], read_no[name])
            return bank_of(name)

        def drain_done(ins, name):
            ins.then_inc(drained[fills[number[name]][2]], 1)

        def wait_drained(eng, name):
            eng.wait_ge(drained[fills[number[name]][2]], free_no[name])

        def link(eng, chain, ins):
            chain[1] += 1
            ins.then_inc(chain[0], 1)
            eng.wait_ge(chain[0], chain[1])

        def mine(names, who):
            return [n for n in names if reader(n) == who]

        def bc_dst(b):
            return (gain1, shift2, gain2, gain4)[b // 2][:, (b % 2) * 512:(b % 2 + 1) * 512]

        def pieces(name):
            kind, b = name[0], name[1]
            src = bank_of(name)
            if kind == "kc":
                return [(kcT[:, 2 * b:2 * b + 2].rearrange("p a n -> p (a n)"), src[:])]
            if kind == "q":
                return [(qTp[0:64, 2 * b], src[0:64]), (qTp[64:P, 2 * b + 1], src[64:P])]
            if kind == "f":
                return [(f_sb[:, b].rearrange("p (e c r) -> p c e r", e=2, r=ROWS),
                         src[:].rearrange("p (c e r) -> p c e r", e=2, r=ROWS))]
            dst = {"k": kT, "vc": vc_sb, "v": v_sb, "bg": bg_sb, "dft1": dft_g}.get(kind)
            if dst is not None:
                return [(dst[:, b], src[:])]
            if kind == "cg":
                return [(z_sb[:, b, 8:520], src[:])]
            if kind == "bc":
                return [(bc_dst(b), src[:])]

        EARLY = [("kc", b) for b in range(2)] + [("k", b) for b in range(4)] + [("q", b) for b in range(4)] \
            + [("vc", b) for b in range(CT)] + [("v", b) for b in range(4)]
        GATES = [("bg", b) for b in range(2)] + [("cg", b) for b in range(2)]

        def wait_slot(eng, key):
            n = PRE.index(key)
            eng.wait_ge(loaded[n % RING], 16 * (n // RING + 1))
            return ring[:, n % RING, :]

        x_v = x[0].rearrange("(r c) d -> c r d", c=GRID_W)
        out_v = out[0].rearrange("(r c) d -> c r d", c=GRID_W)
        pre_src = {}
        for k in range(KT):
            for g in range(3):
                pre_src["mod", g, k] = w_mod[0, k * P:(k + 1) * P, g * SLOT:(g + 1) * SLOT]
        for g in range(5):
            for h in range(2):
                pre_src["in", g, h] = w_in[0, h * 512:(h + 1) * 512, IN_COLS[g]:IN_COLS[g] + 512].rearrange(
                    "(k p) n -> p k n", p=P)
        pre_src["dft", 0, 0] = dft
        for k in range(4):
            pre_src["out", 0, k] = w_out[0, k * 256:(k + 1) * 256, :].rearrange("(k p) n -> p k n", p=P)
        fills_of_slot = [sum(1 for n in range(NPRE) if n % RING == s) for s in range(RING)]
        per_expert = [sum(1 for i in range(STAGE) if (NPRE + i) % RING == s) for s in range(RING)]
        before = [sum(1 for j in range(i) if (NPRE + j) % RING == (NPRE + i) % RING) for i in range(STAGE)]

        def loads_until(e, i):
            s = (NPRE + i) % RING
            return e * (16 * per_expert[s]) + 16 * (fills_of_slot[s] + before[i] + 1)

        block = stack.enter_context(nc.Block())

        @block.sync
        def _(sp):
            for n, key in enumerate(PRE):
                if key == ("mod", 2, 0):
                    wait_fill(sp, ("vc", CT - 1))
                    sp.wait_ge(shifted_loaded, 16 * ROWS)
                    for c in range(WIN_C):
                        first = 64 + (7 - c) * ROWS
                        rows_of_heads = bass.AP(shifted.tensor, shifted.offset + first,
                                                [shifted.ap[0], [HEAD_W, HEADS], [1, 256]])
                        sp.dma_start(raw_bias[8 * c:8 * c + 8], rows_of_heads)\
                            .then_inc(raw_loaded, 16)
                if n >= RING:
                    sp.wait_ge(slots_used, n - RING + 1)
                dst = ring[:, n % RING, :]
                if key[0] == "in":
                    dst = dst.rearrange("p (k n) -> p k n", k=4)
                if key[0] == "out":
                    dst = dst.rearrange("p (k n) -> p k n", k=2)
                sp.dma_start(dst, pre_src[key]).then_inc(loaded[n % RING], 16)
            with sp.Fori(0, E) as e:
                for i in range(STAGE):
                    lag = RING - 2 if i < RING - 1 else RING - 1
                    sp.wait_ge(slots_used, e * STAGE + (NPRE + i - lag))
                    s = (NPRE + i) % RING
                    if i < GU_SLOTS:
                        c, kk, w = i // 8, (i % 8) // 2, (w_gate, w_up)[i % 2]
                        n = 2 * HALVES[c]
                        src = w[0, bass.ds(e, 1), kk * 256:(kk + 1) * 256, CHUNK0[c]:CHUNK0[c] + n].rearrange(
                            "a (k p) n -> p (a k) n", p=P)
                        dst = ring[:, s, 0:2 * n].rearrange("p (k n) -> p k n", k=2)
                    else:
                        c, j = HB[i - GU_SLOTS]
                        src = w_down[0, bass.ds(e, 1), CHUNK0[c]:CHUNK0[c] + 2 * HALVES[c], :].rearrange(
                            "a (h f) n -> f (a h) n", h=2)[j * P:(j + 1) * P]
                        dst = ring[:, s, :].rearrange("p (h n) -> p h n", h=2)
                    sp.dma_start(dst, src).then_inc(loaded[s], 16)

        @block.gpsimd
        def _(pool):
            chain = [pool_chain, 0]
            pool.memset(shifted, 0.0).then_inc(pool_set, 1)
            pool.memset(qTp[:], 0.0).then_inc(pool_set, 1)
            pool.memset(place[:], 0.0).then_inc(pool_set, 1)
            pool.memset(ones[:], 1.0).then_inc(pool_set, 1)

            def times8(dst, src):
                link(pool, chain, pool.tensor_scalar(dst, src, 8.0, 1.0, ALU.mult, ALU.mult))

            def masked(v):
                link(pool, chain, pool.memset(v, 8 * MASKED))

            def from_c(b, k0, k1, col0):
                v = b[:, :, col0:col0 + 8 * (k1 - k0)].rearrange("p h (k i) -> p h k i", i=8)
                return pool.affine_select(
                    out=v, in_=v, pattern=[[0, HEADS], [8, k1 - k0], [0, 8]], compare_op=ALU.is_ge,
                    fill=8 * MASKED, base=8 * k0 + 7, channel_multiplier=-1)

            def to_c(b, k0, k1, col0):
                v = b[:, :, col0:col0 + 8 * (k1 - k0)].rearrange("p h (k i) -> p h k i", i=8)
                return pool.affine_select(
                    out=v, in_=v, pattern=[[0, HEADS], [-8, k1 - k0], [0, 8]], compare_op=ALU.is_ge,
                    fill=8 * MASKED, base=8 * (WIN_C - 1) - 8 * k0, channel_multiplier=1)

            wait_fill(pool, ("xT", 6))
            wait_fill(pool, ("xT", 7))
            pool.wait_ge(raw_loaded, 16 * WIN_C)
            times8(bias[0], raw_bias)
            link(pool, chain, from_c(bias[0], 0, 32, 0))
            to_c(bias[0], 0, 32, 0).then_inc(bias_ready, 1)
            times8(bias[1][:, :, 0:64], raw_bias[:, :, 64:128])
            masked(bias[1][:, :, 64:128])
            times8(bias[1][:, :, 128:256], raw_bias[:, :, 128:256])
            link(pool, chain, from_c(bias[1], 8, 16, 0))
            link(pool, chain, from_c(bias[1], 16, 32, 128))
            to_c(bias[1], 24, 32, 192).then_inc(bias_ready, 1)

            us = units()
            for i, (t, h) in enumerate(us):
                if i == 2 * HEADS:
                    pool.wait_ge(scores_ready, 2 * HEADS)
                    times8(bias[0][:, :, 0:128], raw_bias[:, :, 0:128])
                    masked(bias[0][:, :, 128:192])
                    times8(bias[0][:, :, 192:256], raw_bias[:, :, 128:192])
                    link(pool, chain, from_c(bias[0], 0, 8, 0))
                    link(pool, chain, to_c(bias[0], 0, 16, 0))
                    to_c(bias[0], 16, 24, 192).then_inc(bias_ready, 1)
                pool.wait_ge(inv_ready, i + 1)
                pool.tensor_scalar(prob[i % 4], prob[i % 4], inv[:, i:i + 1], 1.0, ALU.mult, ALU.mult)\
                    .then_inc(prob_ready, 1)

            for t in range(NT):
                wait_drained(pool, ("y", t, 1))
                if t == 0:
                    pool.wait_ge(x_again, 16 * NT)
                pool.tensor_tensor(x1[:, t], x1[:, t], y_tmp[t % 2], ALU.add).then_inc(x1_ready, 1)
                pool.wait_ge(h2_scaled, t + 1)
                pool.tensor_tensor(h2[:, t], h2[:, t], shift2, ALU.add).then_inc(h2_ready, 1)

            wait_fill(pool, ("y", NT - 1, 1))
            pool.memset(acc[:], 0.0).then_inc(start_zero, 1)
            wait_drained(pool, ("rt", NT - 1))
            pool.memset(out_e, 0.0).then_inc(start_zero, 1)
            wait_drained(pool, ("posT", 0))
            pool.memset(gateT[1], 0.0).then_inc(start_zero, 1)

            for t in range(NT):
                pool.wait_ge(f_scaled, t + 1)
                pool.tensor_tensor(fin[t], fin[t], x1[:, t], ALU.add).then_inc(f_ready, 1)

        @block.scalar
        def _(act):
            chain = [act_chain, 0]

            def copy_out(names):
                for name in mine(names, "act"):
                    wait_fill(act, name)
                    for dst, src in pieces(name):
                        ins = nc.scalar.activation(dst, src, ACT.Copy)
                    drain_done(ins, name)

            act.dma_start(c_sb[:], cT).then_inc(c_loaded, 16)
            act.dma_start(x_rows[:, 0], x_v[0:16]).then_inc(x_loaded[0], 16)
            act.dma_start(cst[:], consts[:, 0:768]).then_inc(ident_loaded, 16)
            for t in range(1, NT):
                act.dma_start(x_rows[:, t], x_v[16 * t:16 * (t + 1)]).then_inc(x_loaded[t], 16)
            act.wait_ge(c_loaded, 16)
            act.wait_ge(dve_set, 1)
            nc.scalar.activation(s_pad[:, :, 0:2], c_sb[:], ACT.Silu).then_inc(silu_ready, 1)
            act.dma_start(cols[:], colv).then_inc(consts_loaded, 16)
            act.dma_start(w_rt[:], w_router).then_inc(consts_loaded, 16)
            act.dma_start(dd[:], consts[:, 768:1024]).then_inc(consts_loaded, 16)
            act.wait_ge(dve_set, 2)
            for g in range(3):
                act.dma_start(b_row[0:P:32, g, :], b_mod[0, g * SLOT:(g + 1) * SLOT].rearrange("(a n) -> a n", a=4))\
                    .then_inc(rows_loaded, 16)
            act.dma_start(b_row[1:P:32, 0, :], b_mod[0, 0:SLOT].rearrange("(a n) -> a n", a=4)).then_inc(rows_loaded, 16)
            for rows, g, vec in ((slice(0, 64, 32), 0, g_post_mix), (slice(0, 64, 32), 1, g_pre_ffn),
                                 (slice(64, P, 32), 1, g_post_ffn)):
                act.dma_start(g_row[rows, g, :], vec[0].rearrange("(a n) -> a n", a=2)).then_inc(rows_loaded, 16)
            act.dma_start(ctx_rows[:], ctx[0].rearrange("(t p) d -> p t d", p=P)).then_inc(ctx_loaded, 16)
            act.wait_ge(pool_set, 1)
            for r in range(ROWS):
                act.dma_start(shifted[r:r + 1, 64:64 + HEADS * HEAD_W].rearrange("p (m i) -> p m i", i=8),
                              rpbT[:, :, 7 - r:15 - r].rearrange("(a h) m i -> a (h m) i", a=1))\
                    .then_inc(shifted_loaded, 16)

            act.wait_ge(dve_set, 3)
            for t in range(NT + CT):
                rows = x_rows[:, t] if t < NT else ctx_rows[:, t - NT]
                act.wait_ge(x_loaded[t] if t < NT else ctx_loaded, 16)
                link(act, chain, nc.scalar.activation(junk, rows, ACT.Square, accum_out=x_ss[:, t:t + 1]))
                nc.scalar.activation(x_sd[:, t:t + 1], x_ss[:, t:t + 1], ACT.Sqrt, scale=1.0 / D, bias=eps_col[:, 0:1])\
                    .then_inc(x_sd_ready, 1)

            wait_drained(act, ("modT", 0))
            for kt in range(0, KT, 2):
                b = wait_fill(act, ("xT", kt))
                drain_done(nc.scalar.activation(hT[:, kt], b[:], ACT.Identity, scale=mod_scale[:, 0, kt:kt + 1],
                                                bias=mod_shift[:, 0, kt:kt + 1]), ("xT", kt))
            for f in (0, 2):
                b = wait_fill(act, ("cT", f))
                for j in range(2):
                    kt = 2 * f + j
                    ins = nc.scalar.activation(hcT[:, kt], b[:, j * CTX:(j + 1) * CTX], ACT.Identity,
                                               scale=mod_scale[:, 1, kt:kt + 1], bias=mod_shift[:, 1, kt:kt + 1])
                drain_done(ins, ("cT", f))
            act.wait_ge(pool_set, 2)
            wait_fill(act, ("cT", 3))
            copy_out(EARLY)
            act.wait_ge(raw_loaded, 16 * WIN_C)
            copy_out(GATES)
            copy_out([("f", b) for b in range(2)])
            act.wait_ge(rows_ready, 2)
            copy_out([("dft1", b) for b in range(4)])
            for b in range(2):
                src = wait_fill(act, ("dft2", b))
                nc.scalar.activation(dft_o[:, b], src[:, 256:512], ACT.Copy).then_inc(odd_copied, 1)

            us = units()
            n = len(us)
            for i in range(n + 4):
                if i < n:
                    s = bank_of(("S", i))
                    act.wait_ge(scores_ready, i + 1)
                    nc.scalar.activation(prob[i % 4][:, 0:256], prob[i % 4][:, 0:256], ACT.Exp, scale=-1.0,
                                         bias=neg_max[:, i:i + 1], accum_out=sums[:, i, 0:1])
                    drain_done(nc.scalar.activation(prob[i % 4][:, 256:512], s[:, 256:512], ACT.Exp, scale=SCALE,
                                                    bias=neg_max[:, i:i + 1], accum_out=sums[:, i, 1:2]), ("S", i))
                if i >= 4 and i % 2 == 1:
                    t, h = us[i - 4]
                    src = wait_fill(act, ("PO", i - 4))
                    drain_done(nc.scalar.activation(yT[:, h // 2, t * P:(t + 1) * P], src[:, 0:P], ACT.Copy),
                               ("PO", i - 4))

            act.wait_ge(scores_ready, n)
            for t in range(NT):
                act.dma_start(x1[:, t], x_v[16 * t:16 * (t + 1)]).then_inc(x_again, 16)

            act.wait_ge(conv_ready, 2)
            wait_drained(act, ("dft2", 1))
            wait_drained(act, ("PO", n - 1))
            for j, kt in enumerate((4, 5, 6, 7, 0, 1, 2, 3)):
                if j >= 2:
                    act.wait_ge(squares_used, j - 1)
                nc.scalar.activation(sq[j % 2], yT[:, kt], ACT.Square).then_inc(squares_ready, 1)
            for b, width in enumerate((CONV_W, FO_W, NA_W)):
                src = bank_of(("ss", b))
                act.wait_ge(squares_used, (2, 4, 8)[b])
                drain_done(nc.scalar.activation(sd[b], src[:], ACT.Sqrt, scale=1.0 / width, bias=eps_col[:, 0:1]),
                           ("ss", b))
            copy_out([("bc", b) for b in range(8)])
            for t in range(NT + 1):
                if t < NT:
                    for b in range(2):
                        src = wait_fill(act, ("y", t, b))
                        ins = nc.scalar.activation(sq_row[:, b * 512:(b + 1) * 512], src[:], ACT.Square,
                                                   accum_out=y_ss[:, t, b:b + 1])
                    ins.then_inc(y_sums, 1)
                    act.wait_ge(y_added, t + 1)
                    nc.scalar.activation(y_sd[:, t:t + 1], y_s1[:, t:t + 1], ACT.Sqrt, scale=1.0 / D,
                                         bias=eps_col[:, 0:1]).then_inc(y_sd_ready, 1)
                    act.wait_ge(x1_ready, t + 1)
                    link(act, chain, nc.scalar.activation(sq_row, x1[:, t], ACT.Square, accum_out=z_ss[:, t:t + 1]))
                    nc.scalar.activation(z_sd[:, t:t + 1], z_ss[:, t:t + 1], ACT.Sqrt, scale=1.0 / D,
                                         bias=eps_col[:, 0:1]).then_inc(z_sd_ready, 1)
                if t >= 1:
                    u = t - 1
                    for b in range(2):
                        src = wait_fill(act, ("h2T", u, b))
                        drain_done(nc.scalar.activation(h2T[u % 2][:, 4 * b:4 * b + 4].rearrange("p k n -> p (k n)"),
                                                        src[:], ACT.Copy), ("h2T", u, b))
                    src = wait_fill(act, ("rt", u))
                    drain_done(nc.scalar.activation(logit[:, u], src[:, 0:E], ACT.Copy), ("rt", u))
            act.wait_ge(r_sub_ready, 1)
            nc.scalar.activation(aff[:], logit[:], ACT.Exp).then_inc(r_exp_ready, 1)
            src = wait_fill(act, ("xs", 0))
            drain_done(nc.scalar.activation(xsT[0].rearrange("p k s -> p (k s)"), src[:], ACT.Copy), ("xs", 0))

            with act.Fori(0, E // 2) as pair:
                for s in range(2):
                    e = pair * 2 + s

                    def silu(c):
                        q = (3 * s + c) % 2
                        act.wait_ge(slots_used, e * STAGE + (NPRE + 8 * (c + 1)))
                        nc.scalar.activation(silu_g[q][:, 0:HALVES[c]], bank[q][:, 0:HALVES[c]], ACT.Silu)\
                            .then_inc(silu_done, 1)

                    def from_t(dst, width, fill):
                        act.wait_ge(t_filled, e * 5 + (fill + 1))
                        nc.scalar.activation(dst, bank[4][:, 0:width], ACT.Copy).then_inc(t_drained, 1)

                    silu(0)
                    from_t(hidT[:, 0:4].rearrange("p j n -> p (j n)"), 512, 0)
                    from_t(gateT[s], 512, 1)
                    silu(1)
                    from_t(hidT[:, 4:8].rearrange("p j n -> p (j n)"), 512, 2)
                    from_t(xsT[1 - s].rearrange("p k s -> p (k s)"), 512, 3)
                    silu(2)
                    from_t(hidT[:, 8:11].rearrange("p j n -> p (j n)"), 384, 4)
                    act.wait_ge(slots_used, e * STAGE + (NPRE + STAGE))
                    for b in range(2):
                        ins = nc.scalar.activation(out_e[:, b * 512:(b + 1) * 512], bank[6 + b][:], ACT.Copy)
                    ins.then_inc(d_drained, 1)

            for t in range(NT):
                act.wait_ge(acc_done, t + 1)
                link(act, chain, nc.scalar.activation(out_sq, acc[:, t], ACT.Square, accum_out=z_ss[:, t:t + 1]))
                nc.scalar.activation(z_sd[:, t:t + 1], z_ss[:, t:t + 1], ACT.Sqrt, scale=1.0 / D, bias=eps_col[:, 0:1])\
                    .then_inc(f_sd_ready, 1)
            for t in range(NT):
                act.wait_ge(f_ready, t + 1)
                act.dma_start(out_v[16 * t:16 * (t + 1)], fin[t]).then_inc(stored, 16)
            act.wait_ge(stored, 16 * NT)

        @block.vector
        def _(dve):
            chain = [dve_chain, 0]

            def copy_out(names):
                for name in mine(names, "dve"):
                    wait_fill(dve, name)
                    for dst, src in pieces(name):
                        ins = nc.vector.tensor_copy(dst, src)
                    drain_done(ins, name)

            nc.vector.memset(s_pad[:], 0.0).then_inc(dve_set, 1)
            nc.vector.memset(b_row[:], 0.0)
            nc.vector.memset(g_row[:], 1.0).then_inc(dve_set, 1)
            nc.vector.memset(one_col[:], 0.0)
            nc.vector.memset(eps_col[:], EPS).then_inc(dve_set, 1)
            dve.wait_ge(dve_set, 3)
            nc.vector.memset(one_col[0:64], 1.0).then_inc(dve_set, 1)
            for s, n in ((hid_ready, 3), (t_drained, 5), (m_drained, 8), (d_drained, 1)):
                dve.nop().then_inc(s, n)

            for t in range(NT + CT):
                rows = x_rows[:, t] if t < NT else ctx_rows[:, t - NT]
                dve.wait_ge(x_sd_ready, t + 1)
                link(dve, chain, nc.vector.reciprocal(x_rs[:, t:t + 1], x_sd[:, t:t + 1]))
                nc.vector.tensor_scalar(rows, rows, x_rs[:, t:t + 1], None, ALU.mult).then_inc(xn_ready, 1)

            dve.wait_ge(rows_loaded, 16 * 7)
            src = wait_fill(dve, ("mod", 0))
            drain_done(nc.vector.tensor_tensor(mod_row[:, 0], src[:], b_row[:, 0], ALU.add), ("mod", 0))
            src = wait_fill(dve, ("modT", 0))
            dve.wait_ge(consts_loaded, 16 * 3)
            v = src[:].rearrange("p (b g r) -> p g b r", b=4, g=4)
            for who in range(2):
                nc.vector.tensor_copy(mod_shift[:, who].rearrange("p (g b) -> p g b", g=2), v[:, 0:2, :, who])
                ins = nc.vector.scalar_tensor_tensor(
                    out=mod_scale[:, who].rearrange("p (g b) -> p g b", g=2), in0=v[:, 2:4, :, who], scalar=1.0,
                    in1=g_pre_col.rearrange("p (g b) -> p g b", g=2), op0=ALU.add, op1=ALU.mult)
            drain_done(ins, ("modT", 0))
            wait_drained(dve, ("modT", 0))
            for kt in range(1, KT, 2):
                b = wait_fill(dve, ("xT", kt))
                drain_done(nc.vector.tensor_scalar(hT[:, kt], b[:], mod_scale[:, 0, kt:kt + 1],
                                                   mod_shift[:, 0, kt:kt + 1], ALU.mult, ALU.add), ("xT", kt))
            for f in (1, 3):
                b = wait_fill(dve, ("cT", f))
                for j in range(2):
                    kt = 2 * f + j
                    ins = nc.vector.tensor_scalar(hcT[:, kt], b[:, j * CTX:(j + 1) * CTX], mod_scale[:, 1, kt:kt + 1],
                                                  mod_shift[:, 1, kt:kt + 1], ALU.mult, ALU.add)
                drain_done(ins, ("cT", f))
            dve.wait_ge(pool_set, 2)
            copy_out(EARLY)
            dve.wait_ge(raw_loaded, 16 * WIN_C)
            copy_out(GATES)
            for b in range(2):
                src = wait_fill(dve, ("u", b))
                wait_drained(dve, ("cg", b))
                z = z_sb[:, b, 8:520]
                drain_done(nc.vector.tensor_tensor(z, z, src[:], ALU.mult), ("u", b))
            wait_drained(dve, ("u", 1))
            nc.vector.memset(z_sb[:, :, 0:1], 0.0)
            nc.vector.tensor_copy(z_sb[:, :, 1:8], z_sb[:, :, 512:519])
            nc.vector.tensor_copy(z_sb[:, :, 520:527], z_sb[:, :, 9:16])
            link(dve, chain, nc.vector.memset(z_sb[:, :, 527:528], 0.0))
            for g in (1, 2):
                src = wait_fill(dve, ("mod", g))
                drain_done(nc.vector.tensor_tensor(mod_row[:, g], src[:], b_row[:, g], ALU.add), ("mod", g))
                wait_drained(dve, ("mod", g))
                nc.vector.scalar_tensor_tensor(
                    out=mod_row[:, g], in0=mod_row[:, g], scalar=0.0 if g == 1 else one_col[:, 0:1],
                    in1=g_row[:, g - 1], op0=ALU.add, op1=ALU.mult).then_inc(rows_ready, 1)
            dve.wait_ge(rows_ready, 2)
            copy_out([("dft1", b) for b in range(4)])
            wait_fill(dve, ("f", 1))
            wait_drained(dve, ("bg", 0))
            wait_drained(dve, ("bg", 1))
            for b in range(2):
                y = yT[:, 4 + b]
                link(dve, chain, nc.vector.tensor_scalar(y, z_sb[:, b, 0:512], conv_w[:, b, 0:1], None, ALU.mult))
                for j in (1, 2):
                    link(dve, chain, nc.vector.scalar_tensor_tensor(
                        out=y, in0=z_sb[:, b, 8 * j:8 * j + 512], scalar=conv_w[:, b, j:j + 1], in1=y,
                        op0=ALU.mult, op1=ALU.add))
                nc.vector.tensor_tensor(y, y, bg_sb[:, b], ALU.mult).then_inc(conv_ready, 1)
            for b in range(2):
                src = bank_of(("dft2", b))
                dve.wait_ge(odd_copied, b + 1)
                y = yT[:, 6 + b].rearrange("p (c r) -> p c r", r=8)
                even = src[:, 0:256].rearrange("p (c r) -> p c r", r=4)
                odd = dft_o[:, b].rearrange("p (c r) -> p c r", r=4)
                nc.vector.tensor_tensor(y[:, :, 0:4], even, odd, ALU.add)
                drain_done(nc.vector.tensor_tensor(y[:, :, 4:8], even, odd, ALU.subtract), ("dft2", b))

            us = units()
            n = len(us)
            for i in range(n + 4):
                if i < n:
                    t, h = us[i]
                    if i in (0, 2 * HEADS, 3 * HEADS):
                        dve.wait_ge(bias_ready, 1 + i // HEADS - (1 if i else 0))
                    s = wait_fill(dve, ("S", i))
                    nc.vector.tensor_tensor_reduce(
                        out=prob[i % 4][:, 0:256], in0=s[:, 0:256], in1=bias[1 if t == 0 else 0][:, h], scale=-SCALE,
                        scalar=-3 * MASKED, op0=ALU.add, op1=ALU.min, accum_out=win_max[:, i:i + 1])
                    link(dve, chain, nc.vector.tensor_reduce(ctx_max[:, i:i + 1], s[:, 256:512], AX_X, ALU.max))
                    nc.vector.tensor_scalar(neg_max[:, i:i + 1], ctx_max[:, i:i + 1], -SCALE, win_max[:, i:i + 1],
                                            ALU.mult, ALU.min).then_inc(scores_ready, 1)
                if 1 <= i <= n:
                    j = i - 1
                    wait_drained(dve, ("S", j))
                    link(dve, chain, nc.vector.tensor_tensor(total[:, j:j + 1], sums[:, j, 0:1], sums[:, j, 1:2], ALU.add))
                    nc.vector.reciprocal(inv[:, j:j + 1], total[:, j:j + 1]).then_inc(inv_ready, 1)
                if 2 <= i < n + 2:
                    j = i - 2
                    src = wait_fill(dve, ("PT", j))
                    drain_done(nc.vector.tensor_copy(probT[j % 4], src[:]), ("PT", j))

            for b, kts in enumerate(((4, 5), (6, 7), (0, 1, 2, 3))):
                wait_drained(dve, ("ss", b))
                link(dve, chain, nc.vector.reciprocal(rb[b], sd[b]))
                for kt in kts:
                    nc.vector.scalar_tensor_tensor(out=yT[:, kt], in0=yT[:, kt], scalar=g_mix_col[:, kt:kt + 1],
                                                   in1=rb[b], op0=ALU.mult, op1=ALU.mult).then_inc(yT_ready, 1)
            copy_out([("bc", b) for b in range(8)])
            wait_drained(dve, ("bc", 6))
            for t in range(NT):
                dve.wait_ge(y_sums, t + 1)
                nc.vector.tensor_tensor(y_s1[:, t:t + 1], y_ss[:, t, 0:1], y_ss[:, t, 1:2], ALU.add).then_inc(y_added, 1)
                dve.wait_ge(y_sd_ready, t + 1)
                link(dve, chain, nc.vector.reciprocal(y_rs[:, t:t + 1], y_sd[:, t:t + 1]))
                if t >= 2:
                    dve.wait_ge(x1_ready, t - 1)
                for b in range(2):
                    half = slice(b * 512, (b + 1) * 512)
                    ins = nc.vector.scalar_tensor_tensor(
                        out=y_tmp[t % 2][:, half], in0=bank_of(("y", t, b))[:], scalar=y_rs[:, t:t + 1],
                        in1=gain1[:, half], op0=ALU.mult, op1=ALU.mult)
                    drain_done(ins, ("y", t, b))
                dve.wait_ge(z_sd_ready, t + 1)
                link(dve, chain, nc.vector.reciprocal(z_rs[:, t:t + 1], z_sd[:, t:t + 1]))
                nc.vector.scalar_tensor_tensor(out=h2[:, t], in0=x1[:, t], scalar=z_rs[:, t:t + 1], in1=gain2,
                                               op0=ALU.mult, op1=ALU.mult).then_inc(h2_scaled, 1)

            wait_drained(dve, ("rt", NT - 1))
            link(dve, chain, nc.vector.tensor_reduce(r_max[:], logit[:], AX_X, ALU.max))
            nc.vector.tensor_tensor(logit[:], logit[:], r_max[:].rearrange("p (t a) -> p t a", a=1).to_broadcast([P, NT, E]),
                                    ALU.subtract).then_inc(r_sub_ready, 1)
            dve.wait_ge(r_exp_ready, 1)
            link(dve, chain, nc.vector.tensor_reduce(r_sum[:], aff[:], AX_X, ALU.add))
            link(dve, chain, nc.vector.reciprocal(r_inv[:], r_sum[:]))
            nc.vector.tensor_tensor(aff[:], aff[:], r_inv[:].rearrange("p (t a) -> p t a", a=1).to_broadcast([P, NT, E]),
                                    ALU.mult).then_inc(aff_ready, 1)
            src = wait_fill(dve, ("affT", 0))
            nc.vector.memset(one_row, 1.0)
            drain_done(nc.vector.tensor_copy(work, src[0:E]), ("affT", 0))
            wait_drained(dve, ("affT", 0))
            for _ in range(CAP // 8):
                link(dve, chain, nc.vector.max(top8[0:E], work))
                link(dve, chain, nc.vector.match_replace(work, top8[0:E], work, -1.0))
            link(dve, chain, nc.vector.tensor_scalar(chosen, work, 0.0, None, ALU.is_lt))
            link(dve, chain, nc.vector.tensor_tensor_scan(count, one_row, chosen, 0.0, ALU.mult, ALU.add))
            nc.vector.tensor_tensor(rank, count, chosen, ALU.mult).then_inc(rank_ready, 1)
            src = wait_fill(dve, ("posT", 0))
            ins = nc.vector.tensor_copy(place[:, :, 0:E], src[:, 0:NT * E].rearrange("p (t e) -> p t e", t=NT))
            drain_done(ins, ("posT", 0))
            wait_drained(dve, ("posT", 0))

            def slots_of(dst, e, width):
                nos = iota[:, 0:width].rearrange("p (a s) -> p a s", a=1).to_broadcast([P, NT, width])
                return nc.vector.tensor_tensor(dst, nos, place[:, :, bass.ds(e, 1)].to_broadcast([P, NT, width]),
                                               ALU.is_equal)

            slots_of(pick, 0, CAP).then_inc(pick_ready, 1)
            dve.wait_ge(start_zero, 1)

            with dve.Fori(0, E // 2) as pair:
                for s in range(2):
                    e = pair * 2 + s
                    for i in range(8):
                        t, b = i // 2, i % 2
                        v = acc[:, t, b * 512:(b + 1) * 512]
                        dve.wait_ge(m_filled, e * 8 + (i + 1))
                        nc.vector.tensor_tensor(v, v, bank[5][:], ALU.add).then_inc(m_drained, 1)
                    dve.wait_ge(t_drained, e * 5 + 2)
                    slots_of(gate_pick, e, 2 * CAP).then_inc(gate_pick_ready, 1)
                    dve.wait_ge(gate_pick_ready, e * 2 + 1)
                    nc.vector.tensor_tensor(gate_pick, gate_pick, aff[:, :, bass.ds(e, 1)].to_broadcast([P, NT, 2 * CAP]),
                                            ALU.mult).then_inc(gate_pick_ready, 1)
                    dve.wait_ge(t_drained, e * 5 + 4)
                    slots_of(pick, e + 1, CAP).then_inc(pick_ready, 1)
                    for c in range(3):
                        q = (3 * s + c) % 2
                        w = HALVES[c]
                        dve.wait_ge(silu_done, e * 3 + (c + 1))
                        nc.vector.tensor_tensor(hid[q][:, 0:w], silu_g[q][:, 0:w], bank[2 + q][:, 0:w], ALU.mult)\
                            .then_inc(hid_ready, 1)

            def scale_last(t):
                dve.wait_ge(f_sd_ready, t + 1)
                link(dve, chain, nc.vector.reciprocal(z_rs[:, t:t + 1], z_sd[:, t:t + 1]))
                nc.vector.scalar_tensor_tensor(out=fin[t], in0=acc[:, t], scalar=z_rs[:, t:t + 1], in1=gain4,
                                               op0=ALU.mult, op1=ALU.mult).then_inc(f_scaled, 1)

            for t in range(NT):
                for b in range(2):
                    v = acc[:, t, b * 512:(b + 1) * 512]
                    dve.wait_ge(last_filled, 2 * t + b + 1)
                    ins = nc.vector.tensor_tensor(v, v, bank[2 * t + b][:], ALU.add)
                ins.then_inc(acc_done, 1)
                if t >= 1:
                    scale_last(t - 1)
            scale_last(NT - 1)

        @block.tensor
        def _(pe):
            mm = nc.tensor.matmul

            def turn(dst, src):
                return nc.tensor.transpose(dst, src, ident[0:src.shape[0], 0:src.shape[0]])

            def product(dst, terms):
                for j, (a, b) in enumerate(terms):
                    ins = mm(dst, a, b, start=j == 0, stop=j == len(terms) - 1)
                return ins

            owed = [False]

            def used(ins):
                ins.then_inc(slots_used, 1)

            def used_up_by(ins):
                if owed[0]:
                    used(ins)
                    owed[0] = False

            def transpose_x(kt):
                b = open_fill(pe, ("xT", kt))
                for t in range(NT):
                    ins = turn(b[:, t * P:(t + 1) * P], x_rows[:, t, kt * P:(kt + 1) * P])
                fill_done(ins, ("xT", kt))

            def mod_rows(g):
                b = open_fill(pe, ("mod", g))
                for k in range(KT):
                    w = wait_slot(pe, ("mod", g, k))
                    for j in range(4):
                        ins = mm(b[32 * j:32 * (j + 1)], s_pad[:, k], w[:, j * 512:(j + 1) * 512],
                                 start=k == 0, stop=k == KT - 1)
                        if j == 0 and k == 0:
                            used_up_by(ins)
                    if k < KT - 1:
                        used(ins)
                fill_done(ins, ("mod", g))
                owed[0] = True

            def product(name, dst, terms, last_of=None, part=(True, True)):
                for j, (a, b) in enumerate(terms):
                    ins = mm(dst, a, b, start=j == 0, stop=j == len(terms) - 1)
                    if part[0] and j == 0:
                        used_up_by(ins)
                    if last_of is not None and j == 3:
                        used(ins)
                if part[1]:
                    fill_done(ins, name)
                if last_of is not None:
                    owed[0] = True

            pe.wait_ge(ident_loaded, 16)
            pe.wait_ge(xn_ready, NT)
            for kt in range(6):
                transpose_x(kt)
            pe.wait_ge(silu_ready, 1)
            mod_rows(0)
            wait_drained(pe, ("mod", 0))
            b = open_fill(pe, ("modT", 0))
            for j in range(4):
                ins = turn(b[:, j * P:(j + 1) * P], mod_row[:, 0, j * P:(j + 1) * P])
                if j == 0:
                    used_up_by(ins)
            fill_done(ins, ("modT", 0))
            for kt in (6, 7):
                transpose_x(kt)
            pe.wait_ge(xn_ready, NT + CT)
            for f in range(4):
                b = open_fill(pe, ("cT", f))
                for j in range(4):
                    kt, t = 2 * f + j // 2, j % 2
                    ins = turn(b[:, j * P:(j + 1) * P], ctx_rows[:, t, kt * P:(kt + 1) * P])
                fill_done(ins, ("cT", f))

            def w_cols(g, k, c0, n):
                w = wait_slot(pe, ("in", g, k // 4))
                return w.rearrange("p (k n) -> p k n", k=4)[:, k % 4, c0:c0 + n]

            def columns(name, g, blk, last=False):
                b = open_fill(pe, name)
                product(name, b[:], [(w_cols(g, k, blk * P, P), hT[:, k]) for k in range(KT)], g if last else None)

            wait_drained(pe, ("xT", 6))
            wait_drained(pe, ("xT", 7))
            wait_drained(pe, ("cT", 2))
            wait_drained(pe, ("cT", 3))
            for f in range(2):
                b = open_fill(pe, ("kc", f))
                for j in range(2):
                    product(("kc", f), b[:, j * CTX:(j + 1) * CTX],
                            [(w_cols(IN_K, k, (2 * f + j) * P, P), hcT[:, k]) for k in range(KT)],
                            part=(j == 0, j == 1))
            for blk in range(4):
                columns(("k", blk), IN_K, blk, blk == 3)
            for blk in range(4):
                columns(("q", blk), IN_Q, blk, blk == 3)
            for t in range(CT):
                b = open_fill(pe, ("vc", t))
                product(("vc", t), b[:], [(hcT[:, k, t * P:(t + 1) * P], w_cols(IN_V, k, 0, NA_W)) for k in range(KT)])
            for t in range(3):
                b = open_fill(pe, ("v", t))
                product(("v", t), b[:], [(hT[:, k, 64 + t * P:64 + (t + 1) * P], w_cols(IN_V, k, 0, NA_W))
                                         for k in range(KT)])
            b = open_fill(pe, ("v", 3))
            for k in range(KT):
                mm(b[0:64], hT[:, k, 0:64], w_cols(IN_V, k, 0, NA_W), start=k == 0, stop=k == KT - 1)
                ins = mm(b[64:P], hT[:, k, SEQ - 64:SEQ], w_cols(IN_V, k, 0, NA_W), start=k == 0, stop=k == KT - 1)
                if k == 3:
                    used(ins)
            fill_done(ins, ("v", 3))
            owed[0] = True
            for name, g, last in (("bg", IN_BC, 0), ("cg", IN_BC, 1), ("u", IN_UF, 0), ("f", IN_UF, 1)):
                for blk in range(2):
                    columns((name, blk), g, 2 * last + blk, bool(last and blk))
            for g in (1, 2):
                mod_rows(g)

            for b in range(2):
                wait_drained(pe, ("f", b))
            pe.wait_ge(consts_loaded, 16 * 3)
            for blk in range(4):
                b = open_fill(pe, ("dft1", blk))
                for ch in range(2):
                    product(("dft1", blk), b[:, ch * 256:(ch + 1) * 256], [(f_sb[:, ch, blk * P:(blk + 1) * P], dd[:])],
                            part=(ch == 0, ch == 1))
            tables = wait_slot(pe, ("dft", 0, 0)).rearrange("p (e h s n) -> p e h s n", e=2, h=2, s=2)
            for blk in range(4):
                wait_drained(pe, ("dft1", blk))
            for ch in range(2):
                b = open_fill(pe, ("dft2", ch))
                for par in range(2):
                    product(("dft2", ch), b[:, par * 256:(par + 1) * 256],
                            [(dft_g[:, 2 * par + half, ch * 256 + cs * P:ch * 256 + (cs + 1) * P],
                              tables[:, par, half, cs]) for half in range(2) for cs in range(2)],
                            part=(par == 0, par == 1))
            owed[0] = True

            us = units()
            n = len(us)

            def scores(i):
                t, h = us[i]
                b = open_fill(pe, ("S", i))
                q, keys = qTp[:, h, t * P:(t + 1) * P], kT[:, h // 2]
                at_ends = keys.rearrange("p (a b) -> p a b", b=64)[:, 0:8:7, :]
                for j, kt in enumerate(KEY_TILES[t]):
                    kv = at_ends if kt == 3 else keys[:, 64 + kt * P:64 + (kt + 1) * P]
                    dst = b[:, j * P:(j + 1) * P]
                    if kt == 3:
                        dst = dst.rearrange("p (a b) -> p a b", b=64)
                    ins = mm(dst, q, kv, start=True, stop=True)
                    if j == 0:
                        used_up_by(ins)
                fill_done(mm(b[:, 256:512], q, kcT[:, h // 2], start=True, stop=True), ("S", i))

            for name in [("k", b) for b in range(4)] + [("q", b) for b in range(4)] + [("kc", 1)]:
                wait_drained(pe, name)
            for name in [("v", b) for b in range(4)] + [("vc", b) for b in range(2)]:
                wait_drained(pe, name)
            for i in range(n + 4):
                if i < n:
                    scores(i)
                if 2 <= i < n + 2:
                    j = i - 2
                    b = open_fill(pe, ("PT", j))
                    pe.wait_ge(prob_ready, j + 1)
                    for m in range(4):
                        ins = turn(b[:, m * P:(m + 1) * P], prob[j % 4][:, m * P:(m + 1) * P])
                    fill_done(ins, ("PT", j))
                if i >= 4 and i % 2 == 1:
                    b = open_fill(pe, ("PO", i - 4))
                    wait_drained(pe, ("PT", i - 4))
                    for m in range(4):
                        for j in (i - 5, i - 4):
                            t, h = us[j]
                            hh = slice(h * DH, (h + 1) * DH)
                            v = v_sb[:, KEY_TILES[t][m], hh] if m < 2 else vc_sb[:, m - 2, hh]
                            p0 = (h % 2) * 64
                            ins = mm(b[p0:p0 + 64, 0:P], v, probT[j % 4][:, m * P:(m + 1) * P],
                                     start=m == 0, stop=m == 3)
                    fill_done(ins, ("PO", i - 4))

            pe.wait_ge(pool_set, 4)
            j = 0
            for g, count_ in enumerate((2, 2, 4)):
                b = open_fill(pe, ("ss", g))
                for m in range(count_):
                    pe.wait_ge(squares_ready, j + 1)
                    ins = mm(b[:], ones[:], sq[j % 2], start=m == 0, stop=m == count_ - 1)
                    ins.then_inc(squares_used, 1)
                    j += 1
            pe.wait_ge(rows_ready, 2)
            for v in range(8):
                b = open_fill(pe, ("bc", v))
                fill_done(mm(b[:], sel[:, v % 4], mod_row[:, 1 + v // 4], start=True, stop=True), ("bc", v))
            pe.wait_ge(yT_ready, KT)
            for t in range(NT + 1):
                if t < NT:
                    for b_ in range(2):
                        name = ("y", t, b_)
                        b = open_fill(pe, name)
                        for k in range(KT):
                            w = wait_slot(pe, ("out", 0, k // 2)).rearrange("p (k n) -> p k n", k=2)
                            ins = mm(b[:], yT[:, k, t * P:(t + 1) * P], w[:, k % 2, b_ * 512:(b_ + 1) * 512],
                                     start=k == 0, stop=k == KT - 1)
                            if t == NT - 1 and b_ == 1 and k in (1, 3, 5):
                                used(ins)
                        fill_done(ins, name)
                    owed[0] = t == NT - 1
                if t >= 1:
                    u = t - 1
                    pe.wait_ge(h2_ready, u + 1)
                    for b_ in range(2):
                        b = open_fill(pe, ("h2T", u, b_))
                        for j in range(4):
                            kt = 4 * b_ + j
                            ins = turn(b[:, j * P:(j + 1) * P], h2[:, u, kt * P:(kt + 1) * P])
                            if j == 0:
                                used_up_by(ins)
                        fill_done(ins, ("h2T", u, b_))
                    b = open_fill(pe, ("rt", u))
                    wait_drained(pe, ("h2T", u, 1))
                    product(("rt", u), b[:, 0:E], [(h2T[u % 2][:, k], w_rt[:, k]) for k in range(KT)])
            pe.wait_ge(aff_ready, 1)
            b = open_fill(pe, ("affT", 0))
            for t in range(NT):
                ins = turn(b[0:E, t * P:(t + 1) * P], aff[:, t])
            fill_done(ins, ("affT", 0))
            pe.wait_ge(rank_ready, 1)
            b = open_fill(pe, ("posT", 0))
            for t in range(NT):
                ins = turn(b[:, t * E:(t + 1) * E], rank[:, t * P:(t + 1) * P])
            fill_done(ins, ("posT", 0))

            def gather(dst, kt):
                for t in range(NT):
                    ins = mm(dst[:, kt * CAP:(kt + 1) * CAP], h2[:, t, kt * P:(kt + 1) * P], pick[:, t],
                             start=t == 0, stop=t == NT - 1)
                return ins

            pe.wait_ge(pick_ready, 1)
            b = open_fill(pe, ("xs", 0))
            for kt in range(KT):
                ins = gather(b, kt)
            fill_done(ins, ("xs", 0))
            wait_drained(pe, ("xs", 0))
            wait_drained(pe, ("posT", 0))
            pe.wait_ge(start_zero, 3)

            gate_b, up_b, turn_b, mix_b, down_b = bank[0:2], bank[2:4], bank[4], bank[5], bank[6:8]

            def combine(dst, s, i):
                t, b_ = i // 2, i % 2
                return mm(dst[:], gateT[s][:, t * P:(t + 1) * P], out_e[:, b_ * 512:(b_ + 1) * 512], start=True, stop=True)

            with pe.Fori(0, E // 2) as pair:
                for s in range(2):
                    e = pair * 2 + s

                    def open_turn(fill):
                        pe.wait_ge(t_drained, e * 5 + (5 + fill))

                    def hidden(c, fill):
                        q = (3 * s + c) % 2
                        pe.wait_ge(hid_ready, e * 3 + (c + 4))
                        open_turn(fill)
                        for j in range(HALVES[c] // P):
                            ins = turn(turn_b[:, j * P:(j + 1) * P], hid[q][:, j * P:(j + 1) * P])
                        ins.then_inc(t_filled, 1)

                    def down(j):
                        i = GU_SLOTS + j
                        n_ = (NPRE + i) % RING
                        pe.wait_ge(loaded[n_], loads_until(e, i))
                        w = ring[:, n_].rearrange("p (h n) -> p h n", h=2)
                        for b_ in range(2):
                            for half in range(2):
                                ins = mm(down_b[b_][64 * half:64 * half + 64], hidT[:, j, 64 * half:64 * half + 64],
                                         w[:, half, b_ * 512:(b_ + 1) * 512], start=j == 0, stop=j == DOWN_SLOTS - 1)
                        used(ins)

                    for c in range(3):
                        q, w_ = (3 * s + c) % 2, HALVES[c]
                        pe.wait_ge(hid_ready, e * 3 + (c + 2))
                        for k in range(KT):
                            for which, banks in ((0, gate_b), (1, up_b)):
                                i = 8 * c + 2 * (k // 2) + which
                                n_ = (NPRE + i) % RING
                                if k % 2 == 0:
                                    pe.wait_ge(loaded[n_], loads_until(e, i))
                                w = ring[:, n_, (k % 2) * 2 * w_:(k % 2 + 1) * 2 * w_]
                                for half in range(2):
                                    ins = mm(banks[q][64 * half:64 * half + 64, 0:w_], xsT[s][:, k],
                                             w[:, half * w_:(half + 1) * w_], start=k == 0, stop=k == KT - 1)
                                if k % 2:
                                    used(ins)
                            if c == 0:
                                pe.wait_ge(m_drained, e * 8 + (8 + k))
                                if k == 0:
                                    pe.wait_ge(d_drained, e + 1)
                                combine(mix_b, 1 - s, k).then_inc(m_filled, 1)
                            if (c, k) == (1, 1):
                                hidden(0, 0)
                            if (c, k) == (1, 3):
                                pe.wait_ge(gate_pick_ready, e * 2 + 2)
                                open_turn(1)
                                for t in range(NT):
                                    ins = turn(turn_b[:, t * P:(t + 1) * P], gate_pick[:, t])
                                ins.then_inc(t_filled, 1)
                            if (c, k) == (2, 1):
                                hidden(1, 2)
                            if c == 2 and 3 <= k < 7:
                                if k == 3:
                                    pe.wait_ge(pick_ready, e + 2)
                                    open_turn(3)
                                gather(turn_b, 2 * (k - 3))
                                ins = gather(turn_b, 2 * (k - 3) + 1)
                                if k == 6:
                                    ins.then_inc(t_filled, 1)
                    pe.wait_ge(d_drained, e + 1)
                    for j in range(8):
                        down(j)
                    hidden(2, 4)
                    pe.wait_ge(t_drained, e * 5 + 10)
                    for j in range(8, DOWN_SLOTS):
                        down(j)

            pe.wait_ge(d_drained, E + 1)
            pe.wait_ge(hid_ready, 3 + 3 * E)
            pe.wait_ge(m_drained, 8 + 8 * E)
            pe.wait_ge(t_drained, 5 + 5 * E)
            for i in range(8):
                combine(bank[i], 1, i).then_inc(last_filled, 1)


def constants():
    ident = np.eye(P)
    sel = np.zeros((P, 4, P))
    for g in range(4):
        sel[32 * g, g, :] = 1.0
    slots = np.tile(np.arange(1, CAP + 1), (P, 2))
    k = np.arange(64)
    a = 2 * np.pi * np.outer(k, k) / 64
    dd = np.zeros((P, 2, P))
    for g in range(2):
        dd[64 * g:64 * g + 64, 0, 64 * g:64 * g + 64] = np.cos(a)
        dd[64 * g:64 * g + 64, 1, 64 * g:64 * g + 64] = np.sin(a)
    consts = np.concatenate([ident, sel.reshape(P, -1), slots, dd.reshape(P, -1)], axis=1).astype(np.float32)
    dft = np.zeros((P, 2, 2, 2, 256))
    c16, r8 = np.divmod(np.arange(P), ROWS)
    cf, rf = np.divmod(np.arange(256), 4)
    m = rf * GRID_W + cf
    for par in range(2):
        for half in range(2):
            token = r8 * GRID_W + 32 * half + 2 * c16 + par
            a = 2 * np.pi * (np.outer(token, m) % SEQ) / SEQ
            dft[:, par, half, 0] = np.cos(a)
            dft[:, par, half, 1] = -np.sin(a)
    dft /= np.sqrt(SEQ * 64.0)
    return consts, dft.reshape(P, SLOT).astype(np.float32)


_INS = ["x", "cT", "ctx", "w_mod", "b_mod", "colv", "g_post_mix", "g_pre_ffn", "g_post_ffn", "w_in", "rpbT", "w_out",
        "w_router", "w_gate", "w_up", "w_down", "consts", "dft"]


def lay_out(inputs):
    a = {k: np.ascontiguousarray(v) for k, v in inputs.items()}

    def by_partition(v):
        return v.reshape(-1, P).T

    a["cT"] = np.ascontiguousarray(np.stack([by_partition(a["c"]), by_partition(a["c_ctx"])], axis=-1))
    conv = a["conv_w"][0].reshape(3, 2, P).transpose(2, 1, 0).reshape(P, 6)
    a["colv"] = np.ascontiguousarray(
        np.concatenate([by_partition(a["g_pre_mix"]), by_partition(a["g_mix_out"]), conv], axis=1))
    a["rpbT"] = np.ascontiguousarray(a["rpb"][0].transpose(0, 2, 1))
    a["w_router"] = np.ascontiguousarray(a["w_router"][0].reshape(KT, P, E).transpose(1, 0, 2))
    a["consts"], a["dft"] = constants()
    return {k: a[k] for k in _INS}


def kernel(**inputs):
    import concourse.bacc as bacc
    from concourse.bass_utils import run_bass_kernel_spmd

    nc = bacc.Bacc("TRN2", target_bir_lowering=False, num_devices=1, dynamic_dma_scratch_size=1024)
    arrays, args = {}, []
    for name, a in lay_out(inputs).items():
        arrays[f"in_{name}"] = a
        args.append(nc.dram_tensor(f"in_{name}", a.shape, mybir.dt.from_np(a.dtype), kind="ExternalInput").ap())
    args.append(nc.dram_tensor("out_x", (1, SEQ, D), F32, kind="ExternalOutput").ap())
    build_block(nc, *args)
    r = run_bass_kernel_spmd(nc, [arrays], core_ids=[0])
    return r.results[0]["out_x"]
```

```python
from contextlib import ExitStack

import numpy as np

import concourse.bass as bass
from concourse import mybir

F32 = mybir.dt.float32
ALU = mybir.AluOpType
ACT = mybir.ActivationFunctionType
AX_X = mybir.AxisListType.X

P = 128
D = 1024
KT = D // P
SEQ, CTX = 512, 256
NT = SEQ // P
CT = CTX // P
GRID_W, ROWS = 64, 8
HEADS, DH = 8, 64
PAIRS = HEADS // 2
WIN_C = 16
NA_W, CONV_W, FO_W = 512, 256, 256
EPS = 1e-6
MASKED = -1e30
SCALE = DH ** -0.5
E, CAP = 16, 64
HID = 2816

Q_TILES = (1, 2, 0, 3)
KEY_TILES = {0: (3, 0), 1: (0, 1), 2: (1, 2), 3: (2, 3)}

RING = 10
SLOT = 2048
HALVES = (512, 512, 384)
CHUNK0 = (0, 1024, 2048)
GU_SLOTS = len(HALVES) * 8
HB = [(c, j) for c in range(3) for j in range(HALVES[c] // P)]
DOWN_SLOTS = len(HB)
STAGE = GU_SLOTS + DOWN_SLOTS
SPARE = 4
BIG_RING = RING + SPARE
assert 2 * STAGE % BIG_RING == 0
PRE = [("mod", 0, k) for k in range(KT)] + [("in", 0, h) for h in range(2)]
for g in range(1, 5):
    PRE += [("mod", (g + 1) // 2, 4 * ((g + 1) % 2) + k) for k in range(4)] + [("in", g, h) for h in range(2)]
PRE += [("dft", 0, 0)] + [("out", 0, k) for k in (2, 3, 0, 1)]
NPRE = len(PRE)
USED0 = NPRE + SPARE
IN_K, IN_Q, IN_V, IN_BC, IN_UF = range(5)
IN_COLS = (512, 0, 1024, 1536, 2048)


UNITS = [(t, h) for t in Q_TILES for h in range(HEADS)]
N = len(UNITS)
STEPS = 3
TAIL = 16
AFTER = HEADS + 4


def pre_fills():
    every, ev = tuple(range(8)), ("act", "dve")
    out = [(("xT", k), ev[k % 2], every) for k in range(6)]
    out += [(("mod", 0), "first", every), (("modT", 0), "first", every)]
    out += [(("xT", k), ev[k % 2], every) for k in (6, 7)]
    six, two = tuple(range(6)), (6, 7)
    out += [(("k", b), ev[b % 2], six) for b in range(4)]
    out += [(("cT", k), ev[k % 2], six) for k in range(4)]
    names = [("kc", b) for b in range(2)] + [("q", b) for b in range(4)] + [("v", b) for b in range(4)] \
        + [("vc", b) for b in range(CT)] + [("bg", b) for b in range(2)] + [("cg", b) for b in range(2)]
    for i, name in enumerate(names):
        if name in (("q", 0), ("bg", 0)):
            out.append((("mod", 1 if name[0] == "q" else 2), "mod", two))
        out.append((name, ev[i % 2], six))
    out += [(("u", b), "dve", six) for b in range(2)] + [(("f", b), "act", six) for b in range(2)]
    out += [(("dft1", b), ev[b % 2], every) for b in range(4)]
    out += [(("modT", g), "dve", every) for g in (1, 2)]
    out += [(("bc", b), ev[b % 2], every) for b in range(2)]
    out += [(("dft2", b), "dft2", every) for b in range(2)]
    for i in range(N + TAIL):
        if i < N:
            out.append((("S", i), "S", (0, 1)))
        if STEPS <= i < N + STEPS:
            out.append((("PT", i - STEPS), "PT", (3, 4)))
        if STEPS + 3 <= i <= N + STEPS + 1 and i % 2 == 0:
            out.append((("PO", i - STEPS - 2), "PO", (5,)))
        for name in extra_fills(i):
            out.append((name, name[0], (2, 6, 7)))
    out += [(("affT", 0), "affT", every), (("posT", 0), "posT", every), (("xs", 0), "xs", every)]
    return out


def tile_at(i, offset):
    j, rest = divmod(i - offset - AFTER, HEADS)
    return j if rest == 0 and 0 <= j < NT else None


def extra_fills(i):
    out = []
    if i in (1, 4):
        out.append(("sq", i // 4))
    if i in (3, 6):
        out.append(("rs", i // 6))
    for offset, names in ((9, [("rt",)]), (-3, [("cf", 0)]), (-2, [("cf", 1)]), (1, [("ss",), ("na", 0)]), (2, [("na", 1)]),
                          (7, [("h2Ta",), ("h2Tb",)])):
        j = tile_at(i, offset)
        if j is not None:
            out += [(n[0], j, *n[1:]) for n in names]
    if i == N + 6:
        out += [("last_bc", 2), ("last_bc", 3)]
    return out


def build_block(nc, x, cT, ctx, w_mod, b_mod, colv, g_post_mix, g_pre_ffn, g_post_ffn, w_in, rpbT, w_out,
                w_router, w_gate, w_up, w_down, consts, dft, out):
    fills = pre_fills()
    number = {name: i for i, (name, _, _) in enumerate(fills)}
    stream = {name: st for name, st, _ in fills}
    turn_no, bank_no, bank_before, in_stream, last_in, turns = {}, {}, {}, {}, {}, {}
    for name, st, banks in fills:
        turn_no[name] = in_stream[st] = in_stream.get(st, 0) + 1
        k = turns[banks] = turns.get(banks, -1) + 1
        bank_no[name] = banks[k % len(banks)]
        bank_before[name] = last_in.get(bank_no[name])
        last_in[bank_no[name]] = name

    with ExitStack() as stack:
        def sb(name, *shape):
            return stack.enter_context(nc.sbuf_tensor(name, [P, *shape], F32))

        def sem(name):
            return stack.enter_context(nc.semaphore(name))

        bank = [stack.enter_context(nc.psum_tensor(f"bank{i}", [P, 512], F32)) for i in range(8)]

        ring_ = sb("ring", RING, SLOT)
        cst = sb("cst", P + 2 * CAP)
        ident, iota = cst[:, 0:P], cst[:, P:P + 2 * CAP]
        ones = sb("ones", 128)
        cols = sb("cols", 22)
        g_pre_col, g_mix_col = cols[:, 0:8], cols[:, 8:16]
        conv_w = cols[:, 16:22].rearrange("p (b j) -> p b j", b=2)
        w_rt = sb("w_rt", KT, E)
        dd = sb("dd", 256)
        c_sb = sb("c_sb", KT, 2)
        s_pad = sb("s_pad", KT, 32)
        mod_row = sb("mod_row", 3, 512)
        one_col = sb("one_col", 1)
        mod_scale, mod_shift = sb("mod_scale", 2, KT), sb("mod_shift", 2, KT)
        ffn_gain, ffn_shift = sb("ffn_gain", KT), sb("ffn_shift", KT)
        minus_half = sb("minus_half", 1)
        x_ss, x_ms, x_rs = sb("x_ss", 6), sb("x_ms", 6), sb("x_rs", 6)
        neg_max, win_max, ctx_max = sb("neg_max", 32), sb("win_max", 32), sb("ctx_max", 32)
        sums, total, inv = sb("sums", 32, 2), sb("total", 32), sb("inv", 32)
        cf_ms, cf_rs = sb("cf_ms", 2, NT), sb("cf_rs", 2, NT)
        na_ms, na_rs = sb("na_ms", NT), sb("na_rs", NT)
        y_ss, y_ms, y_rs = sb("y_ss", NT), sb("y_ms", NT), sb("y_rs", NT)
        z_ss, z_ms, z_rs = sb("z_ss", NT), sb("z_ms", NT), sb("z_rs", NT)
        logit, aff = sb("logit", NT, E), sb("aff", NT, E)
        r_max, r_sum, r_inv = sb("r_max", NT), sb("r_sum", NT), sb("r_inv", NT)
        place = sb("place", NT, E + 2)
        top8 = sb("top8", 8)

        arena = sb("arena", 130 * 256)

        def at(kb, *shape):
            n = int(np.prod(shape))
            o = int(kb * 256)
            v = arena[:, o:o + n]
            if len(shape) == 2:
                v = v.rearrange("p (a b) -> p a b", a=shape[0])
            if len(shape) == 3:
                v = v.rearrange("p (a b c) -> p a b c", a=shape[0], b=shape[1])
            return v

        HEAD_W = (2 * WIN_C - 1) * ROWS
        SHIFTED = 64 + HEADS * HEAD_W + 64
        ring = [ring_[:, n] for n in range(RING)] + [at(k, SLOT) for k in (72, 80, 92, 118)]
        hT, hcT = at(0, KT, SEQ), at(16, KT, CTX)
        shifted = at(72, SHIFTED)[0:ROWS]
        ctx_rows = at(88, CT, D)
        x_rows = at(102, NT, D)
        b_row, g_row = at(118, 3, 512), at(124, 2, 512)
        dft_g = at(88, 4, 512)
        dft_o = at(96, 2, 256)
        bg_sb, z_sb, f_sb = at(102, 2, SEQ), at(106, 2, 528), at(110.25, 2, SEQ)
        ycf = at(0, 4, SEQ)
        yna = [at(8 + 2 * i, PAIRS, P) for i in range(2)]
        na_sq = mod_row[:, 0]
        gain1 = at(12, D)
        x1 = at(16, NT, D)
        qTp = at(32, HEADS, SEQ)
        kT, kcT = at(48, PAIRS, SEQ), at(56, PAIRS, CTX)
        v_sb, vc_sb = at(60, 4, NA_W), at(68, CT, NA_W)
        bias = [at(72, HEADS, 256), at(80, HEADS, 256)]
        prob = [at(88 + 2 * i, 512) for i in range(3)] + [at(128, 512)]
        probT = [at(94 + 2 * i, 512) for i in range(4)]
        xn2 = at(102, NT, D)
        y_tmp = at(118, D)
        squares_out = [at(k, 512).bitcast(mybir.dt.bfloat16) for k in (98, 122)]
        h2T = at(124, KT, P)
        cf_sq = [at(118, 512), at(120, 512)]
        xsT = [at(0, KT, CAP), at(2, KT, CAP)]
        gain4 = at(4, D)
        out_e = at(8, D)
        acc = at(32, NT, D)
        silu_g = [at(48, 512), at(50, 512)]
        hid = [at(52, 512), at(54, 512)]
        hidT = at(56, DOWN_SLOTS, P)
        gateT = [at(62, 512), at(64, 512)]
        pick = at(66, NT, CAP)
        gate_pick = at(68, NT, 2 * CAP)
        fin = [at(102 + 4 * t, D) for t in range(NT)]
        work, chosen, count, one_row, rank = [at(k, 512)[0:E] for k in (70, 88, 90, 126, 128)]

        loaded = [sem(f"slot_loaded{i}") for i in range(BIG_RING)]
        x_loaded = [sem(f"x_loaded{t}") for t in range(NT)]
        c_loaded, ident_loaded, consts_loaded = sem("c_loaded"), sem("ident_loaded"), sem("consts_loaded")
        rows_loaded, ctx_loaded, shifted_loaded = sem("rows_loaded"), sem("ctx_loaded"), sem("shifted_loaded")
        shifted_stored = sem("shifted_stored")
        raw_loaded = [sem(f"raw_loaded{i}") for i in range(3)]
        x_again, stored = sem("x_again"), sem("stored")
        filled = {st: sem(f"filled_{st}") for st in in_stream}
        drained = {st: sem(f"drained_{st}") for st in in_stream}
        slots_used = sem("slots_used")
        pool_set, dve_set = sem("pool_set"), sem("dve_set")
        act_chain, dve_chain, pool_chain = sem("act_chain"), sem("dve_chain"), sem("pool_chain")
        silu_ready, x_ss_ready, x_rs_ready, xn_ready = (
            sem("silu_ready"), sem("x_ss_ready"), sem("x_rs_ready"), sem("xn_ready"))
        rows_ready, bias_ready, odd_copied = sem("rows_ready"), sem("bias_ready"), sem("odd_copied")
        scores_ready, inv_ready, prob_ready = sem("scores_ready"), sem("inv_ready"), sem("prob_ready")
        conv_ready, cf_sq_ready, cf_rs_ready = sem("conv_ready"), sem("cf_sq_ready"), sem("cf_rs_ready")
        na_rs_ready = sem("na_rs_ready")
        y_ss_ready, y_rs_ready, x1_ready = sem("y_ss_ready"), sem("y_rs_ready"), sem("x1_ready")
        z_ss_ready, z_rs_ready, xn2_ready = sem("z_ss_ready"), sem("z_rs_ready"), sem("xn2_ready")
        r_sub_ready, r_exp_ready, aff_ready = sem("r_sub_ready"), sem("r_exp_ready"), sem("aff_ready")
        rank_ready, start_zero = sem("rank_ready"), sem("start_zero")
        silu_done, hid_ready = sem("silu_done"), sem("hid_ready")
        t_filled, t_drained = sem("t_filled"), sem("t_drained")
        m_filled, m_drained = sem("m_filled"), sem("m_drained")
        d_drained = sem("d_drained")
        pick_ready, gate_pick_ready = sem("pick_ready"), sem("gate_pick_ready")
        last_filled, acc_done, f_ss_ready, f_rs_ready, f_ready = (
            sem("last_filled"), sem("acc_done"), sem("f_ss_ready"), sem("f_rs_ready"), sem("f_ready"))

        def bank_of(name):
            return bank[bank_no[name]]

        def open_fill(pe, name):
            if bank_before[name] is not None:
                wait_drained(pe, bank_before[name])
            return bank_of(name)

        def fill_done(ins, name):
            ins.then_inc(filled[stream[name]], 1)

        def wait_fill(eng, name):
            eng.wait_ge(filled[stream[name]], turn_no[name])
            return bank_of(name)

        def drain_done(ins, name):
            ins.then_inc(drained[stream[name]], 1)

        def wait_drained(eng, name):
            eng.wait_ge(drained[stream[name]], turn_no[name])

        def link(eng, chain, ins):
            chain[1] += 1
            ins.then_inc(chain[0], 1)
            eng.wait_ge(chain[0], chain[1])

        def mine(names, who):
            return [n for n in names if stream[n] == who]

        def bc_dst(b):
            return (gain1, gain4)[b // 2][:, (b % 2) * 512:(b % 2 + 1) * 512]

        def pieces(name):
            kind, b = name[0], name[1]
            src = bank_of(name)
            if kind == "kc":
                return [(kcT[:, 2 * b:2 * b + 2].rearrange("p a n -> p (a n)"), src[:])]
            if kind == "q":
                return [(qTp[0:64, 2 * b], src[0:64]), (qTp[64:P, 2 * b + 1], src[64:P])]
            if kind == "f":
                return [(f_sb[:, b].rearrange("p (e c r) -> p c e r", e=2, r=ROWS),
                         src[:].rearrange("p (c e r) -> p c e r", e=2, r=ROWS))]
            dst = {"k": kT, "vc": vc_sb, "v": v_sb, "bg": bg_sb, "dft1": dft_g}.get(kind)
            if dst is not None:
                return [(dst[:, b], src[:])]
            if kind == "cg":
                return [(z_sb[:, b, 8:520], src[:])]
            if kind in ("bc", "last_bc"):
                return [(bc_dst(b), src[:])]

        KEYS = [("k", b) for b in range(4)]
        QKV = [("kc", b) for b in range(2)] + [("q", b) for b in range(4)] + [("v", b) for b in range(4)] \
            + [("vc", b) for b in range(CT)]
        GATES = [("bg", b) for b in range(2)] + [("cg", b) for b in range(2)]

        def wait_slot(eng, key):
            n = PRE.index(key)
            eng.wait_ge(loaded[n % RING], 16 * (n // RING + 1))
            return ring[n % RING]

        x_v = x[0].rearrange("(r c) d -> c r d", c=GRID_W)
        out_v = out[0].rearrange("(r c) d -> c r d", c=GRID_W)
        pre_src = {}
        for k in range(KT):
            for g in range(3):
                pre_src["mod", g, k] = w_mod[0, k * P:(k + 1) * P, g * SLOT:(g + 1) * SLOT]
        for g in range(5):
            for h in range(2):
                pre_src["in", g, h] = w_in[0, h * 512:(h + 1) * 512, IN_COLS[g]:IN_COLS[g] + 512].rearrange(
                    "(k p) n -> p k n", p=P)
        pre_src["dft", 0, 0] = dft
        for k in range(4):
            pre_src["out", 0, k] = w_out[0, k * 256:(k + 1) * 256, :].rearrange("(k p) n -> p k n", p=P)
        shifted_dram = nc.dram_tensor("shifted_dram", (ROWS, SHIFTED), F32, kind="Internal").ap()

        def slot_of(i):
            m = i % BIG_RING
            return (NPRE + m) % RING if m < RING else m

        def loads_until(pair, i):
            before = sum(n % RING == slot_of(i) for n in range(NPRE))
            return pair * (16 * (2 * STAGE // BIG_RING)) + 16 * (before + i // BIG_RING + 1)

        def load_window_biases(eng, which, loaded_):
            for c in range(WIN_C):
                rows_of_heads = bass.AP(shifted_dram.tensor, shifted_dram.offset + 64 + (7 - c) * ROWS,
                                        [shifted_dram.ap[0], [HEAD_W, HEADS], [1, 256]])
                eng.dma_start(bias[which][8 * c:8 * c + 8], rows_of_heads).then_inc(loaded_, 16)

        block = stack.enter_context(nc.Block())

        @block.sync
        def _(sp):
            for t in range(NT):
                sp.dma_start(x_rows[:, t], x_v[16 * t:16 * (t + 1)]).then_inc(x_loaded[t], 16)
            for n, key in enumerate(PRE):
                if key == ("in", IN_Q, 0):
                    sp.dma_start(ctx_rows[:], ctx[0].rearrange("(t p) d -> p t d", p=P)).then_inc(ctx_loaded, 16)
                if key == ("in", IN_BC, 0):
                    sp.wait_ge(shifted_stored, 16)
                    for i in range(2):
                        load_window_biases(sp, i, raw_loaded[i])
                if n >= RING:
                    sp.wait_ge(slots_used, n - RING + 1)
                dst = ring[n % RING]
                if key[0] == "in":
                    dst = dst.rearrange("p (k n) -> p k n", k=4)
                if key[0] == "out":
                    dst = dst.rearrange("p (k n) -> p k n", k=2)
                sp.dma_start(dst, pre_src[key]).then_inc(loaded[n % RING], 16)
            with sp.Fori(0, E // 2) as pair:
                for i in range(2 * STAGE):
                    e, i_ = pair * 2 + i // STAGE, i % STAGE
                    sp.wait_ge(slots_used, pair * (2 * STAGE) + (USED0 + i - BIG_RING + 1))
                    s = slot_of(i)
                    if i_ < GU_SLOTS:
                        c, kk, w = i_ // 8, (i_ % 8) // 2, (w_gate, w_up)[i_ % 2]
                        n = 2 * HALVES[c]
                        src = w[0, bass.ds(e, 1), kk * 256:(kk + 1) * 256, CHUNK0[c]:CHUNK0[c] + n].rearrange(
                            "a (k p) n -> p (a k) n", p=P)
                        dst = ring[s][:, 0:2 * n].rearrange("p (k n) -> p k n", k=2)
                    else:
                        c, j = HB[i_ - GU_SLOTS]
                        src = w_down[0, bass.ds(e, 1), CHUNK0[c]:CHUNK0[c] + 2 * HALVES[c], :].rearrange(
                            "a (h f) n -> f (a h) n", h=2)[j * P:(j + 1) * P]
                        dst = ring[s].rearrange("p (h n) -> p h n", h=2)
                    sp.dma_start(dst, src).then_inc(loaded[s], 16)

        @block.gpsimd
        def _(pool):
            chain = [pool_chain, 0]

            def inverse_root(rs, ms):
                return pool.tensor_tensor(rs, ms, minus_half[:, 0:1].to_broadcast([P, ms.shape[1]]), ALU.pow)

            def inverse_rms(rs, ms, ss, width):
                link(pool, chain, pool.tensor_scalar(ms, ss, 1.0 / width, EPS, ALU.mult, ALU.add))
                return inverse_root(rs, ms)

            pool.memset(shifted, 0.0).then_inc(pool_set, 1)
            link(pool, chain, pool.memset(minus_half[:], -0.5))
            for t in range(NT + CT):
                pool.wait_ge(x_ss_ready, t + 1)
                inverse_rms(x_rs[:, t:t + 1], x_ms[:, t:t + 1], x_ss[:, t:t + 1], D).then_inc(x_rs_ready, 1)
                if t == NT - 1:
                    pool.memset(qTp[:], 0.0).then_inc(pool_set, 1)
                    pool.memset(ones[:], 1.0).then_inc(pool_set, 1)
                    pool.memset(place[:], 0.0).then_inc(pool_set, 1)

            def times8(v):
                link(pool, chain, pool.tensor_scalar(v, v, 8.0, 1.0, ALU.mult, ALU.mult))

            def moved(b, dst, src):
                link(pool, chain, pool.tensor_copy(b[:, :, dst:dst + 64], b[:, :, src:src + 64]))
                link(pool, chain, pool.memset(b[:, :, src:src + 64], 8 * MASKED))

            def from_c(b, k0, k1, col0):
                v = b[:, :, col0:col0 + 8 * (k1 - k0)].rearrange("p h (k i) -> p h k i", i=8)
                return pool.affine_select(
                    out=v, in_=v, pattern=[[0, HEADS], [8, k1 - k0], [0, 8]], compare_op=ALU.is_ge,
                    fill=8 * MASKED, base=8 * k0 + 7, channel_multiplier=-1)

            def to_c(b, k0, k1, col0):
                v = b[:, :, col0:col0 + 8 * (k1 - k0)].rearrange("p h (k i) -> p h k i", i=8)
                return pool.affine_select(
                    out=v, in_=v, pattern=[[0, HEADS], [-8, k1 - k0], [0, 8]], compare_op=ALU.is_ge,
                    fill=8 * MASKED, base=8 * (WIN_C - 1) - 8 * k0, channel_multiplier=1)

            inner, edge = bias
            pool.wait_ge(raw_loaded[0], 16 * WIN_C)
            times8(inner)
            link(pool, chain, from_c(inner, 0, 32, 0))
            to_c(inner, 0, 32, 0).then_inc(bias_ready, 1)
            pool.wait_ge(raw_loaded[1], 16 * WIN_C)
            times8(edge)
            moved(edge, 0, 64)
            link(pool, chain, from_c(edge, 8, 16, 0))
            link(pool, chain, from_c(edge, 16, 32, 128))
            to_c(edge, 24, 32, 192).then_inc(bias_ready, 1)

            for i in range(N + TAIL):
                if i < N:
                    pool.wait_ge(inv_ready, i + 1)
                    pool.tensor_scalar(prob[i % 4], prob[i % 4], inv[:, i:i + 1], 1.0, ALU.mult, ALU.mult)\
                        .then_inc(prob_ready, 1)
                if i in (1, 4):
                    g = i // 4
                    wait_drained(pool, ("sq", g))
                    inverse_root(cf_rs[:, g], cf_ms[:, g]).then_inc(cf_rs_ready, 1)
                if i == 2 * HEADS + 1:
                    pool.wait_ge(raw_loaded[2], 16 * WIN_C)
                    times8(inner[:, 0:4])
                if i == 2 * HEADS + 2:
                    times8(inner[:, 4:8])
                if i == 2 * HEADS + 3:
                    moved(inner, 192, 128)
                if i == 2 * HEADS + 4:
                    link(pool, chain, from_c(inner, 0, 8, 0))
                    link(pool, chain, to_c(inner, 0, 16, 0))
                if i == 2 * HEADS + 5:
                    to_c(inner, 16, 24, 192).then_inc(bias_ready, 1)
                j = tile_at(i, 1)
                if j is not None:
                    wait_drained(pool, ("ss", j))
                    inverse_root(na_rs[:, j:j + 1], na_ms[:, j:j + 1]).then_inc(na_rs_ready, 1)
                for offset, ready, (rs, ms, ss), told in ((2, y_ss_ready, (y_rs, y_ms, y_ss), y_rs_ready),
                                                          (4, z_ss_ready, (z_rs, z_ms, z_ss), z_rs_ready)):
                    j = tile_at(i, offset)
                    if j is not None:
                        pool.wait_ge(ready, j + 1)
                        inverse_rms(rs[:, j:j + 1], ms[:, j:j + 1], ss[:, j:j + 1], D).then_inc(told, 1)

            wait_fill(pool, ("na", NT - 1, 1))
            pool.memset(acc[:], 0.0).then_inc(start_zero, 1)
            pool.memset(out_e, 0.0).then_inc(start_zero, 1)
            pool.memset(gateT[1], 0.0).then_inc(start_zero, 1)

            for t in range(NT):
                pool.wait_ge(f_ss_ready, t + 1)
                inverse_rms(y_rs[:, t:t + 1], y_ms[:, t:t + 1], y_ss[:, t:t + 1], D).then_inc(f_rs_ready, 1)

        @block.scalar
        def _(act):
            chain = [act_chain, 0]

            def copy_out(names):
                for name in mine(names, "act"):
                    wait_fill(act, name)
                    for dst, src in pieces(name):
                        ins = nc.scalar.activation(dst, src, ACT.Copy)
                    drain_done(ins, name)

            last_squares = []

            def squares(rows, ss, told, number_, late=1):
                if last_squares:
                    act.wait_ge(*last_squares)
                nc.scalar.activation(squares_out[late], rows, ACT.Square, accum_out=ss).then_inc(told, 1)
                last_squares[:] = [told, number_]

            act.dma_start(c_sb[:], cT).then_inc(c_loaded, 16)
            act.dma_start(cst[:], consts[:, 0:256]).then_inc(ident_loaded, 16)
            act.wait_ge(c_loaded, 16)
            act.wait_ge(dve_set, 1)
            nc.scalar.activation(s_pad[:, :, 0:2], c_sb[:], ACT.Silu).then_inc(silu_ready, 1)
            act.dma_start(cols[:], colv).then_inc(consts_loaded, 16)
            act.dma_start(w_rt[:], w_router).then_inc(consts_loaded, 16)
            act.dma_start(dd[:], consts[:, 256:512]).then_inc(consts_loaded, 16)
            act.wait_ge(dve_set, 2)
            for g in range(3):
                act.dma_start(b_row[0:P:32, g, :], b_mod[0, g * SLOT:(g + 1) * SLOT].rearrange("(a n) -> a n", a=4))\
                    .then_inc(rows_loaded, 16)
            act.dma_start(b_row[1:P:32, 0, :], b_mod[0, 0:SLOT].rearrange("(a n) -> a n", a=4)).then_inc(rows_loaded, 16)
            for rows, g, vec in ((slice(0, 64, 32), 0, g_post_mix), (slice(0, 64, 32), 1, g_pre_ffn),
                                 (slice(64, P, 32), 1, g_post_ffn)):
                act.dma_start(g_row[rows, g, :], vec[0].rearrange("(a n) -> a n", a=2)).then_inc(rows_loaded, 16)
            act.wait_ge(pool_set, 1)
            for r in range(ROWS):
                act.dma_start(shifted[r:r + 1, 64:64 + HEADS * HEAD_W].rearrange("p (m i) -> p m i", i=8),
                              rpbT[:, :, 7 - r:15 - r].rearrange("(a h) m i -> a (h m) i", a=1))\
                    .then_inc(shifted_loaded, 16)
            for t in range(NT):
                act.wait_ge(x_loaded[t], 16)
                squares(x_rows[:, t], x_ss[:, t:t + 1], x_ss_ready, t + 1, 0)
            act.wait_ge(shifted_loaded, 16 * ROWS)
            act.dma_start(shifted_dram, shifted).then_inc(shifted_stored, 16)

            wait_drained(act, ("modT", 0))
            for kt in range(0, KT, 2):
                b = wait_fill(act, ("xT", kt))
                drain_done(nc.scalar.activation(hT[:, kt], b[:], ACT.Identity, scale=mod_scale[:, 0, kt:kt + 1],
                                                bias=mod_shift[:, 0, kt:kt + 1]), ("xT", kt))
            act.wait_ge(ctx_loaded, 16)
            for t in range(CT):
                squares(ctx_rows[:, t], x_ss[:, NT + t:NT + t + 1], x_ss_ready, NT + t + 1, 0)
            copy_out(KEYS)
            for f in (0, 2):
                b = wait_fill(act, ("cT", f))
                for j in range(2):
                    kt = 2 * f + j
                    ins = nc.scalar.activation(hcT[:, kt], b[:, j * CTX:(j + 1) * CTX], ACT.Identity,
                                               scale=mod_scale[:, 1, kt:kt + 1], bias=mod_shift[:, 1, kt:kt + 1])
                drain_done(ins, ("cT", f))
            act.wait_ge(pool_set, 2)
            copy_out(QKV)
            wait_fill(act, ("vc", CT - 1))
            for t in range(NT):
                act.dma_start(x1[:, t], x_v[16 * t:16 * (t + 1)]).then_inc(x_again, 16)
            copy_out(GATES)
            copy_out([("f", b) for b in range(2)])
            copy_out([("dft1", b) for b in range(4)])
            copy_out([("bc", b) for b in range(2)])
            for b in range(2):
                src = wait_fill(act, ("dft2", b))
                nc.scalar.activation(dft_o[:, b], src[:, 256:512], ACT.Copy).then_inc(odd_copied, 1)

            act.wait_ge(rows_ready, 2)
            for i in range(N + TAIL):
                if i < N:
                    s = bank_of(("S", i))
                    act.wait_ge(scores_ready, i + 1)
                    nc.scalar.activation(prob[i % 4][:, 0:256], prob[i % 4][:, 0:256], ACT.Exp, scale=-1.0,
                                         bias=neg_max[:, i:i + 1], accum_out=sums[:, i, 0:1])
                    drain_done(nc.scalar.activation(prob[i % 4][:, 256:512], s[:, 256:512], ACT.Exp, scale=SCALE,
                                                    bias=neg_max[:, i:i + 1], accum_out=sums[:, i, 1:2]), ("S", i))
                if i in (0, 3):
                    g = i // 3
                    if g == 0:
                        act.wait_ge(conv_ready, 2)
                    else:
                        wait_drained(act, ("dft2", 1))
                        wait_fill(act, ("sq", 0))
                    for j in range(2):
                        nc.scalar.activation(cf_sq[j], ycf[:, 2 * g + j], ACT.Square).then_inc(cf_sq_ready, 1)
                if i == 2 * HEADS - 1:
                    load_window_biases(act, 0, raw_loaded[2])
                for name in extra_fills(i - 1):
                    kind, j = name[0], name[1]
                    if kind == "cf":
                        if name[2] == 0 and j >= 1:
                            act.wait_ge(x1_ready, j)
                        src = wait_fill(act, name)
                        drain_done(nc.scalar.activation(y_tmp[:, name[2] * 512:(name[2] + 1) * 512], src[:], ACT.Copy), name)
                    if kind == "h2Ta":
                        src = wait_fill(act, name)
                        for k in range(4):
                            ins = nc.scalar.activation(h2T[:, k], src[:, k * P:(k + 1) * P], ACT.Identity,
                                                       scale=ffn_gain[:, k:k + 1], bias=ffn_shift[:, k:k + 1])
                        drain_done(ins, name)
                    if kind == "rt":
                        src = wait_fill(act, name)
                        drain_done(nc.scalar.activation(logit[:, Q_TILES[j]], src[:, 0:E], ACT.Copy), name)
                    if kind == "last_bc":
                        (dst, src), = pieces(name)
                        wait_fill(act, name)
                        drain_done(nc.scalar.activation(dst, src, ACT.Copy), name)
                j = tile_at(i, 3)
                if j is not None:
                    wait_drained(act, ("na", j, 1))
                    squares(y_tmp, y_ss[:, j:j + 1], y_ss_ready, j + 1)
                j = tile_at(i, 5)
                if j is not None:
                    act.wait_ge(x1_ready, j + 1)
                    squares(x1[:, Q_TILES[j]], z_ss[:, j:j + 1], z_ss_ready, j + 1)
                if STEPS + 3 <= i <= N + STEPS + 1 and i % 2 == 0:
                    po = i - STEPS - 2
                    t, h = UNITS[po]
                    j = po // HEADS
                    src = wait_fill(act, ("PO", po))
                    if h == 1 and j >= 1:
                        wait_fill(act, ("ss", j - 1))
                    if h == 1 and j >= 2:
                        wait_fill(act, ("na", j - 2, 1))
                    nc.scalar.activation(yna[j % 2][:, h // 2], src[:, 0:P], ACT.Identity, scale=g_mix_col[:, h // 2:h // 2 + 1])
                    drain_done(nc.scalar.activation(na_sq[:, (h // 2) * P:(h // 2 + 1) * P], src[:, 0:P], ACT.Square),
                               ("PO", po))

            def expert_tokens(dst, src):
                for k in range(KT):
                    ins = nc.scalar.activation(dst[:, k], src[:, k * CAP:(k + 1) * CAP], ACT.Identity,
                                               scale=ffn_gain[:, k:k + 1], bias=ffn_shift[:, k:k + 1])
                return ins

            act.wait_ge(r_sub_ready, 1)
            nc.scalar.activation(aff[:], logit[:], ACT.Exp).then_inc(r_exp_ready, 1)
            src = wait_fill(act, ("xs", 0))
            drain_done(expert_tokens(xsT[0], src), ("xs", 0))

            with act.Fori(0, E // 2) as pair:
                for s in range(2):
                    e = pair * 2 + s

                    def silu(c):
                        q = (3 * s + c) % 2
                        act.wait_ge(slots_used, pair * (2 * STAGE) + (USED0 + s * STAGE + 8 * (c + 1)))
                        nc.scalar.activation(silu_g[q][:, 0:HALVES[c]], bank[q][:, 0:HALVES[c]], ACT.Silu)\
                            .then_inc(silu_done, 1)

                    def wait_turn(fill):
                        act.wait_ge(t_filled, e * 5 + (fill + 1))

                    def from_t(dst, width, fill):
                        wait_turn(fill)
                        nc.scalar.activation(dst, bank[4][:, 0:width], ACT.Copy).then_inc(t_drained, 1)

                    silu(0)
                    from_t(hidT[:, 0:4].rearrange("p j n -> p (j n)"), 512, 0)
                    from_t(gateT[s], 512, 1)
                    silu(1)
                    from_t(hidT[:, 4:8].rearrange("p j n -> p (j n)"), 512, 2)
                    wait_turn(3)
                    expert_tokens(xsT[1 - s], bank[4]).then_inc(t_drained, 1)
                    silu(2)
                    from_t(hidT[:, 8:11].rearrange("p j n -> p (j n)"), 384, 4)
                    act.wait_ge(slots_used, pair * (2 * STAGE) + (USED0 + (s + 1) * STAGE))
                    for b in range(2):
                        ins = nc.scalar.activation(out_e[:, b * 512:(b + 1) * 512], bank[6 + b][:], ACT.Copy)
                    ins.then_inc(d_drained, 1)

            for t in range(NT):
                act.wait_ge(acc_done, t + 1)
                squares(acc[:, t], y_ss[:, t:t + 1], f_ss_ready, t + 1)
            for t in range(NT):
                act.wait_ge(f_ready, t + 1)
                act.dma_start(out_v[16 * t:16 * (t + 1)], fin[t]).then_inc(stored, 16)
            act.wait_ge(stored, 16 * NT)

        @block.vector
        def _(dve):
            chain = [dve_chain, 0]

            def copy_out(names):
                for name in mine(names, "dve"):
                    wait_fill(dve, name)
                    for dst, src in pieces(name):
                        ins = nc.vector.tensor_copy(dst, src)
                    drain_done(ins, name)

            nc.vector.memset(s_pad[:], 0.0).then_inc(dve_set, 1)
            nc.vector.memset(b_row[:], 0.0)
            nc.vector.memset(g_row[:], 1.0).then_inc(dve_set, 1)
            link(dve, chain, nc.vector.memset(one_col[:], 0.0))
            nc.vector.memset(one_col[0:64], 1.0)
            for s, n in ((hid_ready, 3), (t_drained, 5), (m_drained, 8), (d_drained, 1)):
                dve.nop().then_inc(s, n)

            def normalise_rows(t):
                rows = x_rows[:, t] if t < NT else ctx_rows[:, t - NT]
                dve.wait_ge(x_rs_ready, t + 1)
                nc.vector.tensor_scalar(rows, rows, x_rs[:, t:t + 1], None, ALU.mult).then_inc(xn_ready, 1)

            for t in range(NT):
                normalise_rows(t)
            dve.wait_ge(rows_loaded, 16 * 7)
            src = wait_fill(dve, ("mod", 0))
            drain_done(nc.vector.tensor_tensor(mod_row[:, 0], src[:], b_row[:, 0], ALU.add), ("mod", 0))
            src = wait_fill(dve, ("modT", 0))
            dve.wait_ge(consts_loaded, 16 * 3)
            v = src[:].rearrange("p (b g r) -> p g b r", b=4, g=4)
            for who in range(2):
                nc.vector.tensor_copy(mod_shift[:, who].rearrange("p (g b) -> p g b", g=2), v[:, 0:2, :, who])
                ins = nc.vector.scalar_tensor_tensor(
                    out=mod_scale[:, who].rearrange("p (g b) -> p g b", g=2), in0=v[:, 2:4, :, who], scalar=1.0,
                    in1=g_pre_col.rearrange("p (g b) -> p g b", g=2), op0=ALU.add, op1=ALU.mult)
            drain_done(ins, ("modT", 0))
            wait_drained(dve, ("modT", 0))
            for kt in range(1, KT, 2):
                b = wait_fill(dve, ("xT", kt))
                drain_done(nc.vector.tensor_scalar(hT[:, kt], b[:], mod_scale[:, 0, kt:kt + 1],
                                                   mod_shift[:, 0, kt:kt + 1], ALU.mult, ALU.add), ("xT", kt))
            for t in range(CT):
                normalise_rows(NT + t)
            copy_out(KEYS)
            for f in (1, 3):
                b = wait_fill(dve, ("cT", f))
                for j in range(2):
                    kt = 2 * f + j
                    ins = nc.vector.tensor_scalar(hcT[:, kt], b[:, j * CTX:(j + 1) * CTX], mod_scale[:, 1, kt:kt + 1],
                                                  mod_shift[:, 1, kt:kt + 1], ALU.mult, ALU.add)
                drain_done(ins, ("cT", f))
            dve.wait_ge(pool_set, 2)
            copy_out(QKV)

            def gain_rows(g):
                src = wait_fill(dve, ("mod", g))
                drain_done(nc.vector.tensor_tensor(mod_row[:, g], src[:], b_row[:, g], ALU.add), ("mod", g))
                wait_drained(dve, ("mod", g))
                nc.vector.scalar_tensor_tensor(
                    out=mod_row[:, g], in0=mod_row[:, g], scalar=0.0 if g == 1 else one_col[:, 0:1],
                    in1=g_row[:, g - 1], op0=ALU.add, op1=ALU.mult).then_inc(rows_ready, 1)

            gain_rows(1)
            copy_out(GATES)
            for b in range(2):
                src = wait_fill(dve, ("u", b))
                wait_drained(dve, ("cg", b))
                z = z_sb[:, b, 8:520]
                drain_done(nc.vector.tensor_tensor(z, z, src[:], ALU.mult), ("u", b))
            wait_drained(dve, ("u", 1))
            nc.vector.memset(z_sb[:, :, 0:1], 0.0)
            nc.vector.tensor_copy(z_sb[:, :, 1:8], z_sb[:, :, 512:519])
            nc.vector.tensor_copy(z_sb[:, :, 520:527], z_sb[:, :, 9:16])
            link(dve, chain, nc.vector.memset(z_sb[:, :, 527:528], 0.0))
            wait_fill(dve, ("f", 1))
            wait_drained(dve, ("bg", 0))
            wait_drained(dve, ("bg", 1))
            for b in range(2):
                y = ycf[:, b]
                link(dve, chain, nc.vector.tensor_scalar(y, z_sb[:, b, 0:512], conv_w[:, b, 0:1], None, ALU.mult))
                for j in (1, 2):
                    link(dve, chain, nc.vector.scalar_tensor_tensor(
                        out=y, in0=z_sb[:, b, 8 * j:8 * j + 512], scalar=conv_w[:, b, j:j + 1], in1=y,
                        op0=ALU.mult, op1=ALU.add))
                nc.vector.tensor_tensor(y, y, bg_sb[:, b], ALU.mult).then_inc(conv_ready, 1)
            gain_rows(2)
            copy_out([("dft1", b) for b in range(4)])
            for g, dst, pos in ((1, ffn_shift, 2), (2, ffn_gain, 0)):
                v = wait_fill(dve, ("modT", g))[:].rearrange("p (b g r) -> p g b r", b=4, g=4)
                drain_done(nc.vector.tensor_copy(dst[:].rearrange("p (g b) -> p g b", g=2), v[:, pos:pos + 2, :, 0]),
                           ("modT", g))
            copy_out([("bc", b) for b in range(2)])
            for b in range(2):
                src = bank_of(("dft2", b))
                dve.wait_ge(odd_copied, b + 1)
                y = ycf[:, 2 + b].rearrange("p (c r) -> p c r", r=8)
                even = src[:, 0:256].rearrange("p (c r) -> p c r", r=4)
                odd = dft_o[:, b].rearrange("p (c r) -> p c r", r=4)
                nc.vector.tensor_tensor(y[:, :, 0:4], even, odd, ALU.add)
                drain_done(nc.vector.tensor_tensor(y[:, :, 4:8], even, odd, ALU.subtract), ("dft2", b))
            wait_drained(dve, ("dft2", 1))
            dve.wait_ge(rows_ready, 2)

            for i in range(N + TAIL):
                if i < N:
                    t, h = UNITS[i]
                    if i in (0, 2 * HEADS, 3 * HEADS):
                        dve.wait_ge(bias_ready, 1 + i // HEADS - (1 if i else 0))
                    s = wait_fill(dve, ("S", i))
                    nc.vector.tensor_tensor_reduce(
                        out=prob[i % 4][:, 0:256], in0=s[:, 0:256], in1=bias[1 if t == 0 else 0][:, h], scale=-SCALE,
                        scalar=-3 * MASKED, op0=ALU.add, op1=ALU.min, accum_out=win_max[:, i:i + 1])
                    link(dve, chain, nc.vector.tensor_reduce(ctx_max[:, i:i + 1], s[:, 256:512], AX_X, ALU.max))
                    nc.vector.tensor_scalar(neg_max[:, i:i + 1], ctx_max[:, i:i + 1], -SCALE, win_max[:, i:i + 1],
                                            ALU.mult, ALU.min).then_inc(scores_ready, 1)
                if 1 <= i <= N:
                    j = i - 1
                    wait_drained(dve, ("S", j))
                    link(dve, chain, nc.vector.tensor_tensor(total[:, j:j + 1], sums[:, j, 0:1], sums[:, j, 1:2], ALU.add))
                    nc.vector.reciprocal(inv[:, j:j + 1], total[:, j:j + 1]).then_inc(inv_ready, 1)
                if STEPS <= i < N + STEPS:
                    j = i - STEPS
                    src = wait_fill(dve, ("PT", j))
                    drain_done(nc.vector.tensor_copy(probT[j % 4], src[:]), ("PT", j))
                for name in extra_fills(i - 1):
                    kind, j = name[0], name[1]
                    if kind == "sq":
                        src = wait_fill(dve, name)
                        drain_done(nc.vector.tensor_scalar(cf_ms[:, j], src[:, 0:NT], 1.0 / CONV_W, EPS, ALU.mult, ALU.add), name)
                    if kind == "rs":
                        src = wait_fill(dve, name)
                        for k in (2 * j, 2 * j + 1):
                            ins = nc.vector.scalar_tensor_tensor(
                                out=ycf[:, k], in0=ycf[:, k], scalar=g_mix_col[:, 4 + k:5 + k], in1=src[:],
                                op0=ALU.mult, op1=ALU.mult)
                        drain_done(ins, name)
                    if kind == "ss":
                        src = wait_fill(dve, name)
                        drain_done(nc.vector.tensor_scalar(na_ms[:, j:j + 1], src[:, 0:1], 1.0 / NA_W, EPS,
                                                           ALU.mult, ALU.add), name)
                    if kind == "h2Tb":
                        src = wait_fill(dve, name)
                        for k in range(4, KT):
                            ins = nc.vector.tensor_scalar(h2T[:, k], src[:, (k - 4) * P:(k - 3) * P], ffn_gain[:, k:k + 1],
                                                          ffn_shift[:, k:k + 1], ALU.mult, ALU.add)
                        drain_done(ins, name)
                j = tile_at(i, 3)
                if j is not None:
                    dve.wait_ge(na_rs_ready, j + 1)
                    for b in range(2):
                        half = slice(b * 512, (b + 1) * 512)
                        src = wait_fill(dve, ("na", j, b))
                        wait_drained(dve, ("cf", j, b))
                        drain_done(nc.vector.scalar_tensor_tensor(
                            out=y_tmp[:, half], in0=src[:], scalar=na_rs[:, j:j + 1], in1=y_tmp[:, half],
                            op0=ALU.mult, op1=ALU.add), ("na", j, b))
                j = tile_at(i, 4)
                if j is not None:
                    dve.wait_ge(y_rs_ready, j + 1)
                    link(dve, chain, nc.vector.scalar_tensor_tensor(
                        out=y_tmp, in0=y_tmp, scalar=y_rs[:, j:j + 1], in1=gain1, op0=ALU.mult, op1=ALU.mult))
                    dve.wait_ge(x_again, 16 * NT)
                    v = x1[:, Q_TILES[j]]
                    nc.vector.tensor_tensor(v, v, y_tmp, ALU.add).then_inc(x1_ready, 1)
                j = tile_at(i, 6)
                if j is not None:
                    dve.wait_ge(z_rs_ready, j + 1)
                    t = Q_TILES[j]
                    nc.vector.tensor_scalar(xn2[:, t], x1[:, t], z_rs[:, j:j + 1], None, ALU.mult).then_inc(xn2_ready, 1)

            for j in range(NT):
                wait_drained(dve, ("rt", j))
            link(dve, chain, nc.vector.tensor_reduce(r_max[:], logit[:], AX_X, ALU.max))
            nc.vector.tensor_tensor(logit[:], logit[:], r_max[:].rearrange("p (t a) -> p t a", a=1).to_broadcast([P, NT, E]),
                                    ALU.subtract).then_inc(r_sub_ready, 1)
            dve.wait_ge(r_exp_ready, 1)
            link(dve, chain, nc.vector.tensor_reduce(r_sum[:], aff[:], AX_X, ALU.add))
            link(dve, chain, nc.vector.reciprocal(r_inv[:], r_sum[:]))
            nc.vector.tensor_tensor(aff[:], aff[:], r_inv[:].rearrange("p (t a) -> p t a", a=1).to_broadcast([P, NT, E]),
                                    ALU.mult).then_inc(aff_ready, 1)
            nc.vector.memset(one_row, 1.0)
            src = wait_fill(dve, ("affT", 0))
            drain_done(nc.vector.tensor_copy(work, src[0:E]), ("affT", 0))
            wait_drained(dve, ("affT", 0))
            for _ in range(CAP // 8):
                link(dve, chain, nc.vector.max(top8[0:E], work))
                link(dve, chain, nc.vector.match_replace(work, top8[0:E], work, -1.0))
            link(dve, chain, nc.vector.tensor_scalar(chosen, work, 0.0, None, ALU.is_lt))
            link(dve, chain, nc.vector.tensor_tensor_scan(count, one_row, chosen, 0.0, ALU.mult, ALU.add))
            nc.vector.tensor_tensor(rank, count, chosen, ALU.mult).then_inc(rank_ready, 1)
            dve.wait_ge(pool_set, 4)
            src = wait_fill(dve, ("posT", 0))
            ins = nc.vector.tensor_copy(place[:, :, 0:E], src[:, 0:NT * E].rearrange("p (t e) -> p t e", t=NT))
            drain_done(ins, ("posT", 0))
            wait_drained(dve, ("posT", 0))

            def slots_of(dst, e, width):
                nos = iota[:, 0:width].rearrange("p (a s) -> p a s", a=1).to_broadcast([P, NT, width])
                return nc.vector.tensor_tensor(dst, nos, place[:, :, bass.ds(e, 1)].to_broadcast([P, NT, width]),
                                               ALU.is_equal)

            slots_of(pick, 0, CAP).then_inc(pick_ready, 1)
            dve.wait_ge(start_zero, 1)

            with dve.Fori(0, E // 2) as pair:
                for s in range(2):
                    e = pair * 2 + s
                    for i in range(8):
                        t, b = i // 2, i % 2
                        v = acc[:, t, b * 512:(b + 1) * 512]
                        dve.wait_ge(m_filled, e * 8 + (i + 1))
                        nc.vector.tensor_tensor(v, v, bank[5][:], ALU.add).then_inc(m_drained, 1)
                    dve.wait_ge(t_drained, e * 5 + 2)
                    slots_of(gate_pick, e, 2 * CAP).then_inc(gate_pick_ready, 1)
                    dve.wait_ge(gate_pick_ready, e * 2 + 1)
                    nc.vector.tensor_tensor(gate_pick, gate_pick, aff[:, :, bass.ds(e, 1)].to_broadcast([P, NT, 2 * CAP]),
                                            ALU.mult).then_inc(gate_pick_ready, 1)
                    dve.wait_ge(t_drained, e * 5 + 4)
                    slots_of(pick, e + 1, CAP).then_inc(pick_ready, 1)
                    for c in range(3):
                        q = (3 * s + c) % 2
                        w = HALVES[c]
                        dve.wait_ge(silu_done, e * 3 + (c + 1))
                        nc.vector.tensor_tensor(hid[q][:, 0:w], silu_g[q][:, 0:w], bank[2 + q][:, 0:w], ALU.mult)\
                            .then_inc(hid_ready, 1)

            def scale_last(t):
                dve.wait_ge(f_rs_ready, t + 1)
                link(dve, chain, nc.vector.scalar_tensor_tensor(
                    out=fin[t], in0=acc[:, t], scalar=y_rs[:, t:t + 1], in1=gain4, op0=ALU.mult, op1=ALU.mult))
                nc.vector.tensor_tensor(fin[t], fin[t], x1[:, t], ALU.add).then_inc(f_ready, 1)

            for t in range(NT):
                for b in range(2):
                    v = acc[:, t, b * 512:(b + 1) * 512]
                    dve.wait_ge(last_filled, 2 * t + b + 1)
                    ins = nc.vector.tensor_tensor(v, v, bank[2 * t + b][:], ALU.add)
                ins.then_inc(acc_done, 1)
                if t >= 1:
                    scale_last(t - 1)
            scale_last(NT - 1)

        @block.tensor
        def _(pe):
            mm = nc.tensor.matmul

            def turn(dst, src):
                return nc.tensor.transpose(dst, src, ident[0:src.shape[0], 0:src.shape[0]])

            def product(dst, terms):
                for j, (a, b) in enumerate(terms):
                    ins = mm(dst, a, b, start=j == 0, stop=j == len(terms) - 1)
                return ins

            owed = [False]

            def used(ins):
                ins.then_inc(slots_used, 1)

            def used_up_by(ins):
                if owed[0]:
                    used(ins)
                    owed[0] = False

            def transpose_x(kt):
                b = open_fill(pe, ("xT", kt))
                for t in range(NT):
                    ins = turn(b[:, t * P:(t + 1) * P], x_rows[:, t, kt * P:(kt + 1) * P])
                fill_done(ins, ("xT", kt))

            def mod_part(g, k):
                b = open_fill(pe, ("mod", g)) if k == 0 else bank_of(("mod", g))
                w = wait_slot(pe, ("mod", g, k))
                for j in range(4):
                    ins = mm(b[32 * j:32 * (j + 1)], s_pad[:, k], w[:, j * 512:(j + 1) * 512],
                             start=k == 0, stop=k == KT - 1)
                    if j == 0:
                        used_up_by(ins)
                if k < KT - 1:
                    used(ins)
                else:
                    fill_done(ins, ("mod", g))
                    owed[0] = True

            def product(name, dst, terms, last_of=None, part=(True, True)):
                for j, (a, b) in enumerate(terms):
                    ins = mm(dst, a, b, start=j == 0, stop=j == len(terms) - 1)
                    if part[0] and j == 0:
                        used_up_by(ins)
                    if last_of is not None and j == 3:
                        used(ins)
                if part[1]:
                    fill_done(ins, name)
                if last_of is not None:
                    owed[0] = True

            pe.wait_ge(ident_loaded, 16)
            pe.wait_ge(xn_ready, NT)
            for kt in range(6):
                transpose_x(kt)
            pe.wait_ge(silu_ready, 1)
            for k in range(KT):
                mod_part(0, k)
            wait_drained(pe, ("mod", 0))
            b = open_fill(pe, ("modT", 0))
            for j in range(4):
                ins = turn(b[:, j * P:(j + 1) * P], mod_row[:, 0, j * P:(j + 1) * P])
                if j == 0:
                    used_up_by(ins)
            fill_done(ins, ("modT", 0))
            for kt in (6, 7):
                transpose_x(kt)

            def w_cols(g, k, c0, n):
                w = wait_slot(pe, ("in", g, k // 4))
                return w.rearrange("p (k n) -> p k n", k=4)[:, k % 4, c0:c0 + n]

            def columns(name, g, blk, last=False):
                b = open_fill(pe, name)
                product(name, b[:], [(w_cols(g, k, blk * P, P), hT[:, k]) for k in range(KT)], g if last else None)

            wait_drained(pe, ("xT", 6))
            wait_drained(pe, ("xT", 7))
            for blk in range(4):
                columns(("k", blk), IN_K, blk)
            pe.wait_ge(xn_ready, NT + CT)
            for f in range(4):
                b = open_fill(pe, ("cT", f))
                for j in range(4):
                    kt, t = 2 * f + j // 2, j % 2
                    ins = turn(b[:, j * P:(j + 1) * P], ctx_rows[:, t, kt * P:(kt + 1) * P])
                fill_done(ins, ("cT", f))
            wait_drained(pe, ("cT", 2))
            wait_drained(pe, ("cT", 3))
            for f in range(2):
                b = open_fill(pe, ("kc", f))
                for j in range(2):
                    product(("kc", f), b[:, j * CTX:(j + 1) * CTX],
                            [(w_cols(IN_K, k, (2 * f + j) * P, P), hcT[:, k]) for k in range(KT)],
                            IN_K if (f, j) == (1, 1) else None, part=(j == 0, j == 1))
            for blk in range(4):
                mod_part(1, blk)
                columns(("q", blk), IN_Q, blk, blk == 3)
            for t in range(3):
                mod_part(1, 4 + t)
                b = open_fill(pe, ("v", t))
                product(("v", t), b[:], [(hT[:, k, 64 + t * P:64 + (t + 1) * P], w_cols(IN_V, k, 0, NA_W))
                                         for k in range(KT)])
            mod_part(1, 7)
            b = open_fill(pe, ("v", 3))
            for k in range(KT):
                ins = mm(b[0:64], hT[:, k, 0:64], w_cols(IN_V, k, 0, NA_W), start=k == 0, stop=k == KT - 1)
                if k == 0:
                    used_up_by(ins)
                ins = mm(b[64:P], hT[:, k, SEQ - 64:SEQ], w_cols(IN_V, k, 0, NA_W), start=k == 0, stop=k == KT - 1)
            fill_done(ins, ("v", 3))
            for t in range(CT):
                b = open_fill(pe, ("vc", t))
                product(("vc", t), b[:], [(hcT[:, k, t * P:(t + 1) * P], w_cols(IN_V, k, 0, NA_W)) for k in range(KT)],
                        IN_V if t == CT - 1 else None)
            for name, g, last in (("bg", IN_BC, 0), ("cg", IN_BC, 1), ("u", IN_UF, 0), ("f", IN_UF, 1)):
                for blk in range(2):
                    mod_part(2, (g - IN_BC) * 4 + 2 * last + blk)
                    columns((name, blk), g, 2 * last + blk, bool(last and blk))
            for b in range(2):
                wait_drained(pe, ("f", b))
            pe.wait_ge(consts_loaded, 16 * 3)
            for blk in range(4):
                b = open_fill(pe, ("dft1", blk))
                for ch in range(2):
                    product(("dft1", blk), b[:, ch * 256:(ch + 1) * 256], [(f_sb[:, ch, blk * P:(blk + 1) * P], dd[:])],
                            part=(ch == 0, ch == 1))
            for g in (1, 2):
                pe.wait_ge(rows_ready, g)
                b = open_fill(pe, ("modT", g))
                for j in range(4):
                    ins = turn(b[:, j * P:(j + 1) * P], mod_row[:, g, j * P:(j + 1) * P])
                fill_done(ins, ("modT", g))

            def one_row_of(p0):
                return ident[:, p0:p0 + 1].to_broadcast([P, P])

            def on_every_partition(name, free=0):
                b = open_fill(pe, name)
                for m in range(4):
                    ins = mm(b[:, m * P:(m + 1) * P], one_row_of(32 * (name[1] % 4)),
                             mod_row[:, 1 + name[1] // 2, m * P:(m + 1) * P], start=True, stop=True)
                    if m < free:
                        used(ins)
                fill_done(ins, name)

            for b in range(2):
                on_every_partition(("bc", b))
            tables = wait_slot(pe, ("dft", 0, 0)).rearrange("p (e h s n) -> p e h s n", e=2, h=2, s=2)
            for blk in range(4):
                wait_drained(pe, ("dft1", blk))
            for ch in range(2):
                b = open_fill(pe, ("dft2", ch))
                for par in range(2):
                    product(("dft2", ch), b[:, par * 256:(par + 1) * 256],
                            [(dft_g[:, 2 * par + half, ch * 256 + cs * P:ch * 256 + (cs + 1) * P],
                              tables[:, par, half, cs]) for half in range(2) for cs in range(2)],
                            part=(par == 0, par == 1))
            owed[0] = True

            def scores(i):
                t, h = UNITS[i]
                b = open_fill(pe, ("S", i))
                q, keys = qTp[:, h, t * P:(t + 1) * P], kT[:, h // 2]
                at_ends = keys.rearrange("p (a b) -> p a b", b=64)[:, 0:8:7, :]
                for j, kt in enumerate(KEY_TILES[t]):
                    kv = at_ends if kt == 3 else keys[:, 64 + kt * P:64 + (kt + 1) * P]
                    dst = b[:, j * P:(j + 1) * P]
                    if kt == 3:
                        dst = dst.rearrange("p (a b) -> p a b", b=64)
                    ins = mm(dst, q, kv, start=True, stop=True)
                    if j == 0:
                        used_up_by(ins)
                fill_done(mm(b[:, 256:512], q, kcT[:, h // 2], start=True, stop=True), ("S", i))

            def extra(name):
                kind, j = name[0], name[1]
                last = kind in ("cf", "na") and j == NT - 1
                if kind == "last_bc":
                    on_every_partition(name, 2)
                    owed[0] = False
                    return
                b = open_fill(pe, name)
                if kind == "sq":
                    pe.wait_ge(cf_sq_ready, 2 * j + 2)
                    for t in range(NT):
                        for m in range(2):
                            ins = mm(b[:, t:t + 1], cf_sq[m][:, t * P:(t + 1) * P], ones[:, 0:1], start=m == 0, stop=m == 1)
                if kind == "rs":
                    pe.wait_ge(cf_rs_ready, j + 1)
                    for t in range(NT):
                        ins = mm(b[:, t * P:(t + 1) * P], cf_rs[:, j, t:t + 1].to_broadcast([P, P]), ident,
                                 start=True, stop=True)
                if kind in ("cf", "na"):
                    t, half = Q_TILES[j], slice(name[2] * 512, (name[2] + 1) * 512)
                    if kind == "cf":
                        wait_drained(pe, ("rs", 1))
                    for k in range(4):
                        y = ycf[:, k, t * P:(t + 1) * P] if kind == "cf" else yna[j % 2][:, k]
                        w = wait_slot(pe, ("out", 0, (2 if kind == "cf" else 0) + k // 2))
                        ins = mm(b[:], y, w.rearrange("p (k n) -> p k n", k=2)[:, k % 2, half], start=k == 0, stop=k == 3)
                        if last and name[2] == 1 and k == 1:
                            used(ins)
                    owed[0] = last and name[2] == 1
                if kind == "ss":
                    wait_drained(pe, ("PO", HEADS * j + HEADS - 1))
                    for k in range(PAIRS):
                        ins = mm(b[:, 0:1], na_sq[:, k * P:(k + 1) * P], ones[:, 0:1], start=k == 0, stop=k == PAIRS - 1)
                        if k == 0:
                            used_up_by(ins)
                if kind in ("h2Ta", "h2Tb"):
                    pe.wait_ge(xn2_ready, j + 1)
                    for m in range(4):
                        k = m + 4 * (kind == "h2Tb")
                        ins = turn(b[:, m * P:(m + 1) * P], xn2[:, Q_TILES[j], k * P:(k + 1) * P])
                        if m == 0:
                            used_up_by(ins)
                if kind == "rt":
                    wait_drained(pe, ("h2Ta", j))
                    wait_drained(pe, ("h2Tb", j))
                    for k in range(KT):
                        ins = mm(b[:, 0:E], h2T[:, k], w_rt[:, k], start=k == 0, stop=k == KT - 1)
                fill_done(ins, name)

            for name in KEYS + QKV:
                wait_drained(pe, name)
            pe.wait_ge(pool_set, 3)
            for i in range(N + TAIL):
                if i < N:
                    scores(i)
                if STEPS <= i < N + STEPS:
                    j = i - STEPS
                    b = open_fill(pe, ("PT", j))
                    pe.wait_ge(prob_ready, j + 1)
                    for m in range(4):
                        ins = turn(b[:, m * P:(m + 1) * P], prob[j % 4][:, m * P:(m + 1) * P])
                    fill_done(ins, ("PT", j))
                if STEPS + 3 <= i <= N + STEPS + 1 and i % 2 == 0:
                    po = i - STEPS - 2
                    b = open_fill(pe, ("PO", po))
                    wait_drained(pe, ("PT", po))
                    for m in range(4):
                        for j in (po - 1, po):
                            t, h = UNITS[j]
                            hh = slice(h * DH, (h + 1) * DH)
                            v = v_sb[:, KEY_TILES[t][m], hh] if m < 2 else vc_sb[:, m - 2, hh]
                            p0 = (h % 2) * 64
                            ins = mm(b[p0:p0 + 64, 0:P], v, probT[j % 4][:, m * P:(m + 1) * P],
                                     start=m == 0, stop=m == 3)
                    fill_done(ins, ("PO", po))
                for name in extra_fills(i):
                    extra(name)
            pe.wait_ge(aff_ready, 1)
            b = open_fill(pe, ("affT", 0))
            for t in range(NT):
                ins = turn(b[0:E, t * P:(t + 1) * P], aff[:, t])
                if t == 0:
                    used(ins)
            fill_done(ins, ("affT", 0))
            pe.wait_ge(rank_ready, 1)
            b = open_fill(pe, ("posT", 0))
            for t in range(NT):
                ins = turn(b[:, t * E:(t + 1) * E], rank[:, t * P:(t + 1) * P])
            fill_done(ins, ("posT", 0))

            def gather(dst, kt):
                for t in range(NT):
                    ins = mm(dst[:, kt * CAP:(kt + 1) * CAP], xn2[:, t, kt * P:(kt + 1) * P], pick[:, t],
                             start=t == 0, stop=t == NT - 1)
                return ins

            pe.wait_ge(pick_ready, 1)
            b = open_fill(pe, ("xs", 0))
            for kt in range(KT):
                ins = gather(b, kt)
            fill_done(ins, ("xs", 0))
            wait_drained(pe, ("xs", 0))
            wait_drained(pe, ("posT", 0))
            for kind in ("h2Tb", "rt"):
                wait_drained(pe, (kind, NT - 1))
            pe.wait_ge(start_zero, 3)

            gate_b, up_b, turn_b, mix_b, down_b = bank[0:2], bank[2:4], bank[4], bank[5], bank[6:8]

            def combine(dst, s, i):
                t, b_ = i // 2, i % 2
                return mm(dst[:], gateT[s][:, t * P:(t + 1) * P], out_e[:, b_ * 512:(b_ + 1) * 512], start=True, stop=True)

            with pe.Fori(0, E // 2) as pair:
                for s in range(2):
                    e = pair * 2 + s

                    def open_turn(fill):
                        pe.wait_ge(t_drained, e * 5 + (5 + fill))

                    def hidden(c, fill):
                        q = (3 * s + c) % 2
                        pe.wait_ge(hid_ready, e * 3 + (c + 4))
                        open_turn(fill)
                        for j in range(HALVES[c] // P):
                            ins = turn(turn_b[:, j * P:(j + 1) * P], hid[q][:, j * P:(j + 1) * P])
                        ins.then_inc(t_filled, 1)

                    def down(j):
                        i = s * STAGE + GU_SLOTS + j
                        n_ = slot_of(i)
                        pe.wait_ge(loaded[n_], loads_until(pair, i))
                        w = ring[n_].rearrange("p (h n) -> p h n", h=2)
                        for b_ in range(2):
                            for half in range(2):
                                ins = mm(down_b[b_][64 * half:64 * half + 64], hidT[:, j, 64 * half:64 * half + 64],
                                         w[:, half, b_ * 512:(b_ + 1) * 512], start=j == 0, stop=j == DOWN_SLOTS - 1)
                        used(ins)

                    for c in range(3):
                        q, w_ = (3 * s + c) % 2, HALVES[c]
                        pe.wait_ge(hid_ready, e * 3 + (c + 2))
                        for k in range(KT):
                            for which, banks in ((0, gate_b), (1, up_b)):
                                i = s * STAGE + 8 * c + 2 * (k // 2) + which
                                n_ = slot_of(i)
                                if k % 2 == 0:
                                    pe.wait_ge(loaded[n_], loads_until(pair, i))
                                w = ring[n_][:, (k % 2) * 2 * w_:(k % 2 + 1) * 2 * w_]
                                for half in range(2):
                                    ins = mm(banks[q][64 * half:64 * half + 64, 0:w_], xsT[s][:, k],
                                             w[:, half * w_:(half + 1) * w_], start=k == 0, stop=k == KT - 1)
                                if k % 2:
                                    used(ins)
                            if c == 0:
                                pe.wait_ge(m_drained, e * 8 + (8 + k))
                                if k == 0:
                                    pe.wait_ge(d_drained, e + 1)
                                combine(mix_b, 1 - s, k).then_inc(m_filled, 1)
                            if (c, k) == (1, 1):
                                hidden(0, 0)
                            if (c, k) == (1, 3):
                                pe.wait_ge(gate_pick_ready, e * 2 + 2)
                                open_turn(1)
                                for t in range(NT):
                                    ins = turn(turn_b[:, t * P:(t + 1) * P], gate_pick[:, t])
                                ins.then_inc(t_filled, 1)
                            if (c, k) == (2, 1):
                                hidden(1, 2)
                            if c == 2 and 3 <= k < 7:
                                if k == 3:
                                    pe.wait_ge(pick_ready, e + 2)
                                    open_turn(3)
                                gather(turn_b, 2 * (k - 3))
                                ins = gather(turn_b, 2 * (k - 3) + 1)
                                if k == 6:
                                    ins.then_inc(t_filled, 1)
                    pe.wait_ge(d_drained, e + 1)
                    for j in range(8):
                        down(j)
                    hidden(2, 4)
                    pe.wait_ge(t_drained, e * 5 + 10)
                    for j in range(8, DOWN_SLOTS):
                        down(j)

            pe.wait_ge(d_drained, E + 1)
            pe.wait_ge(hid_ready, 3 + 3 * E)
            pe.wait_ge(m_drained, 8 + 8 * E)
            pe.wait_ge(t_drained, 5 + 5 * E)
            for i in range(8):
                combine(bank[i], 1, i).then_inc(last_filled, 1)


def constants():
    ident = np.eye(P)
    slots = np.tile(np.arange(1, CAP + 1), (P, 2))
    k = np.arange(64)
    a = 2 * np.pi * np.outer(k, k) / 64
    dd = np.zeros((P, 2, P))
    for g in range(2):
        dd[64 * g:64 * g + 64, 0, 64 * g:64 * g + 64] = np.cos(a)
        dd[64 * g:64 * g + 64, 1, 64 * g:64 * g + 64] = np.sin(a)
    consts = np.concatenate([ident, slots, dd.reshape(P, -1)], axis=1).astype(np.float32)
    dft = np.zeros((P, 2, 2, 2, 256))
    c16, r8 = np.divmod(np.arange(P), ROWS)
    cf, rf = np.divmod(np.arange(256), 4)
    m = rf * GRID_W + cf
    for par in range(2):
        for half in range(2):
            token = r8 * GRID_W + 32 * half + 2 * c16 + par
            a = 2 * np.pi * (np.outer(token, m) % SEQ) / SEQ
            dft[:, par, half, 0] = np.cos(a)
            dft[:, par, half, 1] = -np.sin(a)
    dft /= np.sqrt(SEQ * 64.0)
    return consts, dft.reshape(P, SLOT).astype(np.float32)


_INS = ["x", "cT", "ctx", "w_mod", "b_mod", "colv", "g_post_mix", "g_pre_ffn", "g_post_ffn", "w_in", "rpbT", "w_out",
        "w_router", "w_gate", "w_up", "w_down", "consts", "dft"]


def lay_out(inputs):
    a = {k: np.ascontiguousarray(v) for k, v in inputs.items()}

    def by_partition(v):
        return v.reshape(-1, P).T

    a["cT"] = np.ascontiguousarray(np.stack([by_partition(a["c"]), by_partition(a["c_ctx"])], axis=-1))
    conv = a["conv_w"][0].reshape(3, 2, P).transpose(2, 1, 0).reshape(P, 6)
    a["colv"] = np.ascontiguousarray(
        np.concatenate([by_partition(a["g_pre_mix"]), by_partition(a["g_mix_out"]), conv], axis=1))
    a["rpbT"] = np.ascontiguousarray(a["rpb"][0].transpose(0, 2, 1))
    a["w_router"] = np.ascontiguousarray(a["w_router"][0].reshape(KT, P, E).transpose(1, 0, 2))
    a["consts"], a["dft"] = constants()
    return {k: a[k] for k in _INS}


def kernel(**inputs):
    import concourse.bacc as bacc
    from concourse.bass_utils import run_bass_kernel_spmd

    nc = bacc.Bacc("TRN2", target_bir_lowering=False, num_devices=1, dynamic_dma_scratch_size=1024)
    arrays, args = {}, []
    for name, a in lay_out(inputs).items():
        arrays[f"in_{name}"] = a
        args.append(nc.dram_tensor(f"in_{name}", a.shape, mybir.dt.from_np(a.dtype), kind="ExternalInput").ap())
    args.append(nc.dram_tensor("out_x", (1, SEQ, D), F32, kind="ExternalOutput").ap())
    build_block(nc, *args)
    r = run_bass_kernel_spmd(nc, [arrays], core_ids=[0])
    return r.results[0]["out_x"]
```

```python
from contextlib import ExitStack

import numpy as np

import concourse.bass as bass
from concourse import mybir

F32 = mybir.dt.float32
F32R = mybir.dt.float32r
ALU = mybir.AluOpType
ACT = mybir.ActivationFunctionType
AX_X = mybir.AxisListType.X

P = 128
D = 1024
KT = D // P
SEQ, CTX = 512, 256
NT = SEQ // P
CT = CTX // P
GRID_W, ROWS = 64, 8
HEADS, DH = 8, 64
PAIRS = HEADS // 2
WIN_C = 16
NA_W, CONV_W = 512, 256
EPS = 1e-6
MASKED = -1e30
SCALE = DH ** -0.5
E, CAP = 16, 64
HID = 2816

TURNED = 64
Q_TILES = (1, 2, 0, 3)
KEY_TILES = {t: (t, (t + 1) % NT) for t in range(NT)}

RING = 10
SLOT = 2048
HALVES = (512, 512, 384)
CHUNK0 = (0, 1024, 2048)
assert 2 * sum(HALVES) == HID
GU_SLOTS = len(HALVES) * 8
HB = [(c, j) for c in range(3) for j in range(HALVES[c] // P)]
DOWN_SLOTS = len(HB)
STAGE = GU_SLOTS + DOWN_SLOTS
SPARE = 4
BIG_RING = RING + SPARE
assert 2 * STAGE % BIG_RING == 0
PRE = [("mod", 0, k) for k in range(KT)] + [("in", 0, h) for h in range(2)]
for g in range(1, 5):
    for h in range(2):
        PRE += [("mod", (g + 1) // 2, 4 * ((g + 1) % 2) + 2 * h + k) for k in range(2)] + [("in", g, h)]
PRE += [("dft", 0, 0)] + [("out", 0, k) for k in (2, 3, 0, 1)]
NPRE = len(PRE)
USED0 = NPRE + SPARE
IN_COLS = tuple(range(0, 2560, 512))

UNITS = [(t, h) for t in Q_TILES for h in range(HEADS)]
N = len(UNITS)
STEPS = 3
TAIL = 16
AFTER = HEADS + 4

GROUPS = ([("q", b) for b in range(4)], [("k", b) for b in range(4)] + [("kc", b) for b in range(2)],
          [("v", b) for b in range(4)] + [("vc", b) for b in range(CT)], [(n, b) for n in ("bg", "cg") for b in range(2)],
          [(n, b) for n in ("u", "f") for b in range(2)])


def pre_fills():
    every, ev = tuple(range(8)), ("act", "dve")
    out = [(("xT", k), "xT", every) for k in range(6)]
    out += [(("mod", 0), "first", every), (("modT", 0), "first", every)]
    out += [(("xT", k), "xT", (k,)) for k in (6, 7)]
    seven = tuple(range(7))
    for g in range(5):
        if g in (1, 3):
            out.append((("mod", (g + 1) // 2), "mod", (7,)))
        out += [(name, "dve" if name[0] == "u" else "act" if name[0] == "f" else ev[i % 2], (0, 1, 2, 3) if g == 0 else seven)
                for i, name in enumerate(GROUPS[g])]
        if g == 0:
            out += [(("cT", k), "cT", (4, 5, 6)) for k in range(4)]
    out += [(("modT", 1), "dve", every)] + [(("bc", b), ev[b % 2], every) for b in range(2)]
    out += [(("dft1", b), ev[b % 2], every) for b in range(4)]
    out += [(("modT", 2), "dve", every)]
    out += [(("dft2", b), "dft2", every) for b in range(2)]
    for i in range(N + TAIL):
        if i < N:
            out.append((("S", i), "S", (0, 1)))
        if STEPS <= i < N + STEPS:
            out.append((("PT", i - STEPS), "PT", (3, 4)))
        if STEPS + 3 <= i <= N + STEPS + 1 and i % 2 == 0:
            out.append((("PO", i - STEPS - 2), "PO", (5,)))
        for name in extra_fills(i):
            out.append((name, name[0], (2, 6, 7)))
    out += [(("affT", 0), "affT", every), (("posT", 0), "posT", every), (("xg", 0), "xg", every)]
    out += [(("xs", 0), "xs_act", every), (("xs", 1), "xs_dve", every)]
    return out


def tile_at(i, offset):
    j, rest = divmod(i - offset - AFTER, HEADS)
    return j if rest == 0 and 0 <= j < NT else None


def extra_fills(i):
    out = []
    if i in (1, 4):
        out.append(("sq", i // 4))
    if i in (3, 6):
        out.append(("rs", i // 6))
    for offset, names in ((9, [("rt",)]), (-3, [("cf", 0)]), (-2, [("cf", 1)]), (1, [("ss",), ("na", 0)]), (2, [("na", 1)]),
                          (7, [("h2Ta",), ("h2Tb",)])):
        j = tile_at(i, offset)
        if j is not None:
            out += [(n[0], j, *n[1:]) for n in names]
    if i == N + 6:
        out += [("last_bc", 2), ("last_bc", 3)]
    return out


def build_block(nc, x, cT, ctx, w_mod, b_mod, colv, g_post_mix, g_pre_ffn, g_post_ffn, w_in, rpbT, w_out,
                w_router, w_gate, w_up, w_down, consts, dft, out):
    fills = pre_fills()
    stream = {name: st for name, st, _ in fills}
    turn_no, bank_no, bank_before, in_stream, last_in, turns = {}, {}, {}, {}, {}, {}
    for name, st, banks in fills:
        turn_no[name] = in_stream[st] = in_stream.get(st, 0) + 1
        k = turns[banks] = turns.get(banks, -1) + 1
        bank_no[name] = banks[k % len(banks)]
        bank_before[name] = last_in.get(bank_no[name])
        last_in[bank_no[name]] = name

    with ExitStack() as stack:
        def sb(name, *shape):
            return stack.enter_context(nc.sbuf_tensor(name, [P, *shape], F32))

        def sem(name):
            return stack.enter_context(nc.semaphore(name))

        bank = [stack.enter_context(nc.psum_tensor(f"bank{i}", [P, 512], F32)) for i in range(8)]

        ARENA = 130 * 256
        rounded, begin = {}, 0
        with ExitStack() as early:
            ring_rounded = [early.enter_context(nc.sbuf_tensor(f"rounded_slot{n}", [P, SLOT], F32R)) for n in range(RING)]
            for kb, n in ((0, KT * SEQ), (16, KT * CTX), (24, KT * CTX), (48, SLOT), (86, KT * SEQ), (102, SLOT), (110, SLOT)):
                if kb * 256 > begin:
                    early.enter_context(nc.sbuf_tensor(f"gap{kb}", [P, kb * 256 - begin], F32))
                rounded[kb] = early.enter_context(nc.sbuf_tensor(f"rounded{kb}", [P, n], F32R))
                begin = kb * 256 + n
        ring_, arena = sb("ring", RING, SLOT), sb("arena", ARENA)
        cst = sb("cst", P + 2 * CAP)
        ident, iota = cst[:, 0:P], cst[:, P:P + 2 * CAP]
        ones = sb("ones", 128)
        cols = sb("cols", 22)
        g_pre_col, g_mix_col = cols[:, 0:8], cols[:, 8:16]
        conv_w = cols[:, 16:22].rearrange("p (b j) -> p b j", b=2)
        w_rt = sb("w_rt", KT, E)
        dd = sb("dd", 256)
        c_sb = sb("c_sb", KT, 2)
        s_pad = sb("s_pad", KT, 32)
        mod_row = sb("mod_row", 3, 512)
        one_col = sb("one_col", 1)
        mod_scale, mod_shift = sb("mod_scale", 2, KT), sb("mod_shift", 2, KT)
        ffn_gain, ffn_shift = sb("ffn_gain", KT), sb("ffn_shift", KT)
        minus_half, exp_first = sb("minus_half", 1), sb("exp_first", 1)
        x_ss, x_ms, x_rs = sb("x_ss", 6), sb("x_ms", 6), sb("x_rs", 6)
        neg_max, win_max, ctx_max = sb("neg_max", 32), sb("win_max", 32), sb("ctx_max", 32)
        sums, total, inv = sb("sums", 32, 2), sb("total", 32), sb("inv", 32)
        cf_ms, cf_rs = sb("cf_ms", 2, NT), sb("cf_rs", 2, NT)
        na_ms, na_rs = sb("na_ms", NT), sb("na_rs", NT)
        y_ss, y_ms, y_rs = sb("y_ss", NT), sb("y_ms", NT), sb("y_rs", NT)
        z_ss, z_ms, z_rs = sb("z_ss", NT), sb("z_ms", NT), sb("z_rs", NT)
        logit, aff = sb("logit", NT, E), sb("aff", NT, E)
        r_max, r_sum, r_inv = sb("r_max", NT), sb("r_sum", NT), sb("r_inv", NT)
        place = sb("place", NT, E + 2)
        top8 = sb("top8", 8)

        def shaped(v, shape):
            if len(shape) == 2:
                v = v.rearrange("p (a b) -> p a b", a=shape[0])
            if len(shape) == 3:
                v = v.rearrange("p (a b c) -> p a b c", a=shape[0], b=shape[1])
            return v

        def at(kb, *shape):
            o = int(kb * 256)
            return shaped(arena[:, o:o + int(np.prod(shape))], shape)

        def as_rounded(kb, *shape):
            return shaped(rounded[kb][:], shape)

        HEAD_W = (2 * WIN_C - 1) * ROWS
        SHIFTED = 64 + HEADS * HEAD_W + 64
        ring = [ring_[:, n] for n in range(RING)] + [at(k, SLOT) for k in (72, 80, 92, 118)]
        hT, hcT = as_rounded(0, KT, SEQ), as_rounded(16, KT, CTX)
        hT_rest, hT_rest_r = at(86, KT, SEQ), as_rounded(86, KT, SEQ)
        hcT_rest, hcT_rest_r = at(24, KT, CTX), as_rounded(24, KT, CTX)
        w_main = [[as_rounded(48 if g == 0 else 102, SLOT), as_rounded(110, SLOT)] for g in range(5)]
        shifted = at(72, SHIFTED)[0:ROWS]
        ctx_rows = at(60, CT, D)
        x_rows = at(102, NT, D)
        b_row, g_row = at(118, 3, 512), at(124, 2, 512)
        dft_g = at(88, 4, 512)
        dft_o = at(96, 2, 256)
        bg_sb, z_sb, f_sb = at(16, 2, SEQ), at(20, 2, 528), at(24.25, 2, SEQ)
        ycf = at(0, 4, SEQ)
        yna = [at(8 + 2 * i, PAIRS, P) for i in range(2)]
        na_sq = mod_row[:, 0]
        gain1 = at(12, D)
        x1 = at(16, NT, D)
        qTp = at(32, HEADS, SEQ)
        kT, kcT = at(48, PAIRS, SEQ), at(56, PAIRS, CTX)
        v_sb, vc_sb = at(60, 4, NA_W), at(68, CT, NA_W)
        bias = [at(72, HEADS, 256), at(80, HEADS, 256)]
        prob = [at(88 + 2 * i, 512) for i in range(3)] + [at(128, 512)]
        probT = [at(94 + 2 * i, 512) for i in range(4)]
        xn2 = at(102, NT, D)
        y_tmp = at(118, D)
        squares_out = [at(k, 512).bitcast(mybir.dt.bfloat16) for k in (56, 122)]
        h2T = at(124, KT, P)
        cf_sq = [at(118, 512), at(120, 512)]
        xsT = [at(0, KT, CAP), at(2, KT, CAP)]
        gain4 = at(4, D)
        out_e = at(8, D)
        acc = at(32, NT, D)
        first_rows = at(48, 512)
        silu_g = [at(48, 512), at(50, 512)]
        hid = [at(52, 512), at(54, 512)]
        hidT = at(56, DOWN_SLOTS, P)
        gateT = [at(62, 512), at(64, 512)]
        pick = at(66, NT, CAP)
        gate_pick = at(68, NT, 2 * CAP)
        fin = [at(102 + 4 * t, D) for t in range(NT)]
        work, chosen, count, one_row, rank = [at(k, 512)[0:E] for k in (70, 88, 90, 128, 126)]

        loaded = [sem(f"slot_loaded{i}") for i in range(BIG_RING)]
        x_loaded = [sem(f"x_loaded{t}") for t in range(NT)]
        c_loaded, ident_loaded, consts_loaded = sem("c_loaded"), sem("ident_loaded"), sem("consts_loaded")
        rows_loaded, ctx_loaded, shifted_loaded = sem("rows_loaded"), sem("ctx_loaded"), sem("shifted_loaded")
        shifted_stored, cols_loaded, gains_loaded = sem("shifted_stored"), sem("cols_loaded"), sem("gains_loaded")
        w_main_ready, w_ready, h_ready, hc_ready = sem("w_main_ready"), sem("w_ready"), sem("h_ready"), sem("hc_ready")
        raw_loaded = [sem(f"raw_loaded{i}") for i in range(3)]
        x_again, stored = sem("x_again"), sem("stored")
        filled = {st: sem(f"filled_{st}") for st in in_stream}
        drained = {st: sem(f"drained_{st}") for st in in_stream}
        slots_used = sem("slots_used")
        pool_set, dve_set = sem("pool_set"), sem("dve_set")
        act_chain, dve_chain, pool_chain = sem("act_chain"), sem("dve_chain"), sem("pool_chain")
        silu_ready, x_ss_ready, x_rs_ready, xn_ready = (
            sem("silu_ready"), sem("x_ss_ready"), sem("x_rs_ready"), sem("xn_ready"))
        rows_ready, bias_ready, odd_copied = sem("rows_ready"), sem("bias_ready"), sem("odd_copied")
        scores_ready, inv_ready, prob_ready = sem("scores_ready"), sem("inv_ready"), sem("prob_ready")
        conv_ready, cf_sq_ready, cf_rs_ready = sem("conv_ready"), sem("cf_sq_ready"), sem("cf_rs_ready")
        na_rs_ready = sem("na_rs_ready")
        y_ss_ready, y_rs_ready, x1_ready = sem("y_ss_ready"), sem("y_rs_ready"), sem("x1_ready")
        z_ss_ready, z_rs_ready, xn2_ready = sem("z_ss_ready"), sem("z_rs_ready"), sem("xn2_ready")
        r_sub_ready, r_exp_ready, aff_ready = sem("r_sub_ready"), sem("r_exp_ready"), sem("aff_ready")
        rank_ready, start_zero = sem("rank_ready"), sem("start_zero")
        silu_done, hid_ready = sem("silu_done"), sem("hid_ready")
        t_filled, t_drained = sem("t_filled"), sem("t_drained")
        m_filled, m_drained = sem("m_filled"), sem("m_drained")
        d_drained = sem("d_drained")
        pick_ready, gate_pick_ready = sem("pick_ready"), sem("gate_pick_ready")
        last_filled, acc_done, f_ss_ready, f_rs_ready, f_scaled = (
            sem("last_filled"), sem("acc_done"), sem("f_ss_ready"), sem("f_rs_ready"), sem("f_scaled"))
        f_ready = [sem(f"f_ready{t}") for t in range(NT)]

        def bank_of(name):
            return bank[bank_no[name]]

        def open_fill(pe, name):
            if bank_before[name] is not None:
                wait_drained(pe, bank_before[name])
            return bank_of(name)

        def fill_done(ins, name):
            ins.then_inc(filled[stream[name]], 1)

        def wait_fill(eng, name):
            eng.wait_ge(filled[stream[name]], turn_no[name])
            return bank_of(name)

        def drain_done(ins, name):
            ins.then_inc(drained[stream[name]], 1)

        def wait_drained(eng, name):
            eng.wait_ge(drained[stream[name]], turn_no[name])

        def link(eng, chain, ins):
            chain[1] += 1
            ins.then_inc(chain[0], 1)
            eng.wait_ge(chain[0], chain[1])

        def mine(names, who):
            return [n for n in names if stream[n] == who]

        def bc_dst(b):
            return (gain1, gain4)[b // 2][:, (b % 2) * 512:(b % 2 + 1) * 512]

        BACK = ((0, TURNED, SEQ - TURNED), (SEQ - TURNED, 0, TURNED))

        def pieces(name):
            kind, b = name[0], name[1]
            src = bank_of(name)
            if kind == "kc":
                return [(kcT[:, 2 * b:2 * b + 2].rearrange("p a n -> p (a n)"), src[:])]
            if kind == "q":
                return [(qTp[p0:p0 + 64, 2 * b + (p0 > 0), n0:n0 + n], src[p0:p0 + 64, p:p + n])
                        for p0 in (0, 64) for n0, p, n in BACK]
            if kind == "f":
                dst = f_sb[:, b].rearrange("p (e c r) -> p c e r", e=2, r=ROWS)
                src = src[:].rearrange("p (c e r) -> p c e r", e=2, r=ROWS)
                return [(dst[:, n0 // 16:(n0 + n) // 16], src[:, p // 16:(p + n) // 16]) for n0, p, n in BACK]
            if kind in ("bg", "cg"):
                dst = bg_sb[:, b] if kind == "bg" else z_sb[:, b, 8:520]
                return [(dst[:, n0:n0 + n], src[:, p:p + n]) for n0, p, n in BACK]
            dst = {"k": kT, "vc": vc_sb, "v": v_sb, "dft1": dft_g}.get(kind)
            if dst is not None:
                return [(dst[:, b], src[:])]
            if kind in ("bc", "last_bc"):
                return [(bc_dst(b), src[:])]

        def in_slot(g, h):
            n = PRE.index(("in", g, h))
            return n, (ring[n % RING], ring_rounded[n % RING][:]), w_main[g][h]

        def wait_slot(eng, key):
            n = PRE.index(key)
            eng.wait_ge(loaded[n % RING], 16 * (n // RING + 1))
            return ring[n % RING]

        x_v = x[0].rearrange("(r c) d -> c r d", c=GRID_W)
        out_v = out[0].rearrange("(r c) d -> c r d", c=GRID_W)
        pre_src = {}
        for k in range(KT):
            for g in range(3):
                pre_src["mod", g, k] = w_mod[0, k * P:(k + 1) * P, g * SLOT:(g + 1) * SLOT]
        for g in range(5):
            for h in range(2):
                pre_src["in", g, h] = w_in[0, h * 512:(h + 1) * 512, IN_COLS[g]:IN_COLS[g] + 512].rearrange(
                    "(k p) n -> p k n", p=P)
        pre_src["dft", 0, 0] = dft
        for k in range(4):
            pre_src["out", 0, k] = w_out[0, k * 256:(k + 1) * 256, :].rearrange("(k p) n -> p k n", p=P)
        shifted_dram = nc.dram_tensor("shifted_dram", (ROWS, SHIFTED), F32, kind="Internal").ap()

        FIRST_TURNS = [(j, half) for j in range(2) for half in range(2)]

        def slot_of(i):
            m = i % BIG_RING
            return (NPRE + m) % RING if m < RING else m

        def loads_until(pair, i):
            before = sum(n % RING == slot_of(i) for n in range(NPRE))
            return pair * (16 * (2 * STAGE // BIG_RING)) + 16 * (before + i // BIG_RING + 1)

        def load_window_biases(eng, which, loaded_, columns=range(WIN_C)):
            for c in columns:
                rows_of_heads = bass.AP(shifted_dram.tensor, shifted_dram.offset + 64 + (7 - c) * ROWS,
                                        [shifted_dram.ap[0], [HEAD_W, HEADS], [1, 256]])
                eng.dma_start(bias[which][8 * c:8 * c + 8], rows_of_heads).then_inc(loaded_, 16)

        block = stack.enter_context(nc.Block())

        @block.sync
        def _(sp):
            c0 = TURNED // ROWS
            for c, n_, t, p0 in ((GRID_W - c0, c0, 0, 0), (0, 16 - c0, 0, TURNED), (16 - c0, 16, 1, 0), (32 - c0, 16, 2, 0),
                                 (48 - c0, 16, 3, 0)):
                sp.dma_start(x_rows[p0:p0 + n_ * ROWS, t], x_v[c:c + n_]).then_inc(x_loaded[t], 16)
            sp.wait_ge(dve_set, 2)
            small = [(cols[:], colv, cols_loaded)]
            small += [(b_row[rows, g, :], b_mod[0, g * SLOT:(g + 1) * SLOT].rearrange("(a n) -> a n", a=4), rows_loaded)
                      for rows, g in ((slice(0, P, 32), 0), (slice(1, P, 32), 0), (slice(0, P, 32), 1), (slice(0, P, 32), 2))]
            small += [(g_row[rows, g, :], vec[0].rearrange("(a n) -> a n", a=2), gains_loaded)
                      for rows, g, vec in ((slice(0, 64, 32), 0, g_post_mix), (slice(0, 64, 32), 1, g_pre_ffn),
                                           (slice(64, P, 32), 1, g_post_ffn))]
            for n, key in enumerate(PRE):
                if 1 <= n <= len(small):
                    dst, src, told = small[n - 1]
                    sp.dma_start(dst, src).then_inc(told, 16)
                if key == ("mod", 2, 0):
                    sp.dma_start(w_rt[:], w_router).then_inc(consts_loaded, 16)
                    sp.dma_start(dd[:], consts[:, 256:512]).then_inc(consts_loaded, 16)
                if key == ("mod", 1, 0):
                    sp.dma_start(ctx_rows[:], ctx[0].rearrange("(t p) d -> p t d", p=P)).then_inc(ctx_loaded, 16)
                if key == ("mod", 2, 0):
                    sp.wait_ge(shifted_stored, 16)
                    load_window_biases(sp, 0, raw_loaded[0])
                if key == ("out", 0, 2):
                    wait_fill(sp, ("f", 1))
                    load_window_biases(sp, 1, raw_loaded[1])
                if n >= RING:
                    sp.wait_ge(slots_used, n - RING + 1)
                dst = ring[n % RING]
                if key[0] == "in":
                    dst = dst.rearrange("p (k n) -> p k n", k=4)
                if key[0] == "out":
                    dst = dst.rearrange("p (k n) -> p k n", k=2)
                sp.dma_start(dst, pre_src[key]).then_inc(loaded[n % RING], 16)
            with sp.Fori(0, E // 2) as pair:
                for i in range(2 * STAGE):
                    e, i_ = pair * 2 + i // STAGE, i % STAGE
                    sp.wait_ge(slots_used, pair * (2 * STAGE) + (USED0 + i - BIG_RING + 1))
                    s = slot_of(i)
                    if i_ < GU_SLOTS:
                        c, kk, w = i_ // 8, (i_ % 8) // 2, (w_gate, w_up)[i_ % 2]
                        n = 2 * HALVES[c]
                        src = w[0, bass.ds(e, 1), kk * 256:(kk + 1) * 256, CHUNK0[c]:CHUNK0[c] + n].rearrange(
                            "a (k p) n -> p (a k) n", p=P)
                        dst = ring[s][:, 0:2 * n].rearrange("p (k n) -> p k n", k=2)
                    else:
                        c, j = HB[i_ - GU_SLOTS]
                        src = w_down[0, bass.ds(e, 1), CHUNK0[c]:CHUNK0[c] + 2 * HALVES[c], :].rearrange(
                            "a (h f) n -> f (a h) n", h=2)[j * P:(j + 1) * P]
                        dst = ring[s].rearrange("p (h n) -> p h n", h=2)
                    sp.dma_start(dst, src).then_inc(loaded[s], 16)

        @block.gpsimd
        def _(pool):
            chain = [pool_chain, 0]

            def inverse_root(rs, ms):
                return pool.tensor_tensor(rs, ms, minus_half[:, 0:1].to_broadcast([P, ms.shape[1]]), ALU.pow)

            def inverse_rms(rs, ms, ss, width):
                link(pool, chain, pool.tensor_scalar(ms, ss, 1.0 / width, EPS, ALU.mult, ALU.add))
                return inverse_root(rs, ms)

            pool.memset(shifted, 0.0).then_inc(pool_set, 1)
            link(pool, chain, pool.memset(minus_half[:], -0.5))
            for t in range(NT + CT):
                pool.wait_ge(x_ss_ready, t + 1)
                inverse_rms(x_rs[:, t:t + 1], x_ms[:, t:t + 1], x_ss[:, t:t + 1], D).then_inc(x_rs_ready, 1)
                if t == NT - 1:
                    pool.memset(qTp[:], 0.0).then_inc(pool_set, 1)
                    pool.memset(ones[:], 1.0).then_inc(pool_set, 1)
                    pool.memset(place[:], 0.0).then_inc(pool_set, 1)

            def times8(v):
                link(pool, chain, pool.tensor_scalar(v, v, 8.0, 1.0, ALU.mult, ALU.mult))

            def masked(v):
                link(pool, chain, pool.memset(v, 8 * MASKED))

            def from_c(b, k0, k1, col0):
                v = b[:, :, col0:col0 + 8 * (k1 - k0)].rearrange("p h (k i) -> p h k i", i=8)
                return pool.affine_select(
                    out=v, in_=v, pattern=[[0, HEADS], [8, k1 - k0], [0, 8]], compare_op=ALU.is_ge,
                    fill=8 * MASKED, base=8 * k0 + 7, channel_multiplier=-1)

            def to_c(b, k0, k1, col0):
                v = b[:, :, col0:col0 + 8 * (k1 - k0)].rearrange("p h (k i) -> p h k i", i=8)
                return pool.affine_select(
                    out=v, in_=v, pattern=[[0, HEADS], [-8, k1 - k0], [0, 8]], compare_op=ALU.is_ge,
                    fill=8 * MASKED, base=8 * (WIN_C - 1) - 8 * k0, channel_multiplier=1)

            inner, edge = bias
            pool.wait_ge(raw_loaded[0], 16 * WIN_C)
            times8(inner)
            link(pool, chain, from_c(inner, 0, 32, 0))
            to_c(inner, 0, 32, 0).then_inc(bias_ready, 1)
            pool.wait_ge(raw_loaded[1], 16 * WIN_C)
            times8(edge)
            masked(edge[:, :, 0:64])
            link(pool, chain, from_c(edge, 8, 16, 64))
            link(pool, chain, from_c(edge, 16, 32, 128))
            to_c(edge, 24, 32, 192).then_inc(bias_ready, 1)

            for i in range(N + TAIL):
                if i < N:
                    pool.wait_ge(inv_ready, i + 1)
                    pool.tensor_scalar(prob[i % 4], prob[i % 4], inv[:, i:i + 1], 1.0, ALU.mult, ALU.mult)\
                        .then_inc(prob_ready, 1)
                if i in (1, 4):
                    g = i // 4
                    wait_drained(pool, ("sq", g))
                    inverse_root(cf_rs[:, g], cf_ms[:, g]).then_inc(cf_rs_ready, 1)
                if i == 2 * HEADS + 3:
                    pool.wait_ge(raw_loaded[2], 16 * WIN_C)
                    times8(inner[:, 0:4])
                if i == 2 * HEADS + 4:
                    times8(inner[:, 4:8])
                if i == 2 * HEADS + 5:
                    masked(inner[:, :, 192:256])
                if i == 2 * HEADS + 6:
                    link(pool, chain, from_c(inner, 0, 8, 0))
                    to_c(inner, 16, 24, 128).then_inc(bias_ready, 1)
                j = tile_at(i, 1)
                if j is not None:
                    wait_drained(pool, ("ss", j))
                    inverse_root(na_rs[:, j:j + 1], na_ms[:, j:j + 1]).then_inc(na_rs_ready, 1)
                for offset, ready, (rs, ms, ss), told in ((2, y_ss_ready, (y_rs, y_ms, y_ss), y_rs_ready),
                                                          (4, z_ss_ready, (z_rs, z_ms, z_ss), z_rs_ready)):
                    j = tile_at(i, offset)
                    if j is not None:
                        pool.wait_ge(ready, j + 1)
                        inverse_rms(rs[:, j:j + 1], ms[:, j:j + 1], ss[:, j:j + 1], D).then_inc(told, 1)

            wait_fill(pool, ("na", NT - 1, 1))
            pool.memset(acc[:], 0.0).then_inc(start_zero, 1)
            pool.memset(out_e, 0.0).then_inc(start_zero, 1)
            pool.memset(gateT[1], 0.0).then_inc(start_zero, 1)

            for t in range(NT):
                pool.wait_ge(f_ss_ready, t + 1)
                inverse_rms(y_rs[:, t:t + 1], y_ms[:, t:t + 1], y_ss[:, t:t + 1], D).then_inc(f_rs_ready, 1)
                if t in (1, 3):
                    pool.wait_ge(f_scaled, t)
                    pool.tensor_tensor(fin[t - 1], fin[t - 1], x1[:, t - 1], ALU.add).then_inc(f_ready[t - 1], 1)

        @block.scalar
        def _(act):
            chain = [act_chain, 0]

            def copy_out(names):
                for name in mine(names, "act"):
                    wait_fill(act, name)
                    for dst, src in pieces(name):
                        ins = nc.scalar.activation(dst, src, ACT.Copy)
                    drain_done(ins, name)

            last_squares = []

            def squares(rows, ss, told, number_, late=1):
                if last_squares:
                    act.wait_ge(*last_squares)
                nc.scalar.activation(squares_out[late], rows, ACT.Square, accum_out=ss).then_inc(told, 1)
                last_squares[:] = [told, number_]

            act.dma_start(c_sb[:], cT).then_inc(c_loaded, 16)
            act.dma_start(cst[:], consts[:, 0:256]).then_inc(ident_loaded, 16)
            act.wait_ge(c_loaded, 16)
            act.wait_ge(dve_set, 1)
            nc.scalar.activation(s_pad[:, :, 0:2], c_sb[:], ACT.Silu).then_inc(silu_ready, 1)
            for t in range(NT):
                act.wait_ge(x_loaded[t], 16 * 2 if t == 0 else 16)
                squares(x_rows[:, t], x_ss[:, t:t + 1], x_ss_ready, t + 1, 0)
            act.wait_ge(pool_set, 1)
            for r in range(ROWS):
                act.dma_start(shifted[r:r + 1, 64:64 + HEADS * HEAD_W].rearrange("p (m i) -> p m i", i=8),
                              rpbT[:, :, 7 - r:15 - r].rearrange("(a h) m i -> a (h m) i", a=1))\
                    .then_inc(shifted_loaded, 16)

            def main_part(g, h):
                n, (w, _), main = in_slot(g, h)
                act.wait_ge(loaded[n % RING], 16 * (n // RING + 1))
                if (g, h) == (0, 1):
                    wait_fill(act, ("xT", KT - 1))
                if g >= 1 and (g, h) != (1, 0):
                    act.wait_ge(slots_used, in_slot(g - 1, h)[0] + 1)
                nc.scalar.activation(main, w, ACT.Copy).then_inc(w_main_ready, 1)

            def h_of(src, who, kt, main, whole):
                for dst in (whole, main):
                    ins = nc.scalar.activation(dst, src, ACT.Identity, scale=mod_scale[:, who, kt:kt + 1],
                                               bias=mod_shift[:, who, kt:kt + 1])
                return ins

            main_part(0, 0)
            wait_drained(act, ("modT", 0))
            for kt in range(KT):
                b = wait_fill(act, ("xT", kt))
                drain_done(h_of(b[:], 0, kt, hT[:, kt], hT_rest[:, kt]), ("xT", kt))
            main_part(0, 1)
            act.wait_ge(shifted_loaded, 16 * ROWS)
            act.dma_start(shifted_dram, shifted).then_inc(shifted_stored, 16)
            act.wait_ge(ctx_loaded, 16)
            for t in range(CT):
                squares(ctx_rows[:, t], x_ss[:, NT + t:NT + t + 1], x_ss_ready, NT + t + 1, 0)
            main_part(1, 0)
            for f in range(4):
                b = wait_fill(act, ("cT", f))
                for j in range(2):
                    kt = 2 * f + j
                    ins = h_of(b[:, j * CTX:(j + 1) * CTX], 1, kt, hcT[:, kt], hcT_rest[:, kt])
                drain_done(ins, ("cT", f))
            act.wait_ge(pool_set, 2)
            for g in range(5):
                if 1 <= g < 4:
                    main_part(g + 1, 0)
                copy_out(GROUPS[g])
                if g < 4:
                    main_part(g + 1, 1)
            copy_out([("bc", b) for b in range(2)])
            copy_out([("dft1", b) for b in range(4)])
            for b in range(2):
                src = wait_fill(act, ("dft2", b))
                nc.scalar.activation(dft_o[:, b], src[:, 256:512], ACT.Copy).then_inc(odd_copied, 1)
            act.wait_ge(conv_ready, 2)
            wait_fill(act, ("dft1", 3))
            for t in range(NT):
                act.dma_start(x1[:, t], x_v[16 * t:16 * (t + 1)]).then_inc(x_again, 16)

            def features_squared(g):
                for j in range(2):
                    nc.scalar.activation(cf_sq[j], ycf[:, 2 * g + j], ACT.Square).then_inc(cf_sq_ready, 1)

            act.wait_ge(rows_ready, 2)
            features_squared(0)
            nc.scalar.activation(exp_first[:], minus_half[:], ACT.Exp)
            for i in range(N + TAIL):
                if i < N:
                    s = bank_of(("S", i))
                    act.wait_ge(scores_ready, i + 1)
                    nc.scalar.activation(prob[i % 4][:, 0:256], prob[i % 4][:, 0:256], ACT.Exp, scale=-1.0,
                                         bias=neg_max[:, i:i + 1], accum_out=sums[:, i, 0:1])
                    drain_done(nc.scalar.activation(prob[i % 4][:, 256:512], s[:, 256:512], ACT.Exp, scale=SCALE,
                                                    bias=neg_max[:, i:i + 1], accum_out=sums[:, i, 1:2]), ("S", i))
                if i == 3:
                    wait_drained(act, ("dft2", 1))
                    wait_fill(act, ("sq", 0))
                    features_squared(1)
                part = i - (2 * HEADS - 1)
                if 0 <= part < 4:
                    load_window_biases(act, 0, raw_loaded[2], range(4 * part, 4 * part + 4))
                for name in extra_fills(i - 1):
                    kind, j = name[0], name[1]
                    if kind == "cf":
                        if name[2] == 0 and j >= 1:
                            act.wait_ge(x1_ready, j)
                        src = wait_fill(act, name)
                        drain_done(nc.scalar.activation(y_tmp[:, name[2] * 512:(name[2] + 1) * 512], src[:], ACT.Copy), name)
                    if kind == "h2Ta":
                        src = wait_fill(act, name)
                        for k in range(4):
                            ins = nc.scalar.activation(h2T[:, k], src[:, k * P:(k + 1) * P], ACT.Identity,
                                                       scale=ffn_gain[:, k:k + 1], bias=ffn_shift[:, k:k + 1])
                        drain_done(ins, name)
                    if kind == "rt":
                        src = wait_fill(act, name)
                        drain_done(nc.scalar.activation(logit[:, Q_TILES[j]], src[:, 0:E], ACT.Copy), name)
                    if kind == "last_bc":
                        (dst, src), = pieces(name)
                        wait_fill(act, name)
                        drain_done(nc.scalar.activation(dst, src, ACT.Copy), name)
                j = tile_at(i, 3)
                if j is not None:
                    wait_drained(act, ("na", j, 1))
                    squares(y_tmp, y_ss[:, j:j + 1], y_ss_ready, j + 1)
                j = tile_at(i, 5)
                if j is not None:
                    act.wait_ge(x1_ready, j + 1)
                    squares(x1[:, Q_TILES[j]], z_ss[:, j:j + 1], z_ss_ready, j + 1)
                if STEPS + 3 <= i <= N + STEPS + 1 and i % 2 == 0:
                    po = i - STEPS - 2
                    t, h = UNITS[po]
                    j = po // HEADS
                    src = wait_fill(act, ("PO", po))
                    if h == 1 and j >= 1:
                        wait_fill(act, ("ss", j - 1))
                    if h == 1 and j >= 2:
                        wait_fill(act, ("na", j - 2, 1))
                    nc.scalar.activation(yna[j % 2][:, h // 2], src[:, 0:P], ACT.Identity, scale=g_mix_col[:, h // 2:h // 2 + 1])
                    drain_done(nc.scalar.activation(na_sq[:, (h // 2) * P:(h // 2 + 1) * P], src[:, 0:P], ACT.Square),
                               ("PO", po))

            def expert_tokens(dst, src):
                for k in range(KT):
                    ins = nc.scalar.activation(dst[:, k], src[:, k * CAP:(k + 1) * CAP], ACT.Identity,
                                               scale=ffn_gain[:, k:k + 1], bias=ffn_shift[:, k:k + 1])
                return ins

            act.wait_ge(r_sub_ready, 1)
            nc.scalar.activation(aff[:], logit[:], ACT.Exp).then_inc(r_exp_ready, 1)
            src = wait_fill(act, ("xg", 0))
            drain_done(nc.scalar.activation(first_rows, src[:], ACT.Copy), ("xg", 0))
            src = wait_fill(act, ("xs", 0))
            for j, half in FIRST_TURNS:
                k = 4 * half + j
                ins = nc.scalar.activation(xsT[0][:, k], src[:, j * P + half * CAP:j * P + (half + 1) * CAP], ACT.Identity,
                                           scale=ffn_gain[:, k:k + 1], bias=ffn_shift[:, k:k + 1])
            drain_done(ins, ("xs", 0))

            with act.Fori(0, E // 2) as pair:
                for s in range(2):
                    e = pair * 2 + s

                    def silu(c):
                        q = (3 * s + c) % 2
                        act.wait_ge(slots_used, pair * (2 * STAGE) + (USED0 + s * STAGE + 8 * (c + 1)))
                        nc.scalar.activation(silu_g[q][:, 0:HALVES[c]], bank[q][:, 0:HALVES[c]], ACT.Silu)\
                            .then_inc(silu_done, 1)

                    def wait_turn(fill):
                        act.wait_ge(t_filled, e * 5 + (fill + 1))

                    def from_t(dst, width, fill):
                        wait_turn(fill)
                        nc.scalar.activation(dst, bank[4][:, 0:width], ACT.Copy).then_inc(t_drained, 1)

                    silu(0)
                    from_t(hidT[:, 0:4].rearrange("p j n -> p (j n)"), 512, 0)
                    from_t(gateT[s], 512, 1)
                    silu(1)
                    from_t(hidT[:, 4:8].rearrange("p j n -> p (j n)"), 512, 2)
                    wait_turn(3)
                    expert_tokens(xsT[1 - s], bank[4]).then_inc(t_drained, 1)
                    silu(2)
                    from_t(hidT[:, 8:11].rearrange("p j n -> p (j n)"), 384, 4)
                    act.wait_ge(slots_used, pair * (2 * STAGE) + (USED0 + (s + 1) * STAGE))
                    for b in range(2):
                        ins = nc.scalar.activation(out_e[:, b * 512:(b + 1) * 512], bank[6 + b][:], ACT.Copy)
                    ins.then_inc(d_drained, 1)

            for t in range(NT):
                act.wait_ge(acc_done, t + 1)
                squares(acc[:, t], y_ss[:, t:t + 1], f_ss_ready, t + 1)
            for t, c0, c1, count_ in ((0, 0, D, 1), (1, 0, D, 1), (3, 0, 512, 1), (2, 0, D, 1), (3, 512, D, 2)):
                act.wait_ge(f_ready[t], count_)
                act.dma_start(out_v[16 * t:16 * (t + 1), :, c0:c1], fin[t][:, c0:c1]).then_inc(stored, 16)
            act.wait_ge(stored, 16 * (NT + 1))

        @block.vector
        def _(dve):
            chain = [dve_chain, 0]

            def copy_out(names):
                for name in mine(names, "dve"):
                    wait_fill(dve, name)
                    for dst, src in pieces(name):
                        ins = nc.vector.tensor_copy(dst, src)
                    drain_done(ins, name)

            nc.vector.memset(s_pad[:], 0.0).then_inc(dve_set, 1)
            nc.vector.memset(b_row[:], 0.0)
            nc.vector.memset(g_row[:], 1.0).then_inc(dve_set, 1)
            link(dve, chain, nc.vector.memset(one_col[:], 0.0))
            nc.vector.memset(one_col[0:64], 1.0)
            for s, n in ((hid_ready, 3), (t_drained, 5), (m_drained, 8), (d_drained, 1)):
                dve.nop().then_inc(s, n)

            def normalise_rows(t):
                rows = x_rows[:, t] if t < NT else ctx_rows[:, t - NT]
                dve.wait_ge(x_rs_ready, t + 1)
                nc.vector.tensor_scalar(rows, rows, x_rs[:, t:t + 1], None, ALU.mult).then_inc(xn_ready, 1)

            for t in range(NT):
                normalise_rows(t)
            dve.wait_ge(rows_loaded, 16 * 4)
            src = wait_fill(dve, ("mod", 0))
            drain_done(nc.vector.tensor_tensor(mod_row[:, 0], src[:], b_row[:, 0], ALU.add), ("mod", 0))
            src = wait_fill(dve, ("modT", 0))
            dve.wait_ge(cols_loaded, 16)
            v = src[:].rearrange("p (b g r) -> p g b r", b=4, g=4)
            for who in range(2):
                nc.vector.tensor_copy(mod_shift[:, who].rearrange("p (g b) -> p g b", g=2), v[:, 0:2, :, who])
                ins = nc.vector.scalar_tensor_tensor(
                    out=mod_scale[:, who].rearrange("p (g b) -> p g b", g=2), in0=v[:, 2:4, :, who], scalar=1.0,
                    in1=g_pre_col.rearrange("p (g b) -> p g b", g=2), op0=ALU.add, op1=ALU.mult)
            drain_done(ins, ("modT", 0))
            wait_drained(dve, ("modT", 0))
            def rest(g, h):
                _, (w, w_rounded), main = in_slot(g, h)
                dve.wait_ge(w_main_ready, 2 * g + h + 1)
                nc.vector.tensor_tensor(w_rounded, w, main.bitcast(F32), ALU.subtract).then_inc(w_ready, 1)

            rest(0, 0)
            for kt in range(KT):
                wait_drained(dve, ("xT", kt))
                nc.vector.tensor_tensor(hT_rest_r[:, kt], hT_rest[:, kt], hT[:, kt].bitcast(F32), ALU.subtract).then_inc(h_ready, 1)
                if kt == 3:
                    rest(0, 1)
            for t in range(CT):
                normalise_rows(NT + t)
            rest(1, 0)
            for f in range(4):
                wait_drained(dve, ("cT", f))
                ks = slice(2 * f, 2 * f + 2)
                nc.vector.tensor_tensor(hcT_rest_r[:, ks], hcT_rest[:, ks], hcT[:, ks].bitcast(F32), ALU.subtract)\
                    .then_inc(hc_ready, 1)
            dve.wait_ge(pool_set, 2)

            def gain_rows(g):
                dve.wait_ge(gains_loaded, 16 * 3)
                src = wait_fill(dve, ("mod", g))
                drain_done(nc.vector.tensor_tensor(mod_row[:, g], src[:], b_row[:, g], ALU.add), ("mod", g))
                wait_drained(dve, ("mod", g))
                nc.vector.scalar_tensor_tensor(
                    out=mod_row[:, g], in0=mod_row[:, g], scalar=0.0 if g == 1 else one_col[:, 0:1],
                    in1=g_row[:, g - 1], op0=ALU.add, op1=ALU.mult).then_inc(rows_ready, 1)

            for g in range(4):
                if g >= 1:
                    rest(g + 1, 0)
                copy_out(GROUPS[g])
                if g == 2:
                    gain_rows(1)
                rest(g + 1, 1)
            for b in range(2):
                src = wait_fill(dve, ("u", b))
                wait_drained(dve, ("cg", b))
                for n0, p, n in BACK:
                    z = z_sb[:, b, 8 + n0:8 + n0 + n]
                    ins = nc.vector.tensor_tensor(z, z, src[:, p:p + n], ALU.mult)
                drain_done(ins, ("u", b))
            wait_drained(dve, ("u", 1))
            nc.vector.memset(z_sb[:, :, 0:1], 0.0)
            nc.vector.tensor_copy(z_sb[:, :, 1:8], z_sb[:, :, 512:519])
            nc.vector.tensor_copy(z_sb[:, :, 520:527], z_sb[:, :, 9:16])
            link(dve, chain, nc.vector.memset(z_sb[:, :, 527:528], 0.0))
            wait_fill(dve, ("f", 1))
            wait_drained(dve, ("bg", 0))
            wait_drained(dve, ("bg", 1))
            for b in range(2):
                y = ycf[:, b]
                link(dve, chain, nc.vector.tensor_scalar(y, z_sb[:, b, 0:512], conv_w[:, b, 0:1], None, ALU.mult))
                for j in (1, 2):
                    link(dve, chain, nc.vector.scalar_tensor_tensor(
                        out=y, in0=z_sb[:, b, 8 * j:8 * j + 512], scalar=conv_w[:, b, j:j + 1], in1=y,
                        op0=ALU.mult, op1=ALU.add))
                nc.vector.tensor_tensor(y, y, bg_sb[:, b], ALU.mult).then_inc(conv_ready, 1)
            gain_rows(2)

            def column_of(g, dst, pos):
                v = wait_fill(dve, ("modT", g))[:].rearrange("p (b g r) -> p g b r", b=4, g=4)
                drain_done(nc.vector.tensor_copy(dst[:].rearrange("p (g b) -> p g b", g=2), v[:, pos:pos + 2, :, 0]),
                           ("modT", g))

            column_of(1, ffn_shift, 2)
            copy_out([("bc", b) for b in range(2)])
            copy_out([("dft1", b) for b in range(4)])
            column_of(2, ffn_gain, 0)
            for b in range(2):
                src = bank_of(("dft2", b))
                dve.wait_ge(odd_copied, b + 1)
                y = ycf[:, 2 + b].rearrange("p (c r) -> p c r", r=8)
                even = src[:, 0:256].rearrange("p (c r) -> p c r", r=4)
                odd = dft_o[:, b].rearrange("p (c r) -> p c r", r=4)
                nc.vector.tensor_tensor(y[:, :, 0:4], even, odd, ALU.add)
                drain_done(nc.vector.tensor_tensor(y[:, :, 4:8], even, odd, ALU.subtract), ("dft2", b))
            wait_drained(dve, ("dft2", 1))
            dve.wait_ge(rows_ready, 2)

            for i in range(N + TAIL):
                if i < N:
                    t, h = UNITS[i]
                    if i in (0, 2 * HEADS, 3 * HEADS):
                        dve.wait_ge(bias_ready, 1 + i // HEADS - (1 if i else 0))
                    s = wait_fill(dve, ("S", i))
                    nc.vector.tensor_tensor_reduce(
                        out=prob[i % 4][:, 0:256], in0=s[:, 0:256], in1=bias[1 if t == 0 else 0][:, h], scale=-SCALE,
                        scalar=-3 * MASKED, op0=ALU.add, op1=ALU.min, accum_out=win_max[:, i:i + 1])
                    link(dve, chain, nc.vector.tensor_reduce(ctx_max[:, i:i + 1], s[:, 256:512], AX_X, ALU.max))
                    nc.vector.tensor_scalar(neg_max[:, i:i + 1], ctx_max[:, i:i + 1], -SCALE, win_max[:, i:i + 1],
                                            ALU.mult, ALU.min).then_inc(scores_ready, 1)
                if 1 <= i <= N:
                    j = i - 1
                    wait_drained(dve, ("S", j))
                    link(dve, chain, nc.vector.tensor_tensor(total[:, j:j + 1], sums[:, j, 0:1], sums[:, j, 1:2], ALU.add))
                    nc.vector.reciprocal(inv[:, j:j + 1], total[:, j:j + 1]).then_inc(inv_ready, 1)
                if STEPS <= i < N + STEPS:
                    j = i - STEPS
                    src = wait_fill(dve, ("PT", j))
                    drain_done(nc.vector.tensor_copy(probT[j % 4], src[:]), ("PT", j))
                for name in extra_fills(i - 1):
                    kind, j = name[0], name[1]
                    if kind == "sq":
                        src = wait_fill(dve, name)
                        drain_done(nc.vector.tensor_scalar(cf_ms[:, j], src[:, 0:NT], 1.0 / CONV_W, EPS, ALU.mult, ALU.add), name)
                    if kind == "rs":
                        src = wait_fill(dve, name)
                        for k in (2 * j, 2 * j + 1):
                            ins = nc.vector.scalar_tensor_tensor(
                                out=ycf[:, k], in0=ycf[:, k], scalar=g_mix_col[:, 4 + k:5 + k], in1=src[:],
                                op0=ALU.mult, op1=ALU.mult)
                        drain_done(ins, name)
                    if kind == "ss":
                        src = wait_fill(dve, name)
                        drain_done(nc.vector.tensor_scalar(na_ms[:, j:j + 1], src[:, 0:1], 1.0 / NA_W, EPS,
                                                           ALU.mult, ALU.add), name)
                    if kind == "h2Tb":
                        src = wait_fill(dve, name)
                        for k in range(4, KT):
                            ins = nc.vector.tensor_scalar(h2T[:, k], src[:, (k - 4) * P:(k - 3) * P], ffn_gain[:, k:k + 1],
                                                          ffn_shift[:, k:k + 1], ALU.mult, ALU.add)
                        drain_done(ins, name)
                j = tile_at(i, 3)
                if j is not None:
                    dve.wait_ge(na_rs_ready, j + 1)
                    for b in range(2):
                        half = slice(b * 512, (b + 1) * 512)
                        src = wait_fill(dve, ("na", j, b))
                        wait_drained(dve, ("cf", j, b))
                        drain_done(nc.vector.scalar_tensor_tensor(
                            out=y_tmp[:, half], in0=src[:], scalar=na_rs[:, j:j + 1], in1=y_tmp[:, half],
                            op0=ALU.mult, op1=ALU.add), ("na", j, b))
                j = tile_at(i, 4)
                if j is not None:
                    dve.wait_ge(y_rs_ready, j + 1)
                    link(dve, chain, nc.vector.scalar_tensor_tensor(
                        out=y_tmp, in0=y_tmp, scalar=y_rs[:, j:j + 1], in1=gain1, op0=ALU.mult, op1=ALU.mult))
                    dve.wait_ge(x_again, 16 * NT)
                    v = x1[:, Q_TILES[j]]
                    nc.vector.tensor_tensor(v, v, y_tmp, ALU.add).then_inc(x1_ready, 1)
                j = tile_at(i, 6)
                if j is not None:
                    dve.wait_ge(z_rs_ready, j + 1)
                    t = Q_TILES[j]
                    nc.vector.tensor_scalar(xn2[:, t], x1[:, t], z_rs[:, j:j + 1], None, ALU.mult).then_inc(xn2_ready, 1)

            nc.vector.memset(one_row, 1.0)
            for j in range(NT):
                wait_drained(dve, ("rt", j))
            link(dve, chain, nc.vector.tensor_reduce(r_max[:], logit[:], AX_X, ALU.max))
            nc.vector.tensor_tensor(logit[:], logit[:], r_max[:].rearrange("p (t a) -> p t a", a=1).to_broadcast([P, NT, E]),
                                    ALU.subtract).then_inc(r_sub_ready, 1)
            dve.wait_ge(r_exp_ready, 1)
            link(dve, chain, nc.vector.tensor_reduce(r_sum[:], aff[:], AX_X, ALU.add))
            link(dve, chain, nc.vector.reciprocal(r_inv[:], r_sum[:]))
            nc.vector.tensor_tensor(aff[:], aff[:], r_inv[:].rearrange("p (t a) -> p t a", a=1).to_broadcast([P, NT, E]),
                                    ALU.mult).then_inc(aff_ready, 1)
            src = wait_fill(dve, ("affT", 0))
            drain_done(nc.vector.tensor_copy(work, src[0:E]), ("affT", 0))
            wait_drained(dve, ("affT", 0))
            for _ in range(CAP // 8):
                link(dve, chain, nc.vector.max(top8[0:E], work))
                link(dve, chain, nc.vector.match_replace(work, top8[0:E], work, -1.0))
            link(dve, chain, nc.vector.tensor_scalar(chosen, work, 0.0, None, ALU.is_lt))
            link(dve, chain, nc.vector.tensor_tensor_scan(count, one_row, chosen, 0.0, ALU.mult, ALU.add))
            nc.vector.tensor_tensor(rank, count, chosen, ALU.mult).then_inc(rank_ready, 1)
            dve.wait_ge(pool_set, 4)
            src = wait_fill(dve, ("posT", 0))
            ins = nc.vector.tensor_copy(place[:, :, 0:E], src[:, 0:NT * E].rearrange("p (t e) -> p t e", t=NT))
            drain_done(ins, ("posT", 0))
            wait_drained(dve, ("posT", 0))

            def slots_of(dst, e, width):
                nos = iota[:, 0:width].rearrange("p (a s) -> p a s", a=1).to_broadcast([P, NT, width])
                return nc.vector.tensor_tensor(dst, nos, place[:, :, bass.ds(e, 1)].to_broadcast([P, NT, width]),
                                               ALU.is_equal)

            slots_of(pick, 0, CAP).then_inc(pick_ready, 1)
            src = wait_fill(dve, ("xs", 1))
            for j, half in FIRST_TURNS:
                k = 4 * half + 2 + j
                ins = nc.vector.tensor_scalar(xsT[0][:, k], src[:, j * P + half * CAP:j * P + (half + 1) * CAP],
                                              ffn_gain[:, k:k + 1], ffn_shift[:, k:k + 1], ALU.mult, ALU.add)
            drain_done(ins, ("xs", 1))
            dve.wait_ge(start_zero, 1)

            with dve.Fori(0, E // 2) as pair:
                for s in range(2):
                    e = pair * 2 + s
                    for i in range(8):
                        t, b = i // 2, i % 2
                        v = acc[:, t, b * 512:(b + 1) * 512]
                        dve.wait_ge(m_filled, e * 8 + (i + 1))
                        nc.vector.tensor_tensor(v, v, bank[5][:], ALU.add).then_inc(m_drained, 1)
                    dve.wait_ge(t_drained, e * 5 + 2)
                    slots_of(gate_pick, e, 2 * CAP).then_inc(gate_pick_ready, 1)
                    dve.wait_ge(gate_pick_ready, e * 2 + 1)
                    nc.vector.tensor_tensor(gate_pick, gate_pick, aff[:, :, bass.ds(e, 1)].to_broadcast([P, NT, 2 * CAP]),
                                            ALU.mult).then_inc(gate_pick_ready, 1)
                    dve.wait_ge(t_drained, e * 5 + 4)
                    slots_of(pick, e + 1, CAP).then_inc(pick_ready, 1)
                    for c in range(3):
                        q = (3 * s + c) % 2
                        w = HALVES[c]
                        dve.wait_ge(silu_done, e * 3 + (c + 1))
                        nc.vector.tensor_tensor(hid[q][:, 0:w], silu_g[q][:, 0:w], bank[2 + q][:, 0:w], ALU.mult)\
                            .then_inc(hid_ready, 1)

            def scale_last(t):
                dve.wait_ge(f_rs_ready, t + 1)
                nc.vector.scalar_tensor_tensor(out=fin[t], in0=acc[:, t], scalar=y_rs[:, t:t + 1], in1=gain4,
                                               op0=ALU.mult, op1=ALU.mult).then_inc(f_scaled, 1)

            for t in range(NT):
                for b in range(2):
                    v = acc[:, t, b * 512:(b + 1) * 512]
                    dve.wait_ge(last_filled, 2 * t + b + 1)
                    ins = nc.vector.tensor_tensor(v, v, bank[2 * t + b][:], ALU.add)
                ins.then_inc(acc_done, 1)
                if t >= 1:
                    scale_last(t - 1)
            dve.wait_ge(f_scaled, 2)
            nc.vector.tensor_tensor(fin[1], fin[1], x1[:, 1], ALU.add).then_inc(f_ready[1], 1)
            t = NT - 1
            dve.wait_ge(f_rs_ready, t + 1)
            for b in range(2):
                half = slice(b * 512, (b + 1) * 512)
                link(dve, chain, nc.vector.scalar_tensor_tensor(
                    out=fin[t][:, half], in0=acc[:, t, half], scalar=y_rs[:, t:t + 1], in1=gain4[:, half],
                    op0=ALU.mult, op1=ALU.mult))
                nc.vector.tensor_tensor(fin[t][:, half], fin[t][:, half], x1[:, t, half], ALU.add).then_inc(f_ready[t], 1)

        @block.tensor
        def _(pe):
            mm = nc.tensor.matmul

            def turn(dst, src):
                return nc.tensor.transpose(dst, src, ident[0:src.shape[0], 0:src.shape[0]])

            owed = [False]

            def used(ins):
                ins.then_inc(slots_used, 1)

            def used_up_by(ins):
                if owed[0]:
                    used(ins)
                    owed[0] = False

            def transpose_x(kt):
                b = open_fill(pe, ("xT", kt))
                for t in range(NT):
                    ins = turn(b[:, t * P:(t + 1) * P], x_rows[:, t, kt * P:(kt + 1) * P])
                fill_done(ins, ("xT", kt))

            def mod_part(g, k):
                b = open_fill(pe, ("mod", g)) if k == 0 else bank_of(("mod", g))
                w = wait_slot(pe, ("mod", g, k))
                for j in range(4):
                    ins = mm(b[32 * j:32 * (j + 1)], s_pad[:, k], w[:, j * 512:(j + 1) * 512],
                             start=k == 0, stop=k == KT - 1)
                    if j == 0:
                        used_up_by(ins)
                if k < KT - 1:
                    used(ins)
                else:
                    fill_done(ins, ("mod", g))
                    owed[0] = True

            def product(dst, terms):
                for j, (a, b) in enumerate(terms):
                    ins = mm(dst, a, b, start=j == 0, stop=j == len(terms) - 1)
                return ins

            pe.wait_ge(ident_loaded, 16)
            pe.wait_ge(xn_ready, NT)
            for kt in range(6):
                transpose_x(kt)
            pe.wait_ge(silu_ready, 1)
            for k in range(KT):
                mod_part(0, k)
            wait_drained(pe, ("mod", 0))
            b = open_fill(pe, ("modT", 0))
            for j in range(4):
                ins = turn(b[:, j * P:(j + 1) * P], mod_row[:, 0, j * P:(j + 1) * P])
                if j == 0:
                    used_up_by(ins)
            fill_done(ins, ("modT", 0))
            for kt in (6, 7):
                transpose_x(kt)

            def transpose_ctx(f):
                b = open_fill(pe, ("cT", f))
                for j in range(4):
                    kt, t = 2 * f + j // 2, j % 2
                    ins = turn(b[:, j * P:(j + 1) * P], ctx_rows[:, t, kt * P:(kt + 1) * P])
                fill_done(ins, ("cT", f))

            for g, names in enumerate(GROUPS):
                for k in range(KT):
                    if g >= 1 and k % 2 == 0:
                        mod_part((g + 1) // 2, 4 * ((g + 1) % 2) + k // 2)
                    if g == 0:
                        pe.wait_ge(h_ready, k + 1)
                        if k == 5:
                            pe.wait_ge(xn_ready, NT + CT)
                        if k >= 5:
                            transpose_ctx(k - 5)
                    if g == 1:
                        pe.wait_ge(hc_ready, k // 2 + 1)
                    _, (_, w_rest), main = in_slot(g, k // 4)
                    if k % 4 == 0:
                        pe.wait_ge(w_ready, 2 * g + k // 4 + 1)
                    w_parts = [v.rearrange("p (k n) -> p k n", k=4)[:, k % 4] for v in (main, w_rest)]
                    h_parts = [hT[:, k], hT_rest_r[:, k]]
                    hc_parts = [hcT[:, k], hcT_rest_r[:, k]]
                    for i, name in enumerate(names):
                        kind, b_ = name
                        b = open_fill(pe, name) if k == 0 else bank_of(name)
                        if kind in ("v", "vc"):
                            hs = h_parts if kind == "v" else hc_parts
                            terms = [(b[:], [v[:, b_ * P:(b_ + 1) * P] for v in hs], w_parts)]
                        elif kind == "kc":
                            terms = [(b[:, j * CTX:(j + 1) * CTX], [v[:, (2 * b_ + j) * P:(2 * b_ + j + 1) * P] for v in w_parts],
                                      hc_parts) for j in range(2)]
                        else:
                            terms = [(b[:], [v[:, i * P:(i + 1) * P] for v in w_parts], h_parts)]
                        for j, (dst, a, c) in enumerate(terms):
                            for m, (x_, y_) in enumerate(((0, 0), (0, 1), (1, 0))):
                                ins = mm(dst, a[x_], c[y_], start=(k, j, m) == (0, 0, 0),
                                         stop=(k, j, m) == (KT - 1, len(terms) - 1, 2))
                                used_up_by(ins)
                        if k == KT - 1:
                            fill_done(ins, name)
                    if k == 3:
                        used(ins)
                owed[0] = True
                if g == 0:
                    transpose_ctx(3)

            def turn_mod_row(g):
                pe.wait_ge(rows_ready, g)
                b = open_fill(pe, ("modT", g))
                for j in range(4):
                    ins = turn(b[:, j * P:(j + 1) * P], mod_row[:, g, j * P:(j + 1) * P])
                    used_up_by(ins)
                fill_done(ins, ("modT", g))

            def one_row_of(p0):
                return ident[:, p0:p0 + 1].to_broadcast([P, P])

            def on_every_partition(name, free=0):
                b = open_fill(pe, name)
                for m in range(4):
                    ins = mm(b[:, m * P:(m + 1) * P], one_row_of(32 * (name[1] % 4)),
                             mod_row[:, 1 + name[1] // 2, m * P:(m + 1) * P], start=True, stop=True)
                    if m < free:
                        used(ins)
                fill_done(ins, name)

            turn_mod_row(1)
            for b in range(2):
                on_every_partition(("bc", b))

            for b in range(2):
                wait_drained(pe, ("f", b))
            pe.wait_ge(consts_loaded, 16 * 2)
            for blk in range(4):
                b = open_fill(pe, ("dft1", blk))
                for ch in range(2):
                    ins = product(b[:, ch * 256:(ch + 1) * 256], [(f_sb[:, ch, blk * P:(blk + 1) * P], dd[:])])
                fill_done(ins, ("dft1", blk))
            turn_mod_row(2)
            tables = wait_slot(pe, ("dft", 0, 0)).rearrange("p (e h s n) -> p e h s n", e=2, h=2, s=2)
            for blk in range(4):
                wait_drained(pe, ("dft1", blk))
            for ch in range(2):
                b = open_fill(pe, ("dft2", ch))
                for par in range(2):
                    ins = product(b[:, par * 256:(par + 1) * 256],
                                  [(dft_g[:, 2 * par + half, ch * 256 + cs * P:ch * 256 + (cs + 1) * P],
                                    tables[:, par, half, cs]) for half in range(2) for cs in range(2)])
                fill_done(ins, ("dft2", ch))
            owed[0] = True

            def scores(i):
                t, h = UNITS[i]
                b = open_fill(pe, ("S", i))
                q, keys = qTp[:, h, t * P:(t + 1) * P], kT[:, h // 2]
                for j0, j1, p in ((0, 256, t * P),) if t < NT - 1 else ((0, P, t * P), (P, 256, 0)):
                    ins = mm(b[:, j0:j1], q, keys[:, p:p + j1 - j0], start=True, stop=True)
                    used_up_by(ins)
                fill_done(mm(b[:, 256:512], q, kcT[:, h // 2], start=True, stop=True), ("S", i))

            def extra(name):
                kind, j = name[0], name[1]
                last = kind in ("cf", "na") and j == NT - 1
                if kind == "last_bc":
                    on_every_partition(name, 2)
                    owed[0] = False
                    return
                b = open_fill(pe, name)
                if kind == "sq":
                    pe.wait_ge(cf_sq_ready, 2 * j + 2)
                    for t in range(NT):
                        for m in range(2):
                            ins = mm(b[:, t:t + 1], cf_sq[m][:, t * P:(t + 1) * P], ones[:, 0:1], start=m == 0, stop=m == 1)
                if kind == "rs":
                    pe.wait_ge(cf_rs_ready, j + 1)
                    for t in range(NT):
                        ins = mm(b[:, t * P:(t + 1) * P], cf_rs[:, j, t:t + 1].to_broadcast([P, P]), ident,
                                 start=True, stop=True)
                if kind in ("cf", "na"):
                    t, half = Q_TILES[j], slice(name[2] * 512, (name[2] + 1) * 512)
                    if kind == "cf":
                        wait_drained(pe, ("rs", 1))
                    for k in range(4):
                        y = ycf[:, k, t * P:(t + 1) * P] if kind == "cf" else yna[j % 2][:, k]
                        w = wait_slot(pe, ("out", 0, (2 if kind == "cf" else 0) + k // 2))
                        ins = mm(b[:], y, w.rearrange("p (k n) -> p k n", k=2)[:, k % 2, half], start=k == 0, stop=k == 3)
                        if last and name[2] == 1 and k == 1:
                            used(ins)
                    owed[0] = last and name[2] == 1
                if kind == "ss":
                    wait_drained(pe, ("PO", HEADS * j + HEADS - 1))
                    for k in range(PAIRS):
                        ins = mm(b[:, 0:1], na_sq[:, k * P:(k + 1) * P], ones[:, 0:1], start=k == 0, stop=k == PAIRS - 1)
                        if k == 0:
                            used_up_by(ins)
                if kind in ("h2Ta", "h2Tb"):
                    pe.wait_ge(xn2_ready, j + 1)
                    for m in range(4):
                        k = m + 4 * (kind == "h2Tb")
                        ins = turn(b[:, m * P:(m + 1) * P], xn2[:, Q_TILES[j], k * P:(k + 1) * P])
                        if m == 0:
                            used_up_by(ins)
                if kind == "rt":
                    wait_drained(pe, ("h2Ta", j))
                    wait_drained(pe, ("h2Tb", j))
                    for k in range(KT):
                        ins = mm(b[:, 0:E], h2T[:, k], w_rt[:, k], start=k == 0, stop=k == KT - 1)
                fill_done(ins, name)

            for name in GROUPS[0] + GROUPS[1] + GROUPS[2]:
                wait_drained(pe, name)
            pe.wait_ge(pool_set, 3)
            for i in range(N + TAIL):
                if i < N:
                    scores(i)
                if STEPS <= i < N + STEPS:
                    j = i - STEPS
                    b = open_fill(pe, ("PT", j))
                    pe.wait_ge(prob_ready, j + 1)
                    for m in range(4):
                        ins = turn(b[:, m * P:(m + 1) * P], prob[j % 4][:, m * P:(m + 1) * P])
                    fill_done(ins, ("PT", j))
                if STEPS + 3 <= i <= N + STEPS + 1 and i % 2 == 0:
                    po = i - STEPS - 2
                    b = open_fill(pe, ("PO", po))
                    wait_drained(pe, ("PT", po))
                    for m in range(4):
                        for j in (po - 1, po):
                            t, h = UNITS[j]
                            hh = slice(h * DH, (h + 1) * DH)
                            v = v_sb[:, KEY_TILES[t][m], hh] if m < 2 else vc_sb[:, m - 2, hh]
                            p0 = (h % 2) * 64
                            ins = mm(b[p0:p0 + 64, 0:P], v, probT[j % 4][:, m * P:(m + 1) * P],
                                     start=m == 0, stop=m == 3)
                    fill_done(ins, ("PO", po))
                for name in extra_fills(i):
                    extra(name)
            pe.wait_ge(aff_ready, 1)
            b = open_fill(pe, ("affT", 0))
            for t in range(NT):
                ins = turn(b[0:E, t * P:(t + 1) * P], aff[:, t])
                if t == 0:
                    used(ins)
            fill_done(ins, ("affT", 0))
            pe.wait_ge(rank_ready, 1)
            b = open_fill(pe, ("posT", 0))
            for t in range(NT):
                ins = turn(b[:, t * E:(t + 1) * E], rank[:, t * P:(t + 1) * P])
            fill_done(ins, ("posT", 0))

            def gather(dst, kt):
                for t in range(NT):
                    ins = mm(dst[:, kt * CAP:(kt + 1) * CAP], xn2[:, t, kt * P:(kt + 1) * P], pick[:, t],
                             start=t == 0, stop=t == NT - 1)
                return ins

            pe.wait_ge(pick_ready, 1)
            b = open_fill(pe, ("xg", 0))
            for t in range(NT):
                for half in range(2):
                    ins = mm(b[64 * half:64 * half + 64], pick[:, t], xn2[:, t, half * 512:(half + 1) * 512],
                             start=t == 0, stop=t == NT - 1)
            fill_done(ins, ("xg", 0))
            wait_drained(pe, ("xg", 0))
            for i in range(2):
                b = open_fill(pe, ("xs", i))
                for j in range(2):
                    ins = turn(b[:, j * P:(j + 1) * P], first_rows[:, (2 * i + j) * P:(2 * i + j + 1) * P])
                fill_done(ins, ("xs", i))
            for i in range(2):
                wait_drained(pe, ("xs", i))
            wait_drained(pe, ("posT", 0))
            for kind in ("h2Tb", "rt"):
                wait_drained(pe, (kind, NT - 1))
            pe.wait_ge(start_zero, 3)

            gate_b, up_b, turn_b, mix_b, down_b = bank[0:2], bank[2:4], bank[4], bank[5], bank[6:8]

            def combine(dst, s, i):
                t, b_ = i // 2, i % 2
                return mm(dst[:], gateT[s][:, t * P:(t + 1) * P], out_e[:, b_ * 512:(b_ + 1) * 512], start=True, stop=True)

            with pe.Fori(0, E // 2) as pair:
                for s in range(2):
                    e = pair * 2 + s

                    def open_turn(fill):
                        pe.wait_ge(t_drained, e * 5 + (5 + fill))

                    def hidden(c, fill):
                        q = (3 * s + c) % 2
                        pe.wait_ge(hid_ready, e * 3 + (c + 4))
                        open_turn(fill)
                        for j in range(HALVES[c] // P):
                            ins = turn(turn_b[:, j * P:(j + 1) * P], hid[q][:, j * P:(j + 1) * P])
                        ins.then_inc(t_filled, 1)

                    def down(j):
                        i = s * STAGE + GU_SLOTS + j
                        n_ = slot_of(i)
                        pe.wait_ge(loaded[n_], loads_until(pair, i))
                        w = ring[n_].rearrange("p (h n) -> p h n", h=2)
                        for b_ in range(2):
                            for half in range(2):
                                ins = mm(down_b[b_][64 * half:64 * half + 64], hidT[:, j, 64 * half:64 * half + 64],
                                         w[:, half, b_ * 512:(b_ + 1) * 512], start=j == 0, stop=j == DOWN_SLOTS - 1)
                        used(ins)

                    for c in range(3):
                        q, w_ = (3 * s + c) % 2, HALVES[c]
                        pe.wait_ge(hid_ready, e * 3 + (c + 2))
                        for k in range(KT):
                            for which, banks in ((0, gate_b), (1, up_b)):
                                i = s * STAGE + 8 * c + 2 * (k // 2) + which
                                n_ = slot_of(i)
                                if k % 2 == 0:
                                    pe.wait_ge(loaded[n_], loads_until(pair, i))
                                w = ring[n_][:, (k % 2) * 2 * w_:(k % 2 + 1) * 2 * w_]
                                for half in range(2):
                                    ins = mm(banks[q][64 * half:64 * half + 64, 0:w_], xsT[s][:, k],
                                             w[:, half * w_:(half + 1) * w_], start=k == 0, stop=k == KT - 1)
                                if k % 2:
                                    used(ins)
                            if c == 0:
                                pe.wait_ge(m_drained, e * 8 + (8 + k))
                                if k == 0:
                                    pe.wait_ge(d_drained, e + 1)
                                combine(mix_b, 1 - s, k).then_inc(m_filled, 1)
                            if (c, k) == (1, 1):
                                hidden(0, 0)
                            if (c, k) == (1, 3):
                                pe.wait_ge(gate_pick_ready, e * 2 + 2)
                                open_turn(1)
                                for t in range(NT):
                                    ins = turn(turn_b[:, t * P:(t + 1) * P], gate_pick[:, t])
                                ins.then_inc(t_filled, 1)
                            if (c, k) == (2, 1):
                                hidden(1, 2)
                            if c == 2 and 3 <= k < 7:
                                if k == 3:
                                    pe.wait_ge(pick_ready, e + 2)
                                    open_turn(3)
                                gather(turn_b, 2 * (k - 3))
                                ins = gather(turn_b, 2 * (k - 3) + 1)
                                if k == 6:
                                    ins.then_inc(t_filled, 1)
                    pe.wait_ge(d_drained, e + 1)
                    for j in range(8):
                        down(j)
                    hidden(2, 4)
                    pe.wait_ge(t_drained, e * 5 + 10)
                    for j in range(8, DOWN_SLOTS):
                        down(j)

            pe.wait_ge(d_drained, E + 1)
            pe.wait_ge(hid_ready, 3 + 3 * E)
            pe.wait_ge(m_drained, 8 + 8 * E)
            pe.wait_ge(t_drained, 5 + 5 * E)
            for i in range(8):
                combine(bank[i], 1, i).then_inc(last_filled, 1)


def constants():
    ident = np.eye(P)
    slots = np.tile(np.arange(1, CAP + 1), (P, 2))
    k = np.arange(64)
    a = 2 * np.pi * np.outer(k, k) / 64
    dd = np.zeros((P, 2, P))
    for g in range(2):
        dd[64 * g:64 * g + 64, 0, 64 * g:64 * g + 64] = np.cos(a)
        dd[64 * g:64 * g + 64, 1, 64 * g:64 * g + 64] = np.sin(a)
    consts = np.concatenate([ident, slots, dd.reshape(P, -1)], axis=1).astype(np.float32)
    dft = np.zeros((P, 2, 2, 2, 256))
    c16, r8 = np.divmod(np.arange(P), ROWS)
    cf, rf = np.divmod(np.arange(256), 4)
    m = rf * GRID_W + cf
    for par in range(2):
        for half in range(2):
            token = r8 * GRID_W + 32 * half + 2 * c16 + par
            a = 2 * np.pi * (np.outer(token, m) % SEQ) / SEQ
            dft[:, par, half, 0] = np.cos(a)
            dft[:, par, half, 1] = -np.sin(a)
    dft /= np.sqrt(SEQ * 64.0)
    return consts, dft.reshape(P, SLOT).astype(np.float32)


_INS = ["x", "cT", "ctx", "w_mod", "b_mod", "colv", "g_post_mix", "g_pre_ffn", "g_post_ffn", "w_in", "rpbT", "w_out",
        "w_router", "w_gate", "w_up", "w_down", "consts", "dft"]


def lay_out(inputs):
    a = {k: np.ascontiguousarray(v) for k, v in inputs.items()}

    def by_partition(v):
        return v.reshape(-1, P).T

    a["cT"] = np.ascontiguousarray(np.stack([by_partition(a["c"]), by_partition(a["c_ctx"])], axis=-1))
    conv = a["conv_w"][0].reshape(3, 2, P).transpose(2, 1, 0).reshape(P, 6)
    a["colv"] = np.ascontiguousarray(
        np.concatenate([by_partition(a["g_pre_mix"]), by_partition(a["g_mix_out"]), conv], axis=1))
    a["rpbT"] = np.ascontiguousarray(a["rpb"][0].transpose(0, 2, 1))
    a["w_router"] = np.ascontiguousarray(a["w_router"][0].reshape(KT, P, E).transpose(1, 0, 2))
    a["consts"], a["dft"] = constants()
    return {k: a[k] for k in _INS}


def kernel(**inputs):
    import concourse.bacc as bacc
    from concourse.bass_utils import run_bass_kernel_spmd

    nc = bacc.Bacc("TRN2", target_bir_lowering=False, num_devices=1, dynamic_dma_scratch_size=1024)
    arrays, args = {}, []
    for name, a in lay_out(inputs).items():
        arrays[f"in_{name}"] = a
        args.append(nc.dram_tensor(f"in_{name}", a.shape, mybir.dt.from_np(a.dtype), kind="ExternalInput").ap())
    args.append(nc.dram_tensor("out_x", (1, SEQ, D), F32, kind="ExternalOutput").ap())
    build_block(nc, *args)
    r = run_bass_kernel_spmd(nc, [arrays], core_ids=[0])
    return r.results[0]["out_x"]
```
